# Optimizing a Trainium2 kernel written in Bass

```python
import jax, jax.numpy as jnp
from jax import lax
import numpy as np

D_MODEL = 1024
BATCH = 1
SEQ = 256
DEPTH = 4

N_MIXERS = 3
HEAD_DIM = 64
N_HEADS = 12
MIX_WIDTH = N_HEADS * HEAD_DIM
N_MEM = 256
N_MEM_HEADS = 4
MEM_WIDTH = N_MEM_HEADS * HEAD_DIM
ROPE_DIM = HEAD_DIM // 4
ROPE_THETA = 500000.0
POS_OFFSET_RANGE = 8192
IDX_HEADS = 8
IDX_DIM = 64
TOPK_MAX = 256
QBLOCK_A = 64
DIL_PAIRS = ((128, 1), (512, 4), (2048, 16))
B_GROUP_HEADS = 4
B_V_DIM = MIX_WIDTH // B_GROUP_HEADS
MOBA_BLOCK = 256
MOBA_TOPK = 3
QBLOCK_C = 16
D_FF = -(-8 * D_MODEL // (3 * 256)) * 256
ALPHA = (2 * DEPTH) ** 0.25
BETA = (8 * DEPTH) ** -0.25
LN_EPS = 1e-5

WIDTH_A = 3 * MIX_WIDTH + IDX_HEADS * IDX_DIM + IDX_HEADS + IDX_DIM + MEM_WIDTH
WIDTH_BC = 3 * MIX_WIDTH + MEM_WIDTH


def layer_norm(x, g, b):
    xf = x.astype(jnp.float32)
    mu = jnp.mean(xf, -1, keepdims=True)
    var = jnp.mean(jnp.square(xf - mu), -1, keepdims=True)
    return ((xf - mu) * lax.rsqrt(var + LN_EPS) * g + b).astype(x.dtype)

def split_cols(h, widths):
    cuts = [int(c) for c in np.cumsum(widths)[:-1]]
    return jnp.split(h, cuts, axis=-1)

def rope_tables(positions):
    half = ROPE_DIM // 2
    inv = ROPE_THETA ** (-jnp.arange(half, dtype=jnp.float32) / half)
    ang = positions.astype(jnp.float32)[..., None] * inv
    return jnp.cos(ang)[:, :, None, :], jnp.sin(ang)[:, :, None, :]

def apply_rope(x, cos, sin):
    half = ROPE_DIM // 2
    c, s = cos.astype(x.dtype), sin.astype(x.dtype)
    x1, x2, rest = x[..., :half], x[..., half:ROPE_DIM], x[..., ROPE_DIM:]
    return jnp.concatenate([x1 * c - x2 * s, x2 * c + x1 * s, rest], axis=-1)

def dsa_attention(q, k, v, q_idx, w_idx, k_idx):
    Bsz, S, H, dh = q.shape
    topk = min(TOPK_MAX, S // 4)
    key_pos = jnp.arange(S)
    scale = dh ** -0.5

    def block(i):
        t0 = i * QBLOCK_A
        qpos = t0 + jnp.arange(QBLOCK_A)
        qi = lax.dynamic_slice_in_dim(q_idx, t0, QBLOCK_A, axis=1)
        wi = lax.dynamic_slice_in_dim(w_idx, t0, QBLOCK_A, axis=1)
        dots = jnp.einsum('bqhd,bsd->bqhs', qi, k_idx).astype(jnp.float32)
        score = jnp.einsum('bqhs,bqh->bqs', jax.nn.relu(dots), wi.astype(jnp.float32))
        causal = key_pos[None, :] <= qpos[:, None]
        score = jnp.where(causal[None], score, -jnp.inf)
        _, sel = lax.top_k(score, topk)
        valid = sel <= qpos[None, :, None]
        ks = jax.vmap(lambda kb, ib: kb[ib])(k, sel)
        vs = jax.vmap(lambda vb, ib: vb[ib])(v, sel)
        qb = lax.dynamic_slice_in_dim(q, t0, QBLOCK_A, axis=1)
        logits = jnp.einsum('bqhd,bqkhd->bhqk', qb, ks).astype(jnp.float32) * scale
        logits = jnp.where(valid[:, None], logits, -jnp.inf)
        p = jax.nn.softmax(logits, axis=-1).astype(v.dtype)
        return jnp.einsum('bhqk,bqkhd->bqhd', p, vs)

    out = lax.map(block, jnp.arange(S // QBLOCK_A))
    return out.transpose(1, 0, 2, 3, 4).reshape(Bsz, S, H, dh)

def dilated_group(q, k, v, window, dilation):
    Bsz, S, G, dh = q.shape
    dv = v.shape[-1]
    n = window // dilation
    L = S // dilation
    nb = -(-L // n)
    Lp = nb * n

    def to_sub(a):
        a = a.reshape(Bsz, L, dilation, G, a.shape[-1]).transpose(0, 2, 1, 3, 4)
        a = jnp.pad(a, ((0, 0), (0, 0), (0, Lp - L), (0, 0), (0, 0)))
        return a.reshape(Bsz, dilation, nb, n, G, a.shape[-1])

    qs, ks, vs = to_sub(q), to_sub(k), to_sub(v)
    shift = ((0, 0), (0, 0), (1, 0), (0, 0), (0, 0), (0, 0))
    kk = jnp.concatenate([jnp.pad(ks[:, :, :-1], shift), ks], axis=3)
    vv = jnp.concatenate([jnp.pad(vs[:, :, :-1], shift), vs], axis=3)
    qi = jnp.arange(n)[:, None] + n
    ki = jnp.arange(2 * n)[None, :]
    dist = qi - ki
    ksub = jnp.arange(nb)[:, None, None] * n + ki[None] - n
    mask = ((dist >= 0) & (dist <= n))[None] & (ksub >= 0)
    logits = jnp.einsum('brnqgd,brnkgd->brngqk', qs, kk).astype(jnp.float32) * (dh ** -0.5)
    logits = jnp.where(mask[None, None, :, None], logits, -jnp.inf)
    lse = jax.nn.logsumexp(logits, axis=-1)
    p = jnp.exp(logits - lse[..., None]).astype(v.dtype)
    out = jnp.einsum('brngqk,brnkgd->brnqgd', p, vv)
    out = out.reshape(Bsz, dilation, Lp, G, dv)[:, :, :L]
    out = out.transpose(0, 2, 1, 3, 4).reshape(Bsz, S, G, dv)
    lse = lse.transpose(0, 1, 2, 4, 3).reshape(Bsz, dilation, Lp, G)[:, :, :L]
    lse = lse.transpose(0, 2, 1, 3).reshape(Bsz, S, G)
    return out, lse

def dilated_attention(q, k, v):
    outs, lses = [], []
    for g, (window, dilation) in enumerate(DIL_PAIRS):
        hs = slice(g * B_GROUP_HEADS, (g + 1) * B_GROUP_HEADS)
        o, l = dilated_group(q[:, :, hs], k[:, :, hs], v, window, dilation)
        outs.append(o)
        lses.append(l)
    wts = jax.nn.softmax(jnp.stack(lses, 0), axis=0).astype(v.dtype)
    return jnp.einsum('gbsh,gbshd->bshd', wts, jnp.stack(outs, 0))

def moba_attention(q, k, v):
    Bsz, S, H, dh = q.shape
    nblk = -(-S // MOBA_BLOCK)
    Sp = nblk * MOBA_BLOCK
    pad = lambda a: jnp.pad(a, ((0, 0), (0, Sp - S), (0, 0), (0, 0)))
    qp = pad(q)
    kbt = pad(k).reshape(Bsz, nblk, MOBA_BLOCK, H, dh).transpose(0, 3, 1, 2, 4)
    vbt = pad(v).reshape(Bsz, nblk, MOBA_BLOCK, H, dh).transpose(0, 3, 1, 2, 4)
    kmean = jnp.mean(kbt.astype(jnp.float32), axis=3)
    ksel = min(MOBA_TOPK, nblk)
    scale = dh ** -0.5
    bidx = jnp.arange(Bsz)[:, None, None, None]
    hidx = jnp.arange(H)[None, :, None, None]

    def block(i):
        t0 = i * QBLOCK_C
        own = t0 // MOBA_BLOCK
        qpos = t0 + jnp.arange(QBLOCK_C)
        qh = lax.dynamic_slice_in_dim(qp, t0, QBLOCK_C, axis=1).transpose(0, 2, 1, 3)
        gate = jnp.einsum('bhqd,bhnd->bhqn', qh.astype(jnp.float32), kmean)
        gate = jnp.where(jnp.arange(nblk) < own, gate, -jnp.inf)
        _, sel = lax.top_k(gate, ksel)
        valid = jnp.repeat(jnp.arange(ksel) < own, MOBA_BLOCK)
        kg = kbt[bidx, hidx, sel]
        vg = vbt[bidx, hidx, sel]
        ko = lax.dynamic_index_in_dim(kbt, own, axis=2, keepdims=False)
        vo = lax.dynamic_index_in_dim(vbt, own, axis=2, keepdims=False)
        kpos = own * MOBA_BLOCK + jnp.arange(MOBA_BLOCK)
        s_sel = jnp.einsum('bhqd,bhqnkd->bhqnk', qh, kg).astype(jnp.float32)
        s_sel = jnp.where(valid, s_sel.reshape(Bsz, H, QBLOCK_C, ksel * MOBA_BLOCK), -jnp.inf)
        s_own = jnp.einsum('bhqd,bhkd->bhqk', qh, ko).astype(jnp.float32)
        s_own = jnp.where(kpos[None, :] <= qpos[:, None], s_own, -jnp.inf)
        p = jax.nn.softmax(jnp.concatenate([s_sel, s_own], -1) * scale, axis=-1).astype(v.dtype)
        p_sel = p[..., :ksel * MOBA_BLOCK].reshape(Bsz, H, QBLOCK_C, ksel, MOBA_BLOCK)
        o = jnp.einsum('bhqnk,bhqnkd->bhqd', p_sel, vg) + jnp.einsum('bhqk,bhkd->bhqd', p[..., ksel * MOBA_BLOCK:], vo)
        return o.transpose(0, 2, 1, 3)

    out = lax.map(block, jnp.arange(Sp // QBLOCK_C))
    return out.transpose(1, 0, 2, 3, 4).reshape(Bsz, Sp, H, dh)[:, :S]

def memory_attention(q, mk, mv):
    logits = jnp.einsum('bshd,bnhd->bhsn', q, mk).astype(jnp.float32) * (HEAD_DIM ** -0.5)
    p = jax.nn.softmax(logits, axis=-1).astype(mv.dtype)
    return jnp.einsum('bhsn,bnhd->bshd', p, mv)

def swiglu(x, w_gate_up, w_down):
    g, u = jnp.split(x @ w_gate_up, 2, axis=-1)
    return (jax.nn.silu(g) * u) @ w_down

def first_inputs(seed: int = 0) -> dict:
    key = jax.random.key(seed)
    ks = jax.random.split(key, 18)
    n_a, n_b, n_c = (DEPTH + 2) // 3, (DEPTH + 1) // 3, DEPTH // 3
    nrm = lambda k, shape, s: jax.random.normal(k, shape, jnp.float32) * s
    gain = lambda k, shape: 1.0 + nrm(k, shape, 0.02)
    offs = jax.random.randint(ks[2], (BATCH, 1), 0, POS_OFFSET_RANGE, dtype=jnp.int32)
    positions = offs + jnp.arange(SEQ, dtype=jnp.int32)[None, :]
    return {
        'x': nrm(ks[0], (BATCH, SEQ, D_MODEL), 1.0),
        'mem': nrm(ks[1], (BATCH, N_MEM, D_MODEL), 1.0),
        'positions': positions,
        'mem_ln_g': gain(ks[3], (D_MODEL,)),
        'mem_ln_b': nrm(ks[4], (D_MODEL,), 0.02),
        'w_in_a': nrm(ks[5], (n_a, D_MODEL, WIDTH_A), D_MODEL ** -0.5),
        'idx_kn_g': gain(ks[6], (n_a, IDX_DIM)),
        'idx_kn_b': nrm(ks[7], (n_a, IDX_DIM), 0.02),
        'w_in_b': nrm(ks[8], (n_b, D_MODEL, WIDTH_BC), D_MODEL ** -0.5),
        'w_in_c': nrm(ks[9], (n_c, D_MODEL, WIDTH_BC), D_MODEL ** -0.5),
        'w_mem_kv': nrm(ks[10], (DEPTH, D_MODEL, 2 * MEM_WIDTH), D_MODEL ** -0.5),
        'w_out': nrm(ks[11], (DEPTH, MIX_WIDTH + MEM_WIDTH, D_MODEL), BETA * (MIX_WIDTH + MEM_WIDTH) ** -0.5),
        'ln1_g': gain(ks[12], (DEPTH, D_MODEL)),
        'ln1_b': nrm(ks[13], (DEPTH, D_MODEL), 0.02),
        'w_gate_up': nrm(ks[14], (DEPTH, D_MODEL, 2 * D_FF), D_MODEL ** -0.5),
        'w_down': nrm(ks[15], (DEPTH, D_FF, D_MODEL), BETA * D_FF ** -0.5),
        'ln2_g': gain(ks[16], (DEPTH, D_MODEL)),
        'ln2_b': nrm(ks[17], (DEPTH, D_MODEL), 0.02),
    }

def first_block(x, mem, positions, mem_ln_g, mem_ln_b, w_in_a, idx_kn_g, idx_kn_b, w_in_b, w_in_c,
              w_mem_kv, w_out, ln1_g, ln1_b, w_gate_up, w_down, ln2_g, ln2_b):
    Bsz, S, _ = x.shape
    cos, sin = rope_tables(positions)
    mem_n = layer_norm(mem, mem_ln_g, mem_ln_b)
    heads = lambda a, h, d: a.reshape(Bsz, S, h, d)
    for i in range(DEPTH):
        kind, j = i % N_MIXERS, i // N_MIXERS
        if kind == 0:
            q, k, v, qi, wi, ki, qm = split_cols(
                x @ w_in_a[j],
                (MIX_WIDTH, MIX_WIDTH, MIX_WIDTH, IDX_HEADS * IDX_DIM, IDX_HEADS, IDX_DIM, MEM_WIDTH))
            q = apply_rope(heads(q, N_HEADS, HEAD_DIM), cos, sin)
            k = apply_rope(heads(k, N_HEADS, HEAD_DIM), cos, sin)
            qi = apply_rope(heads(qi, IDX_HEADS, IDX_DIM), cos, sin)
            ki = apply_rope(layer_norm(ki, idx_kn_g[j], idx_kn_b[j])[:, :, None, :], cos, sin)[:, :, 0]
            wi = wi * (IDX_HEADS * IDX_DIM) ** -0.5
            mix = dsa_attention(q, k, heads(v, N_HEADS, HEAD_DIM), qi, wi, ki)
        elif kind == 1:
            q, k, v, qm = split_cols(x @ w_in_b[j], (MIX_WIDTH, MIX_WIDTH, MIX_WIDTH, MEM_WIDTH))
            q = apply_rope(heads(q, N_HEADS, HEAD_DIM), cos, sin)
            k = apply_rope(heads(k, N_HEADS, HEAD_DIM), cos, sin)
            mix = dilated_attention(q, k, heads(v, B_GROUP_HEADS, B_V_DIM))
        else:
            q, k, v, qm = split_cols(x @ w_in_c[j], (MIX_WIDTH, MIX_WIDTH, MIX_WIDTH, MEM_WIDTH))
            q = apply_rope(heads(q, N_HEADS, HEAD_DIM), cos, sin)
            k = apply_rope(heads(k, N_HEADS, HEAD_DIM), cos, sin)
            mix = moba_attention(q, k, heads(v, N_HEADS, HEAD_DIM))
        mk, mv = jnp.split(mem_n @ w_mem_kv[i], 2, axis=-1)
        mo = memory_attention(heads(qm, N_MEM_HEADS, HEAD_DIM),
                              mk.reshape(Bsz, N_MEM, N_MEM_HEADS, HEAD_DIM),
                              mv.reshape(Bsz, N_MEM, N_MEM_HEADS, HEAD_DIM))
        mixed = jnp.concatenate([mix.reshape(Bsz, S, MIX_WIDTH), mo.reshape(Bsz, S, MEM_WIDTH)], -1) @ w_out[i]
        x = layer_norm(ALPHA * x + mixed, ln1_g[i], ln1_b[i])
        x = layer_norm(ALPHA * x + swiglu(x, w_gate_up[i], w_down[i]), ln2_g[i], ln2_b[i])
    return x


DEPTH_2 = 2

CHUNK = 64
D_MIX = D_MODEL
D_RET = D_MIX // 2
D_SB = D_MIX - D_RET
RET_HEADS = 4
RET_HEAD_DIM = D_RET // RET_HEADS
SB_HEADS = 8
SB_HEAD_DIM = D_SB // SB_HEADS
Q_BLOCK = 128
ROPE_BASE = 10000.0
EPS = 1e-6
ADA_SCALE = 0.2
SPLIT_SIZES = [D_RET] * 4 + [D_SB] * 4
D_IN = sum(SPLIT_SIZES)


def rms_norm(x, g):
    xf = x.astype(jnp.float32)
    return xf * lax.rsqrt(jnp.mean(xf * xf, axis=-1, keepdims=True) + EPS) * g.astype(jnp.float32)

def split_heads(x, n_heads):
    b, s, _ = x.shape
    return x.reshape(b, s, n_heads, -1).transpose(0, 2, 1, 3)

def merge_heads(x):
    b, h, s, d = x.shape
    return x.transpose(0, 2, 1, 3).reshape(b, s, h * d)

def rotary(x, pos):
    half = x.shape[-1] // 2
    inv = ROPE_BASE ** (-jnp.arange(half, dtype=jnp.float32) / half)
    ang = pos[:, None] * inv[None, :]
    cos, sin = jnp.cos(ang), jnp.sin(ang)
    x1, x2 = x[..., :half], x[..., half:]
    return jnp.concatenate([x1 * cos - x2 * sin, x1 * sin + x2 * cos], axis=-1)

def retention(q, k, v):
    b, h, s, d = q.shape
    n = s // CHUNK
    log_gamma = jnp.log1p(-(2.0 ** (-5.0 - jnp.arange(h, dtype=jnp.float32))))
    idx = jnp.arange(CHUNK, dtype=jnp.float32)
    dmask = jnp.exp(jnp.abs(idx[:, None] - idx[None, :])[None] * log_gamma[:, None, None])
    q_dec = jnp.exp((idx + 1.0)[None, :] * log_gamma[:, None])
    k_dec = jnp.exp((CHUNK - 1.0 - idx)[None, :] * log_gamma[:, None])
    chunk_dec = jnp.exp(CHUNK * log_gamma)

    k = k * (d ** -0.5)
    qc = q.reshape(b, h, n, CHUNK, d)
    kc = k.reshape(b, h, n, CHUNK, d)
    vc = v.reshape(b, h, n, CHUNK, v.shape[-1])

    scores = jnp.einsum('bhncd,bhnmd->bhncm', qc, kc) * dmask[None, :, None]
    o_inner = jnp.einsum('bhncm,bhnme->bhnce', scores, vc)

    kv = jnp.einsum('bhnmd,bhnme->nbhde', kc * k_dec[None, :, None, :, None], vc)

    def step(state, kv_i):
        return state * chunk_dec[None, :, None, None] + kv_i, state

    init = jnp.zeros((b, h, d, v.shape[-1]), dtype=kv.dtype)
    _, prev = lax.scan(step, init, kv)
    o_cross = jnp.einsum('bhncd,nbhde->bhnce', qc, prev) * q_dec[None, :, None, :, None]

    o = (o_inner + o_cross).reshape(b, h, s, v.shape[-1])
    mu = jnp.mean(o, axis=-1, keepdims=True)
    var = jnp.mean(jnp.square(o - mu), axis=-1, keepdims=True)
    return (o - mu) * lax.rsqrt(var + EPS)

def stick_breaking(q, k, v):
    b, h, s, d = q.shape
    nb = s // Q_BLOCK
    scale = d ** -0.5
    q_blocks = q.reshape(b, h, nb, Q_BLOCK, d).transpose(2, 0, 1, 3, 4)
    key_pos = jnp.arange(s)

    def block(args):
        qi, bi = args
        t = bi * Q_BLOCK + jnp.arange(Q_BLOCK)
        mask = key_pos[None, :] < t[:, None]
        z = jnp.einsum('bhqd,bhsd->bhqs', qi, k) * scale
        log_beta = jax.nn.log_sigmoid(z)
        log_keep = jnp.where(mask, jax.nn.log_sigmoid(-z), 0.0)
        suffix = lax.cumsum(log_keep, axis=3, reverse=True) - log_keep
        a = jnp.where(mask, jnp.exp(log_beta + suffix), 0.0)
        return jnp.einsum('bhqs,bhse->bhqe', a, v)

    out = lax.map(block, (q_blocks, jnp.arange(nb)))
    return out.transpose(1, 2, 0, 3, 4).reshape(b, h, s, v.shape[-1])

def hybrid_layer(x, c_act, norm_g, w_ada, b_ada, w_in, w_out, pos):
    mod = c_act @ w_ada + b_ada
    shift, scale, gate = jnp.split(mod, 3, axis=-1)
    h = rms_norm(x, norm_g) * (1.0 + scale[:, None, :]) + shift[:, None, :]
    proj = h @ w_in
    split_at = [int(i) for i in np.cumsum(SPLIT_SIZES)[:-1]]
    rq, rk, rv, rg, sq, sk, sv, sg = jnp.split(proj, split_at, axis=-1)

    y_ret = retention(rotary(split_heads(rq, RET_HEADS), pos),
                      rotary(split_heads(rk, RET_HEADS), pos),
                      split_heads(rv, RET_HEADS))
    y_ret = merge_heads(y_ret) * jax.nn.silu(rg)

    y_sb = stick_breaking(split_heads(sq, SB_HEADS), split_heads(sk, SB_HEADS),
                          split_heads(sv, SB_HEADS))
    y_sb = merge_heads(y_sb) * jax.nn.silu(sg)

    y = jnp.concatenate([y_ret, y_sb], axis=-1) @ w_out
    return x + gate[:, None, :] * y

def second_inputs(seed: int = 0) -> dict:
    key = jax.random.key(seed)
    ks = jax.random.split(key, 8)
    f32 = jnp.float32
    x = jax.random.normal(ks[0], (BATCH, SEQ, D_MODEL), f32)
    c = jax.random.normal(ks[1], (BATCH, D_MODEL), f32)
    norm_g = 1.0 + 0.02 * jax.random.normal(ks[2], (DEPTH_2, D_MODEL), f32)
    w_ada = jax.random.normal(ks[3], (DEPTH_2, D_MODEL, 3 * D_MODEL), f32) * (ADA_SCALE * D_MODEL ** -0.5)
    b_ada = 0.02 * jax.random.normal(ks[4], (DEPTH_2, 3 * D_MODEL), f32)
    w_in = jax.random.normal(ks[5], (DEPTH_2, D_MODEL, D_IN), f32) * (D_MODEL ** -0.5)
    w_out = jax.random.normal(ks[6], (DEPTH_2, D_MIX, D_MODEL), f32) * (D_MIX ** -0.5)
    final_g = 1.0 + 0.02 * jax.random.normal(ks[7], (D_MODEL,), f32)
    return {"x": x, "c": c, "norm_g": norm_g, "w_ada": w_ada, "b_ada": b_ada,
            "w_in": w_in, "w_out": w_out, "final_g": final_g}

def second_block(x, c, norm_g, w_ada, b_ada, w_in, w_out, final_g):
    pos = jnp.arange(x.shape[1], dtype=jnp.float32)
    c_act = jax.nn.silu(c.astype(jnp.float32))
    h = x.astype(jnp.float32)
    for layer in range(DEPTH_2):
        h = hybrid_layer(h, c_act, norm_g[layer], w_ada[layer], b_ada[layer],
                         w_in[layer], w_out[layer], pos)
    return rms_norm(h, final_g).astype(x.dtype)


def setup_inputs(seed=0):
    out = dict(first_inputs(seed))
    for name, value in second_inputs(seed + 1).items():
        if name != "x":
            out[name + "_2"] = value
    return out


def reference(
    x, mem, positions, mem_ln_g, mem_ln_b, w_in_a, idx_kn_g, idx_kn_b, w_in_b, w_in_c, w_mem_kv,
    w_out, ln1_g, ln1_b, w_gate_up, w_down, ln2_g, ln2_b, c_2, norm_g_2, w_ada_2, b_ada_2,
    w_in_2, w_out_2, final_g_2,
):
    x = first_block(
        x, mem, positions, mem_ln_g, mem_ln_b, w_in_a, idx_kn_g, idx_kn_b, w_in_b, w_in_c,
        w_mem_kv, w_out, ln1_g, ln1_b, w_gate_up, w_down, ln2_g, ln2_b,
    )
    return second_block(
        x, c_2, norm_g_2, w_ada_2, b_ada_2, w_in_2, w_out_2, final_g_2,
    )


_drawn_inputs = setup_inputs


def setup_inputs(seed=0):
    import zlib

    import numpy as np

    out = dict(_drawn_inputs(seed))
    spreads = {}
    factors = {'mem_ln_g': 8.0,
     'mem_ln_b': 8.0,
     'idx_kn_g': 8.0,
     'idx_kn_b': 8.0,
     'norm_g_2': 8.0,
     'b_ada_2': 3.584,
     'final_g_2': 2.796}
    for name, (base, spread) in spreads.items():
        noise = np.random.default_rng([zlib.crc32(name.encode()), seed]).standard_normal(out[name].shape)
        drawn = base * np.exp(spread * noise) if base else spread * noise
        out[name] = __import__('jax').numpy.asarray(drawn.astype(out[name].dtype))
    for name, factor in factors.items():
        out[name] = (out[name] * factor).astype(out[name].dtype)
    return out
```

```python
from contextlib import ExitStack

import numpy as np

import concourse.bass as bass
from concourse import mybir

F32 = mybir.dt.float32
F32R = mybir.dt.float32r
BF16 = mybir.dt.bfloat16
I32 = mybir.dt.int32
ALU = mybir.AluOpType
ACT = mybir.ActivationFunctionType
AX = mybir.AxisListType

P = 128
D = 1024
SEQ = 256
RB = SEQ // P
KC = D // P
KINDS = "ABCA"
N_A, N_BC = 2, 1
HD = 64
NH = 12
MIX = NH * HD
MEM_H = 4
MEMW = MEM_H * HD
IDX_H = 8
IDX_W = IDX_H * HD
ROPE_HALF = HD // 8
ROPE_THETA = 500000.0
TOPK = min(256, SEQ // 4)
DIL = 3
DIL_H = 4
DIL_V = MIX // DIL_H
D_FF = 2816
FF_STEP = 256
FF_STEPS = D_FF // FF_STEP
ALPHA = float((2 * len(KINDS)) ** 0.25)
LN_EPS = 1e-5
DEPTH_2 = 2
CHUNK = 64
RET_H, RET_D = 4, 128
SB_H, SB_D = 8, 64
D_HALF = 512
EPS_2 = 1e-6
ROPE_BASE = 10000.0

TW = 2048
BLK = 512
RING = 3
BIG = -1.0e30
TAKEN = -3.0e38


def weight_plan():
    tiles = []

    def block(name, layer, c0):
        tiles.extend((name, layer, "half", (c0, k0), TW) for k0 in (0, 4))

    ia = 0
    for layer, kind in enumerate(KINDS):
        if kind == "A":
            block("w_in_a", ia, 3 * MIX)
            tiles.append(("w_in_a", ia, "narrow", 3 * MIX + IDX_W, KC * (IDX_H + HD)))
            name, j = "w_in_a", ia
            ia += 1
        else:
            name, j = ("w_in_b" if kind == "B" else "w_in_c"), 0
        for c in range(5):
            block(name, j, ("proj", c))
        block("w_mem_kv", layer, 0)
        for c in range(2):
            block("w_out", layer, c * BLK)
        order = [("up", 0), ("up", 1), ("down", 0)]
        for s in range(2, FF_STEPS):
            order += [("up", s), ("down", s - 1)]
        order.append(("down", FF_STEPS - 1))
        for what, s in order:
            if what == "up":
                tiles.extend(("w_gate_up", layer, "up", (s, k0), TW) for k0 in (0, 4))
            else:
                tiles.append(("w_down", layer, "down", s, TW))
    for layer in range(DEPTH_2):
        for c in range(6):
            block("w_ada_2", layer, c * BLK)
        for c in range(8):
            block("w_in_2", layer, c * BLK)
        for c in range(2):
            block("w_out_2", layer, c * BLK)
    return tiles



class Counter:

    def __init__(self, sem):
        self.sem, self.n = sem, 0


class Loop:
    def __init__(self, trips, counters):
        self.trips, self.start, self.per = trips, {c: c.n for c in counters}, {}


class Plan:
    ENGINES = ("pe", "act", "dve", "pool")

    def __init__(self, nc, ctx):
        self.nc, self.ctx = nc, ctx
        self.queue = {e: [] for e in self.ENGINES}
        self.counters = []
        self.loop = None
        self.done = {e: self.counter(f"{e}_done") for e in self.ENGINES}

    def counter(self, name):
        c = Counter(self.ctx.enter_context(self.nc.semaphore(name)))
        self.counters.append(c)
        return c

    def op(self, engine, fn, wait=(), inc=None, by=1):
        inc = inc or self.done[engine]
        inc.n += by
        self.queue[engine].append((fn, tuple(wait), inc, by))
        return (inc, inc.n)

    def begin(self, trips):
        self.loop = Loop(trips, self.counters)
        for q in self.queue.values():
            q.append(self.loop)

    def end(self):
        loop, self.loop = self.loop, None
        for c, n in loop.start.items():
            loop.per[c] = c.n - n
            c.n += (loop.trips - 1) * loop.per[c]
        for q in self.queue.values():
            q.append(None)
        return loop

    @staticmethod
    def last_trip(loop, mark):
        c, v = mark
        return (c, v + (loop.trips - 1) * loop.per[c])

    def emit(self, name, engine):
        items = iter(self.queue[name])
        waited = {}

        def one(item, loop, i):
            fn, waits, inc, by = item
            for c, v in waits:
                per = loop.per[c] if loop else 0
                if per:
                    engine.wait_ge(c.sem, i * per + v)
                elif waited.get(c, 0) < v:
                    engine.wait_ge(c.sem, v)
                    waited[c] = v
            fn(engine).then_inc(inc.sem, by)

        for item in items:
            if isinstance(item, Loop):
                loop, body = item, []
                for inner in items:
                    if inner is None:
                        break
                    body.append(inner)
                if body:
                    with engine.Fori(0, loop.trips) as i:
                        for inner in body:
                            one(inner, loop, i)
            else:
                one(item, None, None)



def stack_kernel(nc, T, out):
    tiles = weight_plan()
    with ExitStack() as ctx:
        plan = Plan(nc, ctx)
        op = plan.op

        def sb(name, shape, dt=F32):
            return ctx.enter_context(nc.sbuf_tensor(name, shape, dt))

        raw = sb("w_raw", [P, RING, TW])
        w_hi = sb("w_high", [P, RING, TW], F32R)
        w_lo = sb("w_low", [P, RING, TW], F32R)
        xt_hi = sb("xt_high", [P, KC, SEQ], F32R)
        xt_lo = sb("xt_low", [P, KC, SEQ], F32R)
        ht_hi = sb("ht_high", [P, 2, SEQ], F32R)
        ht_lo = sb("ht_low", [P, 2, SEQ], F32R)
        x = sb("x_rows", [P, RB, D])
        arena = sb("arena", [P, 10240])
        work = sb("work", [P, 4096])
        kv = sb("mem_kv", [P, 1536])
        par = sb("norm_params", [P, 2, 2 * D])
        proj = arena[:, 0:5120].rearrange("p (r c) -> p r c", r=RB)
        mixed = proj[:, :, 0:D]
        qt = arena[:, 5120:6656].rearrange("p (c s) -> p c s", s=SEQ)
        kt = arena[:, 6656:8192].rearrange("p (c s) -> p c s", s=SEQ)
        qmt = arena[:, 8192:8704].rearrange("p (c s) -> p c s", s=SEQ)
        qit = arena[:, 8704:9728].rearrange("p (c s) -> p c s", s=SEQ)
        kit = arena[:, 9728:9984]
        ff_silu = arena[:, 0:512].rearrange("p (r c) -> p r c", r=RB)
        ff_h = arena[:, 512:1024].rearrange("p (r c) -> p r c", r=RB)
        prob = [work[:, 1024 * n:1024 * n + 1024] for n in range(2)]
        probt = [work[:, 2048 + 1024 * n:3072 + 1024 * n] for n in range(2)]
        idx = work[:, 2048:2048 + RB * 704].rearrange("p (r c) -> p r c", r=RB)
        mkv = kv[:, 0:1024].rearrange("p (r c) -> p r c", r=RB)
        mkt = kv[:, 1024:1536].rearrange("p (c s) -> p c s", s=SEQ)
        score = sb("idx_score", [P, RB, SEQ])
        select = sb("select_bias", [P, RB, SEQ], BF16)
        proj2 = arena[:, 0:8192].rearrange("p (r c) -> p r c", r=RB)
        rows2 = work[:, 0:2048].rearrange("p (r c) -> p r c", r=RB)
        tmp2 = work[:, 2048:4096]
        ident = sb("ident", [P, P])
        masks = sb("masks", [P, 7 * P], BF16)
        identb, m_win, m_causal = masks[:, 0:128], masks[:, 128:256], masks[:, 256:384]
        m_pair = [masks[:, 128:384], masks[:, 384:640], masks[:, 640:896]]
        causal = sb("causal", [P, SEQ])
        half_neg = sb("half_neg", [P, 8])
        rope_c = sb("rope_cos", [P, RB, ROPE_HALF])
        rope_s = sb("rope_sin", [P, RB, ROPE_HALF])
        rope_t = sb("rope_tmp", [P, 4, 24 * ROPE_HALF])
        kn_par = sb("idx_norm_params", [P, 2, HD])
        stats = sb("norm_stats", [P, RB, 4, 6])
        agg = sb("norm_mean_var", [P, RB, 4, 2])
        rstd = sb("norm_rstd", [P, RB, 4])
        negmax = sb("neg_max", [P, 2, 8])
        expsum = sb("exp_sum", [P, 2, 8])
        recip = sb("recip", [P, 2, 8])
        top8 = sb("top8", [P, RB, 8])
        col = sb("c_col", [P, KC])
        pos_i = sb("pos_int", [P, RB], I32)
        pos = sb("pos", [P, RB])
        inv = sb("inv_freq", [P, ROPE_HALF])
        ang = sb("angle", [P, RB, ROPE_HALF])
        turn = sb("turns", [P, RB, ROPE_HALF])
        strict = sb("strict", [P, P])
        memory_scope = ctx.enter_context(ExitStack())
        mt_hi = memory_scope.enter_context(nc.sbuf_tensor("memt_high", [P, KC, SEQ], F32R))
        mt_lo = memory_scope.enter_context(nc.sbuf_tensor("memt_low", [P, KC, SEQ], F32R))

        psum = ctx.enter_context(nc.psum_tensor("psum", [P, 8, BLK], F32))
        GEMM, WIDE, TRB = (0, 1), (2, 4), (6, 7)

        c_raw = [plan.counter(f"w_raw_{n}") for n in range(RING)]
        c_hi = plan.counter("w_high_done")
        c_lo = plan.counter("w_low_done")
        c_tile = plan.counter("tile_used")
        c_gate = plan.counter("ff_gate_ready")
        c_mul = plan.counter("ff_h_ready")
        c_tr = plan.counter("ff_transposed")
        c_ht_hi = plan.counter("ff_ht_high")
        c_ht_lo = plan.counter("ff_ht_low")
        c_out = plan.counter("out_stored")

        def load(name, dst, src, wait=()):
            return op("pool", lambda e: e.dma_start(dst, src), wait, inc=plan.counter(f"ld_{name}"), by=16)

        def rows(vec):
            return vec.partition_broadcast(P)

        free = {("bank", n): [] for n in range(8)}

        def held(*keys):
            return [m for k in keys for m in free.get(k, [])]

        state = {"split": 0, "tile": 0, "trb": 0, "wide": 0, "slot": 0, "par": 0}
        background = []

        def split_next():
            t = state["split"]
            if t >= len(tiles):
                return
            state["split"] += 1
            s, n = t % RING, tiles[t][4]
            c_raw[s].n += 16
            arrived = (c_raw[s], c_raw[s].n)
            used = [(c_tile, t - RING + 1)] if t >= RING else []
            hi = op("act", lambda e: e.activation(w_hi[:, s, 0:n], raw[:, s, 0:n], ACT.Copy),
                    [arrived] + used, inc=c_hi)
            op("dve", lambda e: e.tensor_tensor(w_lo[:, s, 0:n], raw[:, s, 0:n],
                                                w_hi[:, s, 0:n].bitcast(F32), ALU.subtract),
               [hi], inc=c_lo)

        def products(e, dst, a_hi, a_lo, b_hi, b_lo, first, last):
            e.matmul(dst, a_hi, b_hi, start=first, stop=False)
            e.matmul(dst, a_hi, b_lo, start=False, stop=False)
            return e.matmul(dst, a_lo, b_hi, start=False, stop=last)

        def use_tile(parts, wait):
            t = state["tile"]
            state["tile"] += 1
            split_next()
            s = t % RING
            marks = []
            for n, (fn, waits, inc) in enumerate(parts):
                ready = [(c_lo, t + 1)] + list(wait) if n == 0 else []
                fin = n == len(parts) - 1
                marks.append(op("pe", lambda e, fn=fn: fn(e, w_hi[:, s, :], w_lo[:, s, :]),
                                ready + list(waits), inc=c_tile if fin else inc))
            for _ in range(2):
                if background:
                    background.pop(0)()
            return marks

        def gemm_block(a_hi, a_lo, ready, banks, blocks=range(RB)):
            blocks = list(blocks)
            for half in range(2):
                def part(rb, half=half):
                    def fn(e, hi, lo):
                        for k in range(4):
                            kk = 4 * half + k
                            m = products(e, psum[:, banks[rb], :], a_hi[:, kk, rb * P:rb * P + P],
                                         a_lo[:, kk, rb * P:rb * P + P], hi[:, k * BLK:k * BLK + BLK],
                                         lo[:, k * BLK:k * BLK + BLK], kk == 0, kk == KC - 1)
                        return m
                    waits = (held(("bank", banks[rb])) + list(ready[rb])) if half == 0 else []
                    return (fn, waits, None)
                marks = use_tile([part(rb) for rb in blocks], [])
            return dict(zip(blocks, marks))

        def transpose_in(src, src_ready, chunks, dst_fn, width=P):
            b = TRB[state["trb"] % 2]
            state["trb"] += 1

            pieces = [src(c) for c in chunks]

            def fn(e):
                for n, piece in enumerate(pieces):
                    m = e.transpose(psum[0:width, b, n * P:n * P + P], piece, ident[:, :])
                return m
            done = op("pe", fn, held(("bank", b)) + list(src_ready))
            marks = dst_fn(psum[0:width, b, 0:len(chunks) * P], done)
            free[("bank", b)] = marks
            return marks

        def to_stationary(src, ready, dst_hi, dst_lo, rb, hold=()):
            marks = []
            for g in range(2):
                def copy(bank, done):
                    v = bank.rearrange("p (c s) -> p c s", s=P)
                    h = dst_hi[:, 4 * g:4 * g + 4, rb * P:rb * P + P]
                    low = dst_lo[:, 4 * g:4 * g + 4, rb * P:rb * P + P]
                    a = op("act", lambda e: e.activation(h, v, ACT.Copy), [done] + list(hold))
                    return [op("dve", lambda e: e.tensor_tensor(low, v, h.bitcast(F32), ALU.subtract),
                               [a, done])]
                marks += transpose_in(lambda c: src[:, c * P:c * P + P], ready, range(4 * g, 4 * g + 4), copy)
            return marks

        def transpose_to(src, ready, chunks, dst, engine, scale=1.0, hold=()):
            def copy(bank, done):
                v = bank.rearrange("p (c s) -> p c s", s=P) if len(chunks) > 1 else bank
                if engine == "act":
                    return [op("act", lambda e: e.activation(dst, v, ACT.Copy, scale=scale), [done] + list(hold))]
                return [op("dve", lambda e: e.tensor_scalar(dst, v, scale, None, ALU.mult), [done] + list(hold))]
            return transpose_in(src, ready, chunks, copy)

        def power(rb, n, ready):
            return op("pool", lambda e: e.tensor_tensor(rstd[:, rb, 0:n], rstd[:, rb, 0:n],
                                                        half_neg[:, 0:n], ALU.pow), ready)

        def norm_stats(rb, pieces, ready, eps=LN_EPS, one=True):
            for n, piece in enumerate(pieces):
                m = op("dve", lambda e, n=n, piece=piece: e.bn_stats(stats[:, rb, n, :], piece),
                       list(ready) + held("stats"))
            groups = 1 if one else len(pieces)
            for n in range(groups):
                src = (stats[:, rb, 0:len(pieces), :].rearrange("p a b -> p (a b)") if one
                       else stats[:, rb, n, :])
                m2 = op("dve", lambda e, n=n, src=src: e.bn_aggr(agg[:, rb, n, :], src), [m])
            m3 = op("dve", lambda e: e.tensor_scalar(rstd[:, rb, 0:groups], agg[:, rb, 0:groups, 1], eps,
                                                     None, ALU.add), [m2])
            return power(rb, groups, [m3])

        def norm_apply(rb, rows_rb, g, b, ready):
            ready = list(ready)
            a = op("dve", lambda e: e.scalar_tensor_tensor(out=rows_rb, in0=rows_rb, scalar=agg[:, rb, 0, 0:1],
                                                           in1=g, op0=ALU.subtract, op1=ALU.mult),
                   ready[1:])
            return op("dve", lambda e: e.scalar_tensor_tensor(out=rows_rb, in0=rows_rb, scalar=rstd[:, rb, 0:1],
                                                              in1=b, op0=ALU.mult, op1=ALU.add),
                      [a, ready[0]])

        def load_norm(name, g, b):
            s = state["par"] % 2
            state["par"] += 1
            hold = held(("par", s))
            mg = load(name + "_g", par[:, s, 0:D], rows(g), hold)
            mb = load(name + "_b", par[:, s, D:2 * D], rows(b), hold)
            return s, [mg, mb]

        k_ident = load("ident", ident[:, :], T["ident"])
        k_x = [load(f"x{rb}", x[:, rb, :], T["x"][rb * P:rb * P + P, :]) for rb in range(RB)]
        mem_rows = arena[:, 0:2048].rearrange("p (r c) -> p r c", r=RB)
        k_mem = [load(f"mem{rb}", mem_rows[:, rb, :], T["mem"][rb * P:rb * P + P, :]) for rb in range(RB)]
        mem_par, k_mem_par = load_norm("mem", T["mem_ln_g"], T["mem_ln_b"])
        k_pos = load("pos", pos_i[:, :], T["positions"])
        k_inv = load("inv", inv[:, :], rows(T["inv_freq"]))
        masks_f = work[:, 0:7 * P]
        k_masks = load("masks", masks_f, T["masks"])
        k_causal = load("causal", causal[:, :], T["causal"])
        k_hneg = op("dve", lambda e: e.memset(half_neg[:, :], -0.5))
        k_maskb = op("dve", lambda e: e.tensor_copy(masks[:, :], masks_f), [k_masks])
        free["prob"] = [k_maskb]
        const = [k_ident, k_maskb]
        ready_pe = [k_ident, k_maskb]

        two_pi = 2.0 * np.pi
        parts, rest = [], two_pi
        for bits in (8, 8, 8):
            exp = int(np.floor(np.log2(rest)))
            unit = 2.0 ** (exp - bits + 1)
            head = float(np.floor(rest / unit) * unit)
            parts.append(head)
            rest -= head
        parts.append(float(rest))
        MAGIC = 12582912.0
        PI = 3.1415925
        m = op("dve", lambda e: e.tensor_copy(pos[:, :], pos_i[:, :]), [k_pos])
        for rb in range(RB):
            ma = op("dve", lambda e, rb=rb: e.tensor_scalar(ang[:, rb, :], inv[:, :], pos[:, rb:rb + 1], None,
                                                            ALU.mult), [m, k_inv])
        m = op("dve", lambda e: e.tensor_scalar(turn[:, :, :], ang[:, :, :], float(1.0 / two_pi), MAGIC,
                                                ALU.mult, ALU.add), [ma])
        m = op("dve", lambda e: e.tensor_scalar(turn[:, :, :], turn[:, :, :], MAGIC, None, ALU.subtract), [m])
        for part in parts:
            m = op("dve", lambda e, part=part: e.scalar_tensor_tensor(
                out=ang[:, :, :], in0=turn[:, :, :], scalar=-part, in1=ang[:, :, :], op0=ALU.mult,
                op1=ALU.add), [m])
        m = op("dve", lambda e: e.tensor_scalar(rope_c[:, :, :], ang[:, :, :], float(np.pi / 2), None, ALU.add), [m])
        m = op("dve", lambda e: e.tensor_scalar(turn[:, :, :], rope_c[:, :, :], PI, -two_pi, ALU.is_gt, ALU.mult), [m])
        m = op("dve", lambda e: e.tensor_tensor(rope_c[:, :, :], rope_c[:, :, :], turn[:, :, :], ALU.add), [m])
        m = op("dve", lambda e: e.tensor_scalar(rope_c[:, :, :], rope_c[:, :, :], PI, -PI, ALU.min, ALU.max), [m])
        m = op("dve", lambda e: e.tensor_scalar(ang[:, :, :], ang[:, :, :], PI, -PI, ALU.min, ALU.max), [m])
        k_cos = op("act", lambda e: e.activation(rope_c[:, :, :], rope_c[:, :, :], ACT.Sin), [m])
        k_rope = [k_cos, op("act", lambda e: e.activation(rope_s[:, :, :], ang[:, :, :], ACT.Sin), [m])]

        for _ in range(2):
            split_next()
        xt = [to_stationary(x[:, rb, :], ready_pe + [k_x[rb]], xt_hi, xt_lo, rb) for rb in range(RB)]
        mt = []
        for rb in range(RB):
            r = norm_stats(rb, [mem_rows[:, rb, 0:512], mem_rows[:, rb, 512:1024]], [k_mem[rb]])
            r = norm_apply(rb, mem_rows[:, rb, :], par[:, mem_par, 0:D], par[:, mem_par, D:2 * D],
                           [r] + k_mem_par)
            free[("par", mem_par)] = [r]
            mt.append(to_stationary(mem_rows[:, rb, :], [r], mt_hi, mt_lo, rb))
        free["proj"] = [mt[1][-1]]

        def evacuate(banks, marks, dst, wait=(), func=ACT.Copy):
            done = []
            for rb in range(RB):
                v = psum[:, banks[rb], :]
                w = [marks[rb]] + list(wait)
                if rb == 0 or func != ACT.Copy:
                    d = op("act", lambda e, rb=rb, v=v: e.activation(dst(rb), v, func), w)
                else:
                    d = op("dve", lambda e, rb=rb, v=v: e.tensor_copy(dst(rb), v), w)
                free[("bank", banks[rb])] = [d]
                done.append(d)
            return done

        def rotary(rb, v, heads, half, cos, sin, tmp, ready):
            n = heads * half
            t = [tmp[k].rearrange("p (h d) -> p h d", d=half) for k in range(4)]
            c = cos.unsqueeze(1).broadcast_to([P, heads, half])
            s = sin.unsqueeze(1).broadcast_to([P, heads, half])
            x1, x2 = v[:, :, 0:half], v[:, :, half:2 * half]
            w = list(ready) + held("rope_tmp")
            for k, (a, b) in enumerate(((x1, c), (x2, s), (x2, c), (x1, s))):
                m = op("dve", lambda e, k=k, a=a, b=b: e.tensor_tensor(t[k], a, b, ALU.mult), w)
            op("dve", lambda e: e.tensor_tensor(x1, t[0], t[1], ALU.subtract), [m])
            m = op("dve", lambda e: e.tensor_tensor(x2, t[2], t[3], ALU.add), [m])
            free["rope_tmp"] = [m]
            return m

        def rope_heads(rb, cols, heads, ready):
            v = cols.rearrange("p (h d) -> p h d", d=HD)
            tmp = [rope_t[:, k, 0:heads * ROPE_HALF] for k in range(4)]
            return rotary(rb, v, heads, ROPE_HALF, rope_c[:, rb, :], rope_s[:, rb, :], tmp, ready)

        def head_cols(t, h, s0, n):
            p0 = HD * (h % 2)
            return t[p0:p0 + HD, h // 2, s0:s0 + n]

        def wide_pair():
            b = WIDE[state["wide"] % 2]
            state["wide"] += 1
            return b

        def score_pieces(b, n_pieces, nk, joint):
            if joint:
                flat = psum[:, b:b + 2, :].rearrange("p b c -> p (b c)")
                return [(n * nk // BLK, flat[:, n * nk:n * nk + nk]) for n in range(n_pieces)]
            return [(n % 2, psum[:, b + n % 2, n // 2 * nk:n // 2 * nk + nk]) for n in range(n_pieces)]

        def accumulate(e, pieces, products_of, nk):
            banks = [pieces[n][0] for n, *_ in products_of]
            for i, (n, left, right, cols) in enumerate(products_of):
                dst = pieces[n][1] if cols is None else pieces[n][1][:, nk - cols:nk]
                m = e.matmul(dst, left, right, start=banks[i] not in banks[:i], stop=banks[i] not in banks[i + 1:])
            return m

        def attention_unit(segments, rb, joint, values, dst, ready):
            nk = segments[0][3]
            b = wide_pair()
            slot = state["slot"] % 2
            state["slot"] += 1
            pr, pt = prob[slot], probt[slot]
            nseg = len(segments)
            pieces_l = score_pieces(b, nseg, nk, joint)

            def scores(e):
                work_list = [(n, q, k, None) for n, (q, k, _, _) in enumerate(segments)]
                work_list += [(n, identb, bias, bias.shape[1]) for n, (_, _, bias, _) in enumerate(segments)
                              if bias is not None]
                return accumulate(e, pieces_l, work_list, nk)
            s = op("pe", scores, list(ready) + held(("bank", b), ("bank", b + 1)))
            nmax = 1 if joint else nseg
            if joint:
                view = psum[:, b:b + 2, :].rearrange("p b c -> p (b c)")[:, 0:nseg * nk]
                nm_out = negmax[:, slot, 0:1]
            else:
                view = psum[:, b:b + 2, 0:nseg // 2 * nk].rearrange("p b (h k) -> p b h k", k=nk)
                nm_out = negmax[:, slot, 0:nseg].rearrange("p (h b) -> p b h", b=2)
            mx = op("dve", lambda e: e.tensor_reduce(nm_out, view, AX.X, ALU.max, negate=True),
                    [s] + held(("negmax", slot)))
            for n in range(nmax):
                src = view if joint else pieces_l[n][1]
                dst_p = pr[:, 0:nseg * nk] if joint else pr[:, n * nk:n * nk + nk]
                ex = op("act", lambda e, n=n, src=src, dst_p=dst_p: e.activation(
                    dst_p, src, ACT.Exp, bias=negmax[:, slot, n:n + 1], accum_out=expsum[:, slot, n:n + 1]),
                    [mx] + held(("prob", slot), "prob", ("expsum", slot)))
            free[("bank", b)] = free[("bank", b + 1)] = [ex]
            free[("negmax", slot)] = [ex]
            rc = op("dve", lambda e: e.reciprocal(recip[:, slot, 0:nmax], expsum[:, slot, 0:nmax]),
                    [ex] + held(("recip", slot)))
            free[("expsum", slot)] = [rc]
            pready = ex
            if joint:
                for n in range(1, nseg):
                    pready = op("dve", lambda e, n=n: e.tensor_tensor(
                        pr[:, 0:nk], pr[:, 0:nk], pr[:, n * nk:n * nk + nk], ALU.add), [pready])
            pieces = [(n, kb) for n in range(nmax) for kb in range(nk // P)]
            for g in range(0, len(pieces), 4):
                some = pieces[g:g + 4]
                eng = "act" if (g // 4) % 2 else "dve"
                last = transpose_to(lambda i: pr[:, i[0] * nk + i[1] * P:i[0] * nk + i[1] * P + P], [pready],
                                    some, (pt[:, g * P:(g + len(some)) * P].rearrange("p (c s) -> p c s", s=P)
                                           if len(some) > 1 else pt[:, g * P:g * P + P]),
                                    eng, hold=held(("probt", slot), "probt"))
                if g == 0:
                    tmarks = []
                tmarks += last
            free[("prob", slot)] = list(tmarks)
            ob = GEMM[slot]

            def weighted(e):
                c = 0
                for n in range(nmax):
                    for kb in range(nk // P):
                        v, w = values(n, kb)
                        m = e.matmul(psum[:, ob, n * w:n * w + w], pt[:, (n * (nk // P) + kb) * P:(n * (nk // P) + kb + 1) * P],
                                     v, start=kb == 0, stop=kb == nk // P - 1)
                return m
            wv = op("pe", weighted, tmarks + held(("bank", ob)))
            free[("probt", slot)] = [wv]
            w = values(0, 0)[1]
            nm = op("dve", lambda e: e.tensor_tensor(
                dst.rearrange("p (h d) -> p h d", d=w), psum[:, ob, 0:nmax * w].rearrange("p (h d) -> p h d", d=w),
                recip[:, slot, 0:nmax].unsqueeze(2).broadcast_to([P, nmax, w]), ALU.mult), [wv, rc])
            free[("bank", ob)] = [nm]
            free[("recip", slot)] = [nm]
            return nm

        def indexer(a, xt_ready):
            wide = 2 * HD
            kp = [load(f"idx_g{a}", kn_par[:, 0, :], rows(T["idx_kn_g"][a]), held("kn_par")),
                  load(f"idx_b{a}", kn_par[:, 1, :], rows(T["idx_kn_b"][a]), held("kn_par"))]
            marks = gemm_block(xt_hi, xt_lo, xt_ready, GEMM)
            qi = evacuate(GEMM, marks, lambda rb: idx[:, rb, 0:IDX_W],
                          held(("probt", 0), ("probt", 1), "work"))

            def part(rb):
                def fn(e, hi, lo):
                    w = IDX_H + HD
                    for k in range(KC):
                        m = products(e, psum[:, GEMM[rb], 0:w], xt_hi[:, k, rb * P:rb * P + P],
                                     xt_lo[:, k, rb * P:rb * P + P], hi[:, k * w:k * w + w],
                                     lo[:, k * w:k * w + w], k == 0, k == KC - 1)
                    return m
                return (fn, held(("bank", GEMM[rb])), None)
            marks = use_tile([part(rb) for rb in range(RB)], [])
            biases = []
            for rb in range(RB):
                def whole(rb=rb):
                    w_cols = idx[:, rb, IDX_W:IDX_W + IDX_H]
                    ki = idx[:, rb, IDX_W + IDX_H:IDX_W + IDX_H + HD]
                    ki2 = idx[:, rb, IDX_W + IDX_H + HD:IDX_W + IDX_H + wide]
                    both = idx[:, rb, IDX_W + IDX_H:IDX_W + IDX_H + wide]
                    bank = psum[:, GEMM[rb], 0:IDX_H + HD]
                    a1 = op("dve", lambda e: e.tensor_scalar(w_cols, bank[:, 0:IDX_H], float((IDX_H * HD) ** -0.5),
                                                             None, ALU.mult),
                            [marks[rb]] + held(("probt", 0), ("probt", 1), "work"))
                    a2 = op("dve", lambda e: e.tensor_copy(ki, bank[:, IDX_H:IDX_H + HD]), [marks[rb]])
                    free[("bank", GEMM[rb])] = [a2]
                    r = norm_stats(rb, [ki], [a2])
                    r = norm_apply(rb, ki, kn_par[:, 0, :], kn_par[:, 1, :], [r] + kp)
                    free["kn_par"] = [r]
                    r = rope_heads(rb, ki, 1, [r] + k_rope)
                    r2 = op("dve", lambda e: e.tensor_copy(ki2, ki), [r])
                    q = rope_heads(rb, idx[:, rb, 0:IDX_W], IDX_H, [qi[rb]] + k_rope)
                    t1 = transpose_to(lambda c: both, [r2], [0], kit[:, rb * P:rb * P + P], "act",
                                      hold=held("qit"))
                    t2 = transpose_to(lambda c: idx[:, rb, c * P:c * P + P], [q], range(4),
                                      qit[:, :, rb * P:rb * P + P], "act", hold=held("qit"))
                    biases.append((a1, t1 + t2))
                whole()
            tr = [m for _, t in biases for m in t]
            k_idx_w = [b[0] for b in biases]
            out_marks = [None, None]

            def choose(rb):
                nk = (rb + 1) * P
                per = 1024 // nk
                acc = causal[:, (1 - rb) * P:(1 - rb) * P + nk]
                m = k_causal
                for g in range(0, IDX_H, per):
                    b = wide_pair()
                    dots = psum[:, b:b + 2, :]
                    pieces = score_pieces(b, per, nk, False)
                    slot = state["slot"] % 2
                    state["slot"] += 1

                    def fn(e, g=g, pieces=pieces):
                        return accumulate(e, pieces, [
                            (n, head_cols(qit, g + n, rb * P, P), kit[HD * (n % 2):HD * (n % 2) + HD, 0:nk], None)
                            for n in range(per)], nk)
                    s = op("pe", fn, tr + held(("bank", b), ("bank", b + 1)))
                    r = op("act", lambda e, dots=dots, slot=slot: e.activation(prob[slot].rearrange("p (b c) -> p b c", b=2), dots, ACT.Relu),
                           [s] + held(("prob", slot), "prob"))
                    free[("bank", b)] = free[("bank", b + 1)] = [r]
                    for n in range(per):
                        h, at = g + n, n % 2 * BLK + n // 2 * nk
                        m = op("dve", lambda e, at=at, h=h, slot=slot, acc=acc: e.scalar_tensor_tensor(
                            out=score[:, rb, 0:nk], in0=prob[slot][:, at:at + nk],
                            scalar=idx[:, rb, IDX_W + h:IDX_W + h + 1], in1=acc, op0=ALU.mult, op1=ALU.add),
                            [m, r, k_idx_w[rb]] + held(("score", rb)))
                        acc = score[:, rb, 0:nk]
                    free[("prob", slot)] = [m]
                return m

            def rounds(rb, m):
                nk = (rb + 1) * P
                v = score[:, rb, 0:nk]
                for _ in range(TOPK // 8):
                    m = op("dve", lambda e: e.max(top8[:, rb, :], v), [m])
                    m = op("dve", lambda e: e.match_replace(v, top8[:, rb, :], v, TAKEN), [m])
                m = op("dve", lambda e: e.tensor_scalar(v, v, -2.0e38, BIG, ALU.is_ge, ALU.mult), [m])
                m = op("dve", lambda e: e.tensor_tensor(select[:, rb, 0:nk], v, causal[:, (1 - rb) * P:(1 - rb) * P + nk],
                                                        ALU.add), [m] + held("select"))
                free[("score", rb)] = [m]
                out_marks[rb] = m

            for rb in range(RB):
                rounds(rb, choose(rb))
            free["work"] = [out_marks[1]]
            free["probt"] = [out_marks[1]]
            free["qit"] = [out_marks[1]]
            return out_marks

        def feed_forward(xt_ready):
            acc = [[2 + 2 * rb + h for h in range(2)] for rb in range(RB)]

            def up(ready, banks_free):
                for half in range(2):
                    def part(rb, half=half):
                        def fn(e, hi, lo):
                            for k in range(4):
                                kk = 4 * half + k
                                m = products(e, psum[:, GEMM[rb], :], xt_hi[:, kk, rb * P:rb * P + P],
                                             xt_lo[:, kk, rb * P:rb * P + P], hi[:, k * BLK:k * BLK + BLK],
                                             lo[:, k * BLK:k * BLK + BLK], kk == 0, kk == KC - 1)
                            return m
                        w = (list(ready[rb]) + [banks_free[rb]] if ready else [banks_free[rb]]) if half == 0 else []
                        return (fn, w, c_gate if half else None)
                    marks = use_tile([part(rb) for rb in range(RB)], [])
                return marks

            def gate(marks, muls, tr):
                done = []
                for rb in range(RB):
                    bank = psum[:, GEMM[rb], :]
                    s = op("act", lambda e, rb=rb, bank=bank: e.activation(ff_silu[:, rb, :], bank[:, 0:FF_STEP], ACT.Silu),
                           [marks[rb], muls[rb]] if muls else [marks[rb]] + held("proj"))
                    done.append(op("dve", lambda e, rb=rb, bank=bank: e.tensor_tensor(
                        ff_h[:, rb, :], ff_silu[:, rb, :], bank[:, FF_STEP:BLK], ALU.mult),
                        [s] + ([tr] if tr else []), inc=c_mul))
                return done

            def turn_h(muls, lo, used):
                def fn(e):
                    for c in range(2):
                        for rb in range(RB):
                            m = e.transpose(psum[:, 6, (2 * c + rb) * P:(2 * c + rb + 1) * P],
                                            ff_h[:, rb, c * P:c * P + P], ident[:, :])
                    return m
                tr = op("pe", fn, list(muls) + ([lo] if lo else held(("bank", 6))), inc=c_tr)
                v = psum[:, 6, :].rearrange("p (c s) -> p c s", s=SEQ)
                h = op("act", lambda e: e.activation(ht_hi[:, :, :], v, ACT.Copy), [tr] + used, inc=c_ht_hi)
                low = op("dve", lambda e: e.tensor_tensor(ht_lo[:, :, :], v, ht_hi[:, :, :].bitcast(F32),
                                                          ALU.subtract), [h], inc=c_ht_lo)
                return tr, low

            def down(low, first, last):
                def part(rb):
                    def fn(e, hi, lo):
                        for c in range(2):
                            for h in range(2):
                                w = c * D + h * BLK
                                m = products(e, psum[:, acc[rb][h], :], ht_hi[:, c, rb * P:rb * P + P],
                                             ht_lo[:, c, rb * P:rb * P + P], hi[:, w:w + BLK], lo[:, w:w + BLK],
                                             first and c == 0, last and c == 1)
                        return m
                    w = [low] if rb == 0 else []
                    if first:
                        w += held(("bank", acc[rb][0]), ("bank", acc[rb][1]))
                    return (fn, w, None)
                return use_tile([part(rb) for rb in range(RB)], [])

            marks = up(xt_ready, [held(("bank", GEMM[rb]))[0] for rb in range(RB)])
            muls = gate(marks, None, None)
            tr, low = turn_h(muls, None, [])
            marks = up(None, muls)
            muls = gate(marks, muls, tr)
            used = down(low, True, False)
            tr, low = turn_h(muls, low, [used[-1]])
            plan.begin(FF_STEPS - 2)
            t_in = state["tile"]
            marks = up(None, muls)
            muls = gate(marks, muls, tr)
            used = down(low, False, False)
            tr, low = turn_h(muls, low, [used[-1]])
            loop = plan.end()
            more = (FF_STEPS - 3) * 3
            assert state["tile"] - t_in == 3
            state["tile"] += more
            state["split"] += more
            muls = [plan.last_trip(loop, m) for m in muls]
            low = plan.last_trip(loop, low)
            for rb in range(RB):
                free[("bank", GEMM[rb])] = [muls[rb]]
            free[("bank", 6)] = [low]
            free["proj"] = [muls[1]]
            marks = down(low, False, True)
            return marks, acc

        def residual_norm(marks, banks, s, par_ready):
            rs = []
            for rb in range(RB):
                for h in range(2):
                    v = x[:, rb, h * BLK:h * BLK + BLK]
                    m = op("dve", lambda e, v=v, rb=rb, h=h: e.scalar_tensor_tensor(
                        out=v, in0=v, scalar=ALPHA, in1=psum[:, banks[rb][h], :], op0=ALU.mult, op1=ALU.add),
                        [marks[rb][h]] + held("x"))
                    free[("bank", banks[rb][h])] = [m]
                rs.append(norm_stats(rb, [x[:, rb, 0:512], x[:, rb, 512:1024]], [m]))
            ready = []
            for rb in range(RB):
                r = norm_apply(rb, x[:, rb, :], par[:, s, 0:D], par[:, s, D:2 * D], [rs[rb]] + par_ready)
                free[("par", s)] = [r]
                ready.append(to_stationary(x[:, rb, :], [r], xt_hi, xt_lo, rb, hold=[(c_tile, state["tile"])]))
            return ready

        def out_product(name_ready):
            banks = [[2 + 2 * rb + h for h in range(2)] for rb in range(RB)]
            marks = [[None, None], [None, None]]
            for h in range(2):
                done = gemm_block(xt_hi, xt_lo, name_ready, [banks[rb][h] for rb in range(RB)])
                for rb in range(RB):
                    marks[rb][h] = done[rb]
            return marks, banks

        a = 0
        for layer, kind in enumerate(KINDS):
            ln1, k_ln1 = load_norm(f"ln1_{layer}", T["ln1_g"][layer], T["ln1_b"][layer])
            ln2, k_ln2 = load_norm(f"ln2_{layer}", T["ln2_g"][layer], T["ln2_b"][layer])
            chosen = None
            if kind == "A":
                chosen = indexer(a, xt)
                a += 1
            blocks = []
            for c in range(5):
                marks = gemm_block(xt_hi, xt_lo, xt, GEMM)
                blocks.append(evacuate(GEMM, marks, lambda rb, c=c: proj[:, rb, c * BLK:c * BLK + BLK],
                                       held("proj")))
            xt_used = (c_tile, state["tile"])
            ready = {}
            for rb in range(RB):
                r = rope_heads(rb, proj[:, rb, 0:2 * MIX], 2 * NH, [blocks[c][rb] for c in range(3)] + k_rope)
                w = held("heads")
                tq = transpose_to(lambda n: proj[:, rb, n * P:n * P + P], [r], range(0, 4),
                                  qt[:, 0:4, rb * P:rb * P + P], "act", HD ** -0.5, w)
                tq += transpose_to(lambda n: proj[:, rb, n * P:n * P + P], [r], range(4, 6),
                                   qt[:, 4:6, rb * P:rb * P + P], "dve", HD ** -0.5, w)
                tk = transpose_to(lambda n: proj[:, rb, MIX + n * P:MIX + n * P + P], [r], range(0, 4),
                                  kt[:, 0:4, rb * P:rb * P + P], "act", 1.0, w)
                tk += transpose_to(lambda n: proj[:, rb, MIX + n * P:MIX + n * P + P], [r], range(4, 6),
                                   kt[:, 4:6, rb * P:rb * P + P], "dve", 1.0, w)
                tm = transpose_to(lambda n: proj[:, rb, 3 * MIX + n * P:3 * MIX + n * P + P], [blocks[4][rb]],
                                  range(2), qmt[:, :, rb * P:rb * P + P], "act", HD ** -0.5, w)
                ready[rb] = (tq, tk, tm)
            vready = [blocks[c][rb] for c in (3, 4) for rb in range(RB)]
            turned = [m for rb in range(RB) for t in ready[rb] for m in t]
            marks = gemm_block(mt_hi, mt_lo, mt, GEMM)
            mk = evacuate(GEMM, marks, lambda rb: mkv[:, rb, :], held("mkv"))
            tmk = []
            for rb in range(RB):
                tmk += transpose_to(lambda n: mkv[:, rb, n * P:n * P + P], [mk[rb]], range(2),
                                    mkt[:, :, rb * P:rb * P + P], "dve", 1.0, held("mkv"))
            outs = [[], []]
            for rb in range(RB):
                nk = (rb + 1) * P
                seg = [(head_cols(qmt, h, rb * P, P), head_cols(mkt, h, 0, SEQ), None, SEQ) for h in range(MEM_H)]
                outs[rb].append(attention_unit(
                    seg, rb, False, lambda n, kb: (mkv[:, kb, MEMW + n * HD:MEMW + n * HD + HD], HD),
                    mixed[:, rb, MIX:MIX + MEMW], turned + tmk + mk))
                if kind == "B":
                    for h in range(DIL_H):
                        seg = [(head_cols(qt, g * DIL_H + h, rb * P, P), head_cols(kt, g * DIL_H + h, 0, nk),
                                m_pair[g] if rb else m_pair[g][:, P:2 * P], nk) for g in range(DIL)]
                        outs[rb].append(attention_unit(
                            seg, rb, True, lambda n, kb, h=h: (proj[:, kb, 2 * MIX + h * DIL_V:2 * MIX + h * DIL_V + DIL_V], DIL_V),
                            mixed[:, rb, h * DIL_V:h * DIL_V + DIL_V], turned + vready))
                else:
                    per = 4 if rb else 6
                    for h0 in range(0, NH, per):
                        bias = select[:, rb, 0:nk] if kind == "A" else m_causal
                        seg = [(head_cols(qt, h, rb * P, P), head_cols(kt, h, 0, nk), bias, nk)
                               for h in range(h0, h0 + per)]
                        outs[rb].append(attention_unit(
                            seg, rb, False,
                            lambda n, kb, h0=h0: (proj[:, kb, 2 * MIX + (h0 + n) * HD:2 * MIX + (h0 + n) * HD + HD], HD),
                            mixed[:, rb, h0 * HD:(h0 + per) * HD],
                            turned + vready + ([chosen[rb]] if chosen else [])))
            free["heads"] = [outs[1][-1]]
            free["select"] = [outs[1][-1]]
            free["mkv"] = [outs[1][-1]]
            free["probt"] = free["work"] = free["prob"] = []
            mx = [to_stationary(mixed[:, rb, :], [outs[rb][-1]], xt_hi, xt_lo, rb, hold=[xt_used])
                  for rb in range(RB)]
            free["proj"] = [m for t in mx for m in t]
            marks, banks = out_product(mx)
            xt = residual_norm(marks, banks, ln1, k_ln1)
            marks, banks = feed_forward(xt)
            xt = residual_norm([[m, m] for m in marks], banks, ln2, k_ln2)

        mod = par[:, :, :].rearrange("p s c -> p (s c)")
        shift, gain, gate_row, gvec = [mod[:, n * D:n * D + D] for n in range(4)]
        decay = kv[:, 0:1536].rearrange("p (h c) -> p h c", h=RET_H)
        memory_scope.close()
        cb_hi = sb("c_high", [P, KC, P], F32R)
        cb_lo = sb("c_low", [P, KC, P], F32R)
        rt = sb("heads_t2", [P, 8, SEQ])
        k_par_free = held(("par", 0), ("par", 1))
        k_decay = load("decay", decay, T["decay"], held("mkv"))
        ret_cs = score
        k_ret = load("ret_cs", ret_cs[:, :, 0:P], T["ret_cos_sin"].rearrange("(r p) c -> p r c", p=P),
                     held(("score", 0), ("score", 1)))
        tri = causal
        k_tri = load("tri", tri[:, :], T["tri"], held("select"))
        k_strict = load("strict", strict[:, :], T["strict"])
        strict_b_f = rt[:, 0, 0:P]
        k_sbf = load("strict_bias", strict_b_f, T["strict_bias"], held("mkv"))
        strict_b = masks[:, P:2 * P]
        k_sb = op("dve", lambda e: e.tensor_copy(strict_b, strict_b_f), [k_sbf] + held("select"))
        free["rt"] = [k_sb]
        k_c = load("c", col[:, :], T["c_2"])
        k_c = op("act", lambda e: e.activation(col[:, :], col[:, :], ACT.Silu), [k_c])
        cb = col[:, :].unsqueeze(2).broadcast_to([P, KC, P])
        c1 = op("act", lambda e: e.activation(cb_hi[:, :, :], cb, ACT.Copy), [k_c] + held("mkv"))
        c2 = op("dve", lambda e: e.tensor_tensor(cb_lo[:, :, :], cb, cb_hi[:, :, :].bitcast(F32), ALU.subtract),
                [c1])
        xready = [m for t in xt for m in t]

        def rms(rb, ready, scratch):
            q = op("act", lambda e: e.activation(scratch, x[:, rb, :], ACT.Square, accum_out=expsum[:, rb, 0:1]),
                   list(ready) + held(("expsum", 0), ("expsum", 1), "work"))
            m = op("dve", lambda e: e.tensor_scalar(rstd[:, rb, 0:1], expsum[:, rb, 0:1], 1.0 / D, EPS_2,
                                                    ALU.mult, ALU.add), [q])
            free[("expsum", rb)] = [m]
            return power(rb, 1, [m])

        for layer in range(DEPTH_2):
            k_b = [load(f"b_ada{layer}", mod[:, 0:3 * D], rows(T["b_ada_2"][layer]), k_par_free),
                   load(f"g2_{layer}", gvec, rows(T["norm_g_2"][layer]), k_par_free)]
            rs = [rms(rb, xready, rows2[:, rb, :]) for rb in range(RB)]
            mods = []
            for c in range(6):
                bank = GEMM[c % 2]
                marks = gemm_block(cb_hi, cb_lo, {0: [c2]}, [bank], [0])
                v = mod[:, c * BLK:c * BLK + BLK]
                m = op("dve", lambda e, v=v, bank=bank: e.tensor_tensor(v, psum[:, bank, :], v, ALU.add),
                       [marks[0]] + k_b)
                free[("bank", bank)] = [m]
                if c in (2, 3):
                    g = gvec[:, (c - 2) * BLK:(c - 1) * BLK]
                    m = op("dve", lambda e, v=v, g=g: e.scalar_tensor_tensor(
                        out=v, in0=v, scalar=1.0, in1=g, op0=ALU.add, op1=ALU.mult), [m])
                mods.append(m)
            ready = []
            for rb in range(RB):
                m = op("dve", lambda e, rb=rb: e.scalar_tensor_tensor(
                    out=rows2[:, rb, :], in0=x[:, rb, :], scalar=rstd[:, rb, 0:1], in1=gain, op0=ALU.mult,
                    op1=ALU.mult), [mods[3], rs[rb]])
                m = op("dve", lambda e, rb=rb: e.tensor_tensor(rows2[:, rb, :], rows2[:, rb, :], shift, ALU.add), [m])
                ready.append(to_stationary(rows2[:, rb, :], [m], xt_hi, xt_lo, rb, hold=[(c_tile, state["tile"])]))
            blocks = []
            for c in range(8):
                marks = gemm_block(xt_hi, xt_lo, ready, GEMM)
                blocks.append(evacuate(GEMM, marks, lambda rb, c=c: proj2[:, rb, c * BLK:c * BLK + BLK],
                                       held("proj", "heads"), ACT.Silu if c % 4 == 3 else ACT.Copy))
            xt_used = (c_tile, state["tile"])
            tr = []
            for rb in range(RB):
                v = proj2[:, rb, 0:D].rearrange("p (h d) -> p h d", d=RET_D)
                tmp = [tmp2[:, k * 512:k * 512 + 512] for k in range(4)]
                r = rotary(rb, v, 8, RET_D // 2, ret_cs[:, rb, 0:64], ret_cs[:, rb, 64:128], tmp,
                           [blocks[0][rb], blocks[1][rb], k_ret] + held("work"))
                for g in range(2):
                    tr += transpose_to(lambda n: proj2[:, rb, n * P:n * P + P], [r], range(4 * g, 4 * g + 4),
                                       rt[:, 4 * g:4 * g + 4, rb * P:rb * P + P], "act" if g else "dve", 1.0,
                                       held("rt"))
            ret_scores = [tmp2[:, 512 * n:512 * n + 384] for n in range(2)]
            y_marks = [[], []]
            vr = [blocks[2][rb] for rb in range(RB)]
            last_rot = held("rope_tmp")
            for h in range(RET_H):
                b = wide_pair()
                s = ret_scores[h % 2]

                def fn(e, h=h, b=b):
                    e.matmul(psum[:, b, 0:256], rt[:, 4 + h, 0:P], rt[:, h, :], start=True, stop=True)
                    return e.matmul(psum[:, b, 256:384], rt[:, 4 + h, P:SEQ], rt[:, h, P:SEQ], start=True, stop=True)
                m = op("pe", fn, tr + held(("bank", b)))
                d = op("dve", lambda e, s=s, b=b, h=h: e.tensor_tensor(s, psum[:, b, 0:384], decay[:, h, :], ALU.mult),
                       [m, k_decay] + last_rot + held(("ret_s", h % 2)))
                free[("bank", b)] = [d]

                def pv(e, h=h, s=s, b=b):
                    v = [proj2[:, kb, D + h * P:D + h * P + P] for kb in range(RB)]
                    e.matmul(psum[:, b + 1, 0:128], s[:, 0:128], v[0], start=True, stop=True)
                    e.matmul(psum[:, b + 1, 128:256], s[:, 128:256], v[0], start=True, stop=False)
                    return e.matmul(psum[:, b + 1, 128:256], s[:, 256:384], v[1], start=False, stop=True)
                o = op("pe", pv, [d] + vr + held(("bank", b + 1)))
                free[("ret_s", h % 2)] = [o]
                for rb in range(RB):
                    dst = rows2[:, rb, h * P:h * P + P]
                    src = psum[:, b + 1, rb * P:rb * P + P]
                    m1 = op("dve", lambda e, rb=rb, h=h, src=src: e.bn_stats(stats[:, rb, h, :], src), [o] + held("stats2"))
                    m2 = op("dve", lambda e, rb=rb, h=h: e.bn_aggr(agg[:, rb, h, :], stats[:, rb, h, :]), [m1])
                    m3 = op("dve", lambda e, rb=rb, h=h, dst=dst, src=src: e.tensor_scalar(
                        dst, src, agg[:, rb, h, 0:1], None, ALU.subtract), [m2] + [m for t in ready for m in t])
                    y_marks[rb].append(m3)
                free[("bank", b + 1)] = [m3]
            ys = []
            for rb in range(RB):
                m = op("dve", lambda e, rb=rb: e.tensor_scalar(rstd[:, rb, :], agg[:, rb, :, 1], EPS_2, None, ALU.add),
                       [y_marks[rb][-1]])
                m = power(rb, RET_H, [m])
                for h in range(RET_H):
                    dst = rows2[:, rb, h * P:h * P + P]
                    g = proj2[:, rb, 1536 + h * P:1536 + h * P + P]
                    m5 = op("dve", lambda e, rb=rb, h=h, dst=dst, g=g: e.scalar_tensor_tensor(
                        out=dst, in0=dst, scalar=rstd[:, rb, h:h + 1], in1=g, op0=ALU.mult, op1=ALU.mult),
                        [m, blocks[3][rb]])
                ys.append(m5)
            tr2 = []
            for rb in range(RB):
                for g in range(2):
                    c0 = 2048 + 512 * g
                    tr2 += transpose_to(lambda n, c0=c0: proj2[:, rb, c0 + n * P:c0 + n * P + P],
                                        [blocks[4 + g][rb]], range(4), rt[:, 4 * g:4 * g + 4, rb * P:rb * P + P],
                                        "act" if g else "dve", 1.0 if g else SB_D ** -0.5, [o])
            sb_bufs = [arena[:, 8192 + 1024 * n:8192 + 1024 * n + 1024] for n in range(2)]
            sv = [blocks[6][rb] for rb in range(RB)]
            for h in range(SB_H):
                b = wide_pair()
                z = psum[:, b, 0:384]
                buf = sb_bufs[h % 2]
                mag, sp = buf[:, 0:384], buf[:, 384:768]
                k0, k1, q0, q1 = (head_cols(rt[:, 4:8, :], h, 0, P), head_cols(rt[:, 4:8, :], h, P, P),
                                  head_cols(rt[:, 0:4, :], h, 0, SEQ), head_cols(rt[:, 0:4, :], h, P, P))

                def fn(e, z=z, k0=k0, k1=k1, q0=q0, q1=q1):
                    e.matmul(z[:, 0:256], k0, q0, start=True, stop=True)
                    return e.matmul(z[:, 256:384], k1, q1, start=True, stop=True)
                m = op("pe", fn, tr2 + [k_sb] + held(("bank", b)))
                s1 = op("act", lambda e, z=z, mag=mag: e.activation(mag, z, ACT.Abs), [m] + held(("sbuf", h % 2), "heads"))
                s2 = op("act", lambda e, mag=mag: e.activation(mag, mag, ACT.Exp, scale=-1.0), [s1])
                s3 = op("act", lambda e, mag=mag: e.activation(mag, mag, ACT.Ln, bias=1.0), [s2])
                m = op("dve", lambda e, z=z, mag=mag, sp=sp: e.scalar_tensor_tensor(
                    out=sp, in0=z, scalar=0.0, in1=mag, op0=ALU.max, op1=ALU.add), [s3])
                op("dve", lambda e, sp=sp: e.tensor_tensor(sp[:, 0:128], sp[:, 0:128], strict[:, :], ALU.mult), [m, k_strict])
                m = op("dve", lambda e, sp=sp: e.tensor_tensor(sp[:, 256:384], sp[:, 256:384], strict[:, :], ALU.mult), [m])
                zc = psum[:, b + 1, 0:384]

                def fn2(e, zc=zc, sp=sp, k0=k0, k1=k1, q0=q0, q1=q1):
                    e.matmul(zc[:, 0:256], k0, q0, start=True, stop=False)
                    e.matmul(zc[:, 0:256], tri[:, 0:P], sp[:, 0:256], start=False, stop=False)
                    e.matmul(zc[:, 128:256], tri[:, P:SEQ], sp[:, 256:384], start=False, stop=False)
                    e.matmul(zc[:, 0:128], identb, strict_b, start=False, stop=True)
                    e.matmul(zc[:, 256:384], k1, q1, start=True, stop=False)
                    e.matmul(zc[:, 256:384], tri[:, 0:P], sp[:, 256:384], start=False, stop=False)
                    return e.matmul(zc[:, 256:384], identb, strict_b, start=False, stop=True)
                m2 = op("pe", fn2, [m, k_tri] + held(("bank", b + 1)))
                free[("bank", b)] = [m]
                a1 = op("act", lambda e, zc=zc, mag=mag: e.activation(mag, zc, ACT.Exp), [m2])
                free[("bank", b + 1)] = [a1]
                ob = GEMM[h % 2]

                def pv2(e, h=h, mag=mag, ob=ob):
                    v = [proj2[:, kb, 3072 + h * HD:3072 + h * HD + HD] for kb in range(RB)]
                    e.matmul(psum[:, ob, 0:64], mag[:, 0:128], v[0], start=True, stop=True)
                    e.matmul(psum[:, ob, 64:128], mag[:, 128:256], v[0], start=True, stop=False)
                    return e.matmul(psum[:, ob, 64:128], mag[:, 256:384], v[1], start=False, stop=True)
                o2 = op("pe", pv2, [a1] + sv + held(("bank", ob)))
                free[("sbuf", h % 2)] = [o2]
                for rb in range(RB):
                    m6 = op("dve", lambda e, rb=rb, h=h, ob=ob: e.tensor_tensor(
                        rows2[:, rb, 512 + h * HD:512 + h * HD + HD], psum[:, ob, rb * 64:rb * 64 + 64],
                        proj2[:, rb, 3584 + h * HD:3584 + h * HD + HD], ALU.mult), [o2, blocks[7][rb]])
                free[("bank", ob)] = [m6]
            free["rt"] = [o2]
            yt = [to_stationary(rows2[:, rb, :], [ys[rb], m6], xt_hi, xt_lo, rb, hold=[xt_used]) for rb in range(RB)]
            free["proj"] = free["heads"] = [m for t in yt for m in t] + [m6]
            marks, banks = out_product(yt)
            for h in range(2):
                for rb in range(RB):
                    t = tmp2[:, (2 * h + rb) * 512:(2 * h + rb) * 512 + 512]
                    v = x[:, rb, h * BLK:h * BLK + BLK]
                    m = op("dve", lambda e, t=t, rb=rb, h=h: e.tensor_tensor(
                        t, psum[:, banks[rb][h], :], gate_row[:, h * BLK:h * BLK + BLK], ALU.mult),
                        [marks[rb][h], mods[-1]])
                    free[("bank", banks[rb][h])] = [m]
                    m = op("dve", lambda e, t=t, v=v: e.tensor_tensor(v, v, t, ALU.add), [m])
            xready = [m]
            free["work"] = [m] + yt[1]
            k_par_free = [m]

        k_f = load("final_g", shift, rows(T["final_g_2"]), k_par_free)
        rs = [rms(rb, xready, rows2[:, rb, :]) for rb in range(RB)]
        for rb in range(RB):
            m = op("dve", lambda e, rb=rb: e.scalar_tensor_tensor(
                out=x[:, rb, :], in0=x[:, rb, :], scalar=rstd[:, rb, 0:1], in1=shift, op0=ALU.mult, op1=ALU.mult),
                [rs[rb], k_f])
            stored = op("act", lambda e, rb=rb: e.dma_start(out[rb * P:rb * P + P, :], x[:, rb, :]), [m],
                        inc=c_out, by=16)
        assert state["tile"] == len(tiles), (state, len(tiles))

        block = ctx.enter_context(nc.Block())

        @block.sync
        def _(sp):
            n = len(tiles)
            W = T["weights"]
            for t in range(RING):
                sp.dma_start(raw[:, t, :], W[t]).then_inc(c_raw[t].sem, 16)
            trips = (n - RING) // RING
            with sp.Fori(0, trips) as i:
                for s in range(RING):
                    sp.wait_ge(c_lo.sem, i * RING + s + 1)
                    src = W[bass.ds(i * RING + RING + s, 1), :, :].rearrange("a p c -> (a p) c")
                    sp.dma_start(raw[:, s, :], src).then_inc(c_raw[s].sem, 16)
            for t in range(RING + trips * RING, n):
                sp.wait_ge(c_lo.sem, t - RING + 1)
                sp.dma_start(raw[:, t % RING, :], W[t]).then_inc(c_raw[t % RING].sem, 16)

        @block.tensor
        def _(e):
            plan.emit("pe", e)

        @block.scalar
        def _(e):
            plan.emit("act", e)
            e.wait_ge(c_out.sem, 16 * RB)

        @block.vector
        def _(e):
            plan.emit("dve", e)

        @block.gpsimd
        def _(e):
            plan.emit("pool", e)



def pack_weights(inputs):
    tiles = weight_plan()
    w = np.zeros((len(tiles), P, TW), np.float32)

    def chunks(a):
        k, n = a.shape
        return a.reshape(k // P, P, n).transpose(1, 0, 2).reshape(P, -1)

    for n, (name, layer, what, where, cols) in enumerate(tiles):
        m = inputs[name][layer]
        if what == "half":
            c0, k0 = where
            r = slice(k0 * P, k0 * P + 4 * P)
            if isinstance(c0, tuple):
                width = m.shape[1]
                a, b = c0[1] * BLK, c0[1] * BLK + BLK
                own = m[r, a:min(b, 3 * MIX)]
                if b > 3 * MIX:
                    own = np.concatenate([own, m[r, width - MEMW:width]], axis=1)
            else:
                own = m[r, c0:c0 + BLK]
        elif what == "narrow":
            own = m[:, where:where + IDX_H + HD]
        elif what == "up":
            s, k0 = where
            r = slice(k0 * P, k0 * P + 4 * P)
            own = np.concatenate([m[r, s * FF_STEP:(s + 1) * FF_STEP],
                                  m[r, D_FF + s * FF_STEP:D_FF + (s + 1) * FF_STEP]], axis=1)
        else:
            own = m[where * FF_STEP:(where + 1) * FF_STEP, :]
        w[n, :, 0:cols] = chunks(own)
    return w


def shape_constants():
    i = np.arange(P)
    q, s = i[:, None], i[None, :]
    big = lambda keep: np.where(keep, 0.0, BIG).astype(np.float32)
    pieces = [np.eye(P, dtype=np.float32), big(s >= q), big(s <= q)]
    for dil in (4, 16):
        same = (q - s) % dil == 0
        pieces += [big(same), big(same & (s <= q))]
    n, m = np.arange(SEQ)[None, :], np.arange(SEQ)[:, None]
    head = np.arange(RET_H, dtype=np.float64)
    log_gamma = np.log1p(-(2.0 ** (-5.0 - head)))
    seen = m // CHUNK <= n // CHUNK
    decay = np.where(seen, np.exp(np.abs(n - m)[None] * log_gamma[:, None, None]), 0.0) * RET_D ** -0.5
    decay = np.concatenate([decay[:, 0:P, :], decay[:, P:, P:]], axis=2).transpose(1, 0, 2)
    half = RET_D // 2
    inv2 = ROPE_BASE ** (-np.arange(half, dtype=np.float32) / np.float32(half))
    ang = np.arange(SEQ, dtype=np.float32)[:, None] * inv2.astype(np.float32)[None, :]
    f = lambda a: np.ascontiguousarray(a, dtype=np.float32)
    return {
        "ident": np.eye(P, dtype=np.float32),
        "masks": f(np.concatenate(pieces, axis=1)),
        "causal": f(np.concatenate([np.zeros((P, P)), big(s <= q)], axis=1)),
        "inv_freq": f(np.float32(ROPE_THETA) ** (-np.arange(ROPE_HALF, dtype=np.float32) / np.float32(ROPE_HALF))),
        "decay": f(decay),
        "ret_cos_sin": f(np.concatenate([np.cos(ang), np.sin(ang)], axis=1)),
        "tri": f(np.concatenate([-(q >= s).astype(np.float32), -np.ones((P, P))], axis=1)),
        "strict": f(q < s),
        "strict_bias": big(q < s),
    }


_SMALL = ["x", "mem", "positions", "mem_ln_g", "mem_ln_b", "idx_kn_g", "idx_kn_b", "ln1_g", "ln1_b", "ln2_g",
          "ln2_b", "c_2", "norm_g_2", "b_ada_2", "final_g_2"]
_FLAT = {"x": (SEQ, D), "mem": (SEQ, D)}


def kernel(**inputs):
    import concourse.bacc as _bacc
    from concourse.bass_utils import run_bass_kernel_spmd as _run

    nc = _bacc.Bacc("TRN2", target_bir_lowering=False, num_devices=1)
    given = {k: np.asarray(v) for k, v in inputs.items()}
    arrays = {k: np.ascontiguousarray(given[k].reshape(_FLAT.get(k, given[k].shape))) for k in _SMALL}
    for name in ("positions", "c_2"):
        arrays[name] = np.ascontiguousarray(given[name].reshape(-1, P).T)
    arrays.update(shape_constants())
    arrays["weights"] = pack_weights(given)
    T, feed = {}, {}
    for name, a in arrays.items():
        feed[f"in_{name}"] = a
        T[name] = nc.dram_tensor(f"in_{name}", a.shape, mybir.dt.from_np(a.dtype), kind="ExternalInput").ap()
    out = nc.dram_tensor("out_rows", (SEQ, D), F32, kind="ExternalOutput").ap()
    stack_kernel(nc, T, out)
    r = _run(nc, [feed], core_ids=[0])
    return r.results[0]["out_rows"].reshape(1, SEQ, D)
```

```python
from contextlib import ExitStack

import numpy as np

import concourse.bass as bass
from concourse import mybir

F32 = mybir.dt.float32
F32R = mybir.dt.float32r
BF16 = mybir.dt.bfloat16
I32 = mybir.dt.int32
ALU = mybir.AluOpType
ACT = mybir.ActivationFunctionType
AX = mybir.AxisListType

P = 128
D = 1024
SEQ = 256
RB = SEQ // P
KC = D // P
KINDS = "ABCA"
N_A, N_BC = 2, 1
HD = 64
NH = 12
MIX = NH * HD
MEM_H = 4
MEMW = MEM_H * HD
IDX_H = 8
IDX_W = IDX_H * HD
ROPE_HALF = HD // 8
ROPE_THETA = 500000.0
TOPK = min(256, SEQ // 4)
DIL = 3
DIL_H = 4
DIL_V = MIX // DIL_H
D_FF = 2816
FF_STEP = 256
FF_STEPS = D_FF // FF_STEP
ALPHA = float((2 * len(KINDS)) ** 0.25)
LN_EPS = 1e-5
DEPTH_2 = 2
CHUNK = 64
RET_H, RET_D = 4, 128
SB_H, SB_D = 8, 64
D_HALF = 512
EPS_2 = 1e-6
ROPE_BASE = 10000.0

TW = 2048
BLK = 512
RING = 3
BIG = -1.0e30
TAKEN = -3.0e38


N_TILES = (2 * KINDS.count("A") * 1 + KINDS.count("A")
           + len(KINDS) * 2 * (5 + 1 + 2) + len(KINDS) * 3 * FF_STEPS
           + DEPTH_2 * 2 * (6 + 8 + 2))



class Counter:

    def __init__(self, sem):
        self.sem, self.n = sem, 0


class Loop:
    def __init__(self, trips, counters):
        self.trips, self.start, self.per = trips, {c: c.n for c in counters}, {}


class Plan:
    ENGINES = ("pe", "act", "dve", "pool")

    def __init__(self, nc, ctx):
        self.nc, self.ctx = nc, ctx
        self.queue = {e: [] for e in self.ENGINES}
        self.counters = []
        self.loop = None
        self.done = {e: self.counter(f"{e}_done") for e in self.ENGINES}

    def counter(self, name):
        c = Counter(self.ctx.enter_context(self.nc.semaphore(name)))
        self.counters.append(c)
        return c

    def op(self, engine, fn, wait=(), inc=None, by=1):
        inc = inc or self.done[engine]
        inc.n += by
        self.queue[engine].append((fn, tuple(wait), inc, by))
        return (inc, inc.n)

    def begin(self, trips):
        self.loop = Loop(trips, self.counters)
        for q in self.queue.values():
            q.append(self.loop)

    def end(self):
        loop, self.loop = self.loop, None
        for c, n in loop.start.items():
            loop.per[c] = c.n - n
            c.n += (loop.trips - 1) * loop.per[c]
        for q in self.queue.values():
            q.append(None)
        return loop

    @staticmethod
    def last_trip(loop, mark):
        c, v = mark
        return (c, v + (loop.trips - 1) * loop.per[c])

    def emit(self, name, engine):
        items = iter(self.queue[name])
        waited = {}

        def one(item, loop, i):
            fn, waits, inc, by = item
            for c, v in waits:
                per = loop.per[c] if loop else 0
                if per:
                    engine.wait_ge(c.sem, i * per + v)
                elif waited.get(c, 0) < v:
                    engine.wait_ge(c.sem, v)
                    waited[c] = v
            fn(engine).then_inc(inc.sem, by)

        for item in items:
            if isinstance(item, Loop):
                loop, body = item, []
                for inner in items:
                    if inner is None:
                        break
                    body.append(inner)
                if body:
                    with engine.Fori(0, loop.trips) as i:
                        for inner in body:
                            one(inner, loop, i)
            else:
                one(item, None, None)



def stack_kernel(nc, T, out):
    order = []
    with ExitStack() as ctx:
        plan = Plan(nc, ctx)
        op = plan.op

        def sb(name, shape, dt=F32):
            return ctx.enter_context(nc.sbuf_tensor(name, shape, dt))

        raw = sb("w_raw", [P, RING, TW])
        w_hi = sb("w_high", [P, RING, TW], F32R)
        w_lo = sb("w_low", [P, RING, TW], F32R)
        xt_hi = sb("xt_high", [P, KC, SEQ], F32R)
        xt_lo = sb("xt_low", [P, KC, SEQ], F32R)
        ht_hi = sb("ht_high", [P, 2, SEQ], F32R)
        ht_lo = sb("ht_low", [P, 2, SEQ], F32R)
        x = sb("x_rows", [P, RB, D])
        arena = sb("arena", [P, 10240])
        work = sb("work", [P, 4096])
        kv = sb("mem_kv", [P, 1536])
        par = sb("norm_params", [P, 2, 2 * D])
        proj = arena[:, 0:5120].rearrange("p (r c) -> p r c", r=RB)
        mixed = proj[:, :, 0:D]
        qt = arena[:, 5120:6656].rearrange("p (c s) -> p c s", s=SEQ)
        kt = arena[:, 6656:8192].rearrange("p (c s) -> p c s", s=SEQ)
        qmt = arena[:, 8192:8704].rearrange("p (c s) -> p c s", s=SEQ)
        qit = arena[:, 8704:9728].rearrange("p (c s) -> p c s", s=SEQ)
        kit = arena[:, 9728:9984]
        ff_silu = arena[:, 0:512].rearrange("p (r c) -> p r c", r=RB)
        ff_h = arena[:, 512:1024].rearrange("p (r c) -> p r c", r=RB)
        prob = [work[:, 1024 * n:1024 * n + 1024] for n in range(2)]
        probt = [work[:, 2048 + 1024 * n:3072 + 1024 * n] for n in range(2)]
        idx = work[:, 2048:2048 + RB * 704].rearrange("p (r c) -> p r c", r=RB)
        mkv = kv[:, 0:1024].rearrange("p (r c) -> p r c", r=RB)
        mkt = kv[:, 1024:1536].rearrange("p (c s) -> p c s", s=SEQ)
        score = sb("idx_score", [P, RB, SEQ])
        select = sb("select_bias", [P, RB, SEQ], BF16)
        proj2 = arena[:, 0:8192].rearrange("p (r c) -> p r c", r=RB)
        rows2 = work[:, 0:2048].rearrange("p (r c) -> p r c", r=RB)
        tmp2 = work[:, 2048:4096]
        ident = sb("ident", [P, P])
        masks = sb("masks", [P, 7 * P], BF16)
        identb, m_win, m_causal = masks[:, 0:128], masks[:, 128:256], masks[:, 256:384]
        m_pair = [masks[:, 128:384], masks[:, 384:640], masks[:, 640:896]]
        causal = sb("causal", [P, SEQ])
        half_neg = sb("half_neg", [P, 8])
        rope_c = sb("rope_cos", [P, RB, ROPE_HALF])
        rope_s = sb("rope_sin", [P, RB, ROPE_HALF])
        rope_t = sb("rope_tmp", [P, 4, 24 * ROPE_HALF])
        kn_par = sb("idx_norm_params", [P, 4, HD])
        ada = sb("ada_rows", [12, BLK])
        cond_hi = sb("c_high", [P, KC], F32R)
        cond_lo = sb("c_low", [P, KC], F32R)
        stats = sb("norm_stats", [P, RB, 4, 6])
        agg = sb("norm_mean_var", [P, RB, 4, 2])
        rstd = sb("norm_rstd", [P, RB, 4])
        negmax = sb("neg_max", [P, 2, 8])
        expsum = sb("exp_sum", [P, 2, 8])
        recip = sb("recip", [P, 2, 8])
        top8 = sb("top8", [P, RB, 8])
        col = sb("c_col", [P, KC])
        pos_i = sb("pos_int", [P, RB], I32)
        pos = sb("pos", [P, RB])
        inv = sb("inv_freq", [P, ROPE_HALF])
        ang = sb("angle", [P, RB, ROPE_HALF])
        turn = sb("turns", [P, RB, ROPE_HALF])
        strict = sb("strict", [P, P])
        memory_scope = ctx.enter_context(ExitStack())
        mt_hi = memory_scope.enter_context(nc.sbuf_tensor("memt_high", [P, KC, SEQ], F32R))
        mt_lo = memory_scope.enter_context(nc.sbuf_tensor("memt_low", [P, KC, SEQ], F32R))

        psum = ctx.enter_context(nc.psum_tensor("psum", [P, 8, BLK], F32))
        GEMM, WIDE, TRB = (0, 1), (2, 4), (6, 7)

        c_raw = [plan.counter(f"w_raw_{n}") for n in range(RING)]
        c_hi = plan.counter("w_high_done")
        c_lo = plan.counter("w_low_done")
        c_tile = plan.counter("tile_used")
        c_gate = plan.counter("ff_gate_ready")
        c_mul = plan.counter("ff_h_ready")
        c_tr = plan.counter("ff_transposed")
        c_ht_hi = plan.counter("ff_ht_high")
        c_ht_lo = plan.counter("ff_ht_low")
        c_out = plan.counter("out_stored")

        def load(name, dst, src, wait=()):
            return op("pool", lambda e: e.dma_start(dst, src), wait, inc=plan.counter(f"ld_{name}"), by=16)

        def rows(vec):
            return vec.partition_broadcast(P)

        free = {("bank", n): [] for n in range(8)}

        def held(*keys):
            return [m for k in keys for m in free.get(k, [])]

        state = {"split": 0, "tile": 0, "trb": 0, "wide": 0, "slot": 0, "par": 0}
        background = []

        def step_background():
            if background and next(background[0], background) is background:
                background.pop(0)

        def drain_background():
            while background:
                step_background()

        def pipelined(units):
            waiting, middle, oldest = list(units), None, None
            while waiting or middle or oldest:
                if oldest:
                    next(oldest, None)
                new = waiting.pop(0) if waiting else None
                if new:
                    next(new)
                if middle:
                    next(middle)
                oldest, middle = middle, new
                yield

        def split_next():
            t = state["split"]
            if t >= N_TILES:
                return
            state["split"] += 1
            s = t % RING
            c_raw[s].n += 16
            arrived = (c_raw[s], c_raw[s].n)
            used = [(c_tile, t - RING + 1)] if t >= RING else []
            hi = op("act", lambda e: e.activation(w_hi[:, s, :], raw[:, s, :], ACT.Copy),
                    [arrived] + used, inc=c_hi)
            op("dve", lambda e: e.tensor_tensor(w_lo[:, s, :], raw[:, s, :],
                                                w_hi[:, s, :].bitcast(F32), ALU.subtract),
               [hi], inc=c_lo)

        def products(e, dst, a_hi, a_lo, b_hi, b_lo, first, last):
            e.matmul(dst, a_hi, b_hi, start=first, stop=False)
            e.matmul(dst, a_hi, b_lo, start=False, stop=False)
            return e.matmul(dst, a_lo, b_hi, start=False, stop=last)

        def use_tile(tile, parts):
            order.append(tile)
            t = state["tile"]
            state["tile"] += 1
            split_next()
            s = t % RING
            marks = []
            for n, (fn, waits, inc) in enumerate(parts):
                ready = [(c_lo, t + 1)] if n == 0 else []
                fin = n == len(parts) - 1
                marks.append(op("pe", lambda e, fn=fn: fn(e, w_hi[:, s, :], w_lo[:, s, :]),
                                ready + list(waits), inc=c_tile if fin else inc))
            step_background()
            return marks

        def gemm_block(weight, a_hi, a_lo, ready, banks, blocks=range(RB), shared=False):
            blocks = list(blocks)
            for half in range(2):
                def part(rb, half=half):
                    def fn(e, hi, lo):
                        for k in range(4):
                            kk = 4 * half + k
                            left = [(v[:, kk:kk + 1].broadcast_to([P, P]) if shared
                                     else v[:, kk, rb * P:rb * P + P]) for v in (a_hi, a_lo)]
                            m = products(e, psum[:, banks[rb], :], left[0], left[1], hi[:, k * BLK:k * BLK + BLK],
                                         lo[:, k * BLK:k * BLK + BLK], kk == 0, kk == KC - 1)
                        return m
                    waits = (held(("bank", banks[rb])) + list(ready[rb])) if half == 0 else []
                    return (fn, waits, None)
                marks = use_tile(weight + ("half", 4 * half), [part(rb) for rb in blocks])
            return dict(zip(blocks, marks))

        def transpose_in(src, src_ready, chunks, dst_fn, width=P):
            b = TRB[state["trb"] % 2]
            state["trb"] += 1

            pieces = [src(c) for c in chunks]

            def fn(e):
                for n, piece in enumerate(pieces):
                    m = e.transpose(psum[0:width, b, n * P:n * P + P], piece, ident[:, :])
                return m
            done = op("pe", fn, held(("bank", b)) + list(src_ready))
            marks = dst_fn(psum[0:width, b, 0:len(chunks) * P], done)
            free[("bank", b)] = marks
            return marks

        def to_stationary(src, ready, dst_hi, dst_lo, rb, hold=()):
            marks = []
            for g in range(2):
                def copy(bank, done):
                    v = bank.rearrange("p (c s) -> p c s", s=P)
                    h = dst_hi[:, 4 * g:4 * g + 4, rb * P:rb * P + P]
                    low = dst_lo[:, 4 * g:4 * g + 4, rb * P:rb * P + P]
                    a = op("act", lambda e: e.activation(h, v, ACT.Copy), [done] + list(hold))
                    return [op("dve", lambda e: e.tensor_tensor(low, v, h.bitcast(F32), ALU.subtract),
                               [a, done])]
                marks += transpose_in(lambda c: src[:, c * P:c * P + P], ready[g], range(4 * g, 4 * g + 4), copy)
            return marks

        def transpose_to(src, ready, chunks, dst, engine, scale=1.0, hold=()):
            def copy(bank, done):
                v = bank.rearrange("p (c s) -> p c s", s=P) if len(chunks) > 1 else bank
                if engine == "act":
                    return [op("act", lambda e: e.activation(dst, v, ACT.Copy, scale=scale), [done] + list(hold))]
                return [op("dve", lambda e: e.tensor_scalar(dst, v, scale, None, ALU.mult), [done] + list(hold))]
            return transpose_in(src, ready, chunks, copy)

        def power(rb, n, ready):
            return op("pool", lambda e: e.tensor_tensor(rstd[:, rb, 0:n], rstd[:, rb, 0:n],
                                                        half_neg[:, 0:n], ALU.pow), list(ready) + [k_hneg])

        def norm_stats(rb, pieces, ready, eps=LN_EPS):
            for n, piece in enumerate(pieces):
                m = op("dve", lambda e, n=n, piece=piece: e.bn_stats(stats[:, rb, n, :], piece), list(ready))
            src = stats[:, rb, 0:len(pieces), :].rearrange("p a b -> p (a b)")
            m2 = op("dve", lambda e: e.bn_aggr(agg[:, rb, 0, :], src), [m])
            m3 = op("dve", lambda e: e.tensor_scalar(rstd[:, rb, 0:1], agg[:, rb, 0:1, 1], eps, None, ALU.add), [m2])
            return m2, power(rb, 1, [m3])

        def norm_gain(rb, pieces, gains, ready):
            return [op("dve", lambda e, v=v, g=g: e.scalar_tensor_tensor(
                out=v, in0=v, scalar=agg[:, rb, 0, 0:1], in1=g, op0=ALU.subtract, op1=ALU.mult), ready)
                for v, g in zip(pieces, gains)]

        def norm_bias(rb, pieces, biases, marks, ready):
            return [op("dve", lambda e, v=v, b=b: e.scalar_tensor_tensor(
                out=v, in0=v, scalar=rstd[:, rb, 0:1], in1=b, op0=ALU.mult, op1=ALU.add), [m, ready])
                for v, b, m in zip(pieces, biases, marks)]

        def halves(v):
            return [v[:, h * BLK:h * BLK + BLK] for h in range(2)]

        def load_norm(name, g, b):
            s = state["par"] % 2
            state["par"] += 1
            hold = held(("par", s))
            mg = load(name + "_g", par[:, s, 0:D], rows(g), hold)
            mb = load(name + "_b", par[:, s, D:2 * D], rows(b), hold)
            return s, [mg, mb]

        k_x, c_first = [], plan.counter("ld_first")
        k_ident = op("act", lambda e: e.dma_start(ident[:, :], T["ident"]), inc=c_first, by=16)
        for rb in range(RB):
            k_x.append(op("act", lambda e, rb=rb: e.dma_start(x[:, rb, :], T["x"][rb * P:rb * P + P, :]),
                          inc=plan.counter(f"ld_x{rb}"), by=16))
        k_pos = load("pos", pos_i[:, :], T["positions"])
        k_inv = load("inv", inv[:, :], rows(T["inv_freq"]))
        k_kn = [[load(f"idx_g{a}", kn_par[:, 2 * a, :], rows(T["idx_kn_g"][a])),
                 load(f"idx_b{a}", kn_par[:, 2 * a + 1, :], rows(T["idx_kn_b"][a]))] for a in range(KINDS.count("A"))]
        k_causal = load("causal", causal[:, :], T["causal"])
        masks_f = arena[:, 5120:5120 + 7 * P]
        k_masks = load("masks", masks_f, T["masks"])
        k_c = load("c", col[:, :], T["c_2"])
        k_ada = load("b_ada", ada[:, :], T["b_ada_2"].rearrange("l (c n) -> (l c) n", n=BLK))
        mem_rows = proj[:, :, 3 * BLK:5 * BLK]
        k_mem = [load(f"mem{rb}", mem_rows[:, rb, :], T["mem"][rb * P:rb * P + P, :]) for rb in range(RB)]
        mem_par, k_mem_par = load_norm("mem", T["mem_ln_g"], T["mem_ln_b"])
        op("dve", lambda e: e.memset(half_neg[:, :], -0.5))
        k_hneg = (plan.done["dve"], plan.done["dve"].n)

        for _ in range(2):
            split_next()
        xt = [to_stationary(x[:, rb, :], [[k_ident, k_x[rb]]] * 2, xt_hi, xt_lo, rb) for rb in range(RB)]

        two_pi = 2.0 * np.pi
        parts, rest = [], two_pi
        for bits in (8, 8, 8):
            exp = int(np.floor(np.log2(rest)))
            unit = 2.0 ** (exp - bits + 1)
            head = float(np.floor(rest / unit) * unit)
            parts.append(head)
            rest -= head
        parts.append(float(rest))
        MAGIC = 12582912.0
        PI = 3.1415925
        m = op("dve", lambda e: e.tensor_copy(pos[:, :], pos_i[:, :]), [k_pos])
        for rb in range(RB):
            ma = op("dve", lambda e, rb=rb: e.tensor_scalar(ang[:, rb, :], inv[:, :], pos[:, rb:rb + 1], None,
                                                            ALU.mult), [m, k_inv])
        m = op("dve", lambda e: e.tensor_scalar(turn[:, :, :], ang[:, :, :], float(1.0 / two_pi), MAGIC,
                                                ALU.mult, ALU.add), [ma])
        m = op("dve", lambda e: e.tensor_scalar(turn[:, :, :], turn[:, :, :], MAGIC, None, ALU.subtract), [m])
        for part in parts:
            m = op("dve", lambda e, part=part: e.scalar_tensor_tensor(
                out=ang[:, :, :], in0=turn[:, :, :], scalar=-part, in1=ang[:, :, :], op0=ALU.mult,
                op1=ALU.add), [m])
        m = op("dve", lambda e: e.tensor_scalar(rope_c[:, :, :], ang[:, :, :], float(np.pi / 2), None, ALU.add), [m])
        m = op("dve", lambda e: e.tensor_scalar(turn[:, :, :], rope_c[:, :, :], PI, -two_pi, ALU.is_gt, ALU.mult), [m])
        m = op("dve", lambda e: e.tensor_tensor(rope_c[:, :, :], rope_c[:, :, :], turn[:, :, :], ALU.add), [m])
        m = op("dve", lambda e: e.tensor_scalar(rope_c[:, :, :], rope_c[:, :, :], PI, -PI, ALU.min, ALU.max), [m])
        m = op("dve", lambda e: e.tensor_scalar(ang[:, :, :], ang[:, :, :], PI, -PI, ALU.min, ALU.max), [m])
        k_cos = op("act", lambda e: e.activation(rope_c[:, :, :], rope_c[:, :, :], ACT.Sin), [m])
        k_rope = [k_cos, op("act", lambda e: e.activation(rope_s[:, :, :], ang[:, :, :], ACT.Sin), [m])]

        k_maskb = op("dve", lambda e: e.tensor_copy(masks[:, :], masks_f), [k_masks])
        free["heads"] = [k_maskb]
        m = op("act", lambda e: e.activation(col[:, :], col[:, :], ACT.Silu), [k_c])
        m = op("act", lambda e: e.activation(cond_hi[:, :], col[:, :], ACT.Copy), [m])
        k_col = op("dve", lambda e: e.tensor_tensor(cond_lo[:, :], col[:, :], cond_hi[:, :].bitcast(F32), ALU.subtract), [m])

        mt = []

        def memory_work():
            for rb in range(RB):
                v = halves(mem_rows[:, rb, :])
                am, rm = norm_stats(rb, v, [k_mem[rb]])
                r = norm_gain(rb, v, halves(par[:, mem_par, 0:D]), [am] + k_mem_par)
                yield
                r = norm_bias(rb, v, halves(par[:, mem_par, D:2 * D]), r, rm)
                free[("par", mem_par)] = [r[1]]
                mt.append(to_stationary(mem_rows[:, rb, :], [[r[0]], [r[1]]], mt_hi, mt_lo, rb))
                free["values"] = mt[-1]
                yield

        def evacuate(banks, marks, dst, wait=(), func=ACT.Copy):
            done = []
            for rb in range(RB):
                v = psum[:, banks[rb], :]
                w = [marks[rb]] + list(wait)
                if rb == 0 or func != ACT.Copy:
                    d = op("act", lambda e, rb=rb, v=v: e.activation(dst(rb), v, func), w)
                else:
                    d = op("dve", lambda e, rb=rb, v=v: e.tensor_copy(dst(rb), v), w)
                free[("bank", banks[rb])] = [d]
                done.append(d)
            return done

        def rotary(rb, v, heads, half, cos, sin, tmp, ready):
            n = heads * half
            t = [tmp[k].rearrange("p (h d) -> p h d", d=half) for k in range(4)]
            c = cos.unsqueeze(1).broadcast_to([P, heads, half])
            s = sin.unsqueeze(1).broadcast_to([P, heads, half])
            x1, x2 = v[:, :, 0:half], v[:, :, half:2 * half]
            w = list(ready) + held("rope_tmp")
            for k, (a, b) in enumerate(((x1, c), (x2, s), (x2, c), (x1, s))):
                m = op("dve", lambda e, k=k, a=a, b=b: e.tensor_tensor(t[k], a, b, ALU.mult), w)
            op("dve", lambda e: e.tensor_tensor(x1, t[0], t[1], ALU.subtract), [m])
            m = op("dve", lambda e: e.tensor_tensor(x2, t[2], t[3], ALU.add), [m])
            free["rope_tmp"] = [m]
            return m

        def rope_heads(rb, cols, heads, ready):
            v = cols.rearrange("p (h d) -> p h d", d=HD)
            tmp = [rope_t[:, k, 0:heads * ROPE_HALF] for k in range(4)]
            return rotary(rb, v, heads, ROPE_HALF, rope_c[:, rb, :], rope_s[:, rb, :], tmp, ready)

        def head_cols(t, h, s0, n):
            p0 = HD * (h % 2)
            return t[p0:p0 + HD, h // 2, s0:s0 + n]

        def wide_pair():
            b = WIDE[state["wide"] % 2]
            state["wide"] += 1
            return b

        def score_pieces(b, n_pieces, nk, joint):
            if joint:
                flat = psum[:, b:b + 2, :].rearrange("p b c -> p (b c)")
                return [(n * nk // BLK, flat[:, n * nk:n * nk + nk]) for n in range(n_pieces)]
            return [(n % 2, psum[:, b + n % 2, n // 2 * nk:n // 2 * nk + nk]) for n in range(n_pieces)]

        def accumulate(e, pieces, products_of, nk):
            banks = [pieces[n][0] for n, *_ in products_of]
            for i, (n, left, right, cols) in enumerate(products_of):
                dst = pieces[n][1] if cols is None else pieces[n][1][:, nk - cols:nk]
                m = e.matmul(dst, left, right, start=banks[i] not in banks[:i], stop=banks[i] not in banks[i + 1:])
            return m

        def attention_unit(segments, joint, values, dst, ready, finished):
            nk = segments[0][3]
            b = wide_pair()
            slot = state["slot"] % 2
            state["slot"] += 1
            pr, pt = prob[slot], probt[slot]
            nseg = len(segments)
            pieces_l = score_pieces(b, nseg, nk, joint)

            def scores(e):
                work_list = [(n, q, k, None) for n, (q, k, _, _) in enumerate(segments)]
                work_list += [(n, identb, bias, bias.shape[1]) for n, (_, _, bias, _) in enumerate(segments)
                              if bias is not None]
                return accumulate(e, pieces_l, work_list, nk)
            s = op("pe", scores, list(ready()) + held(("bank", b), ("bank", b + 1)))
            nmax = 1 if joint else nseg
            if joint:
                view = psum[:, b:b + 2, :].rearrange("p b c -> p (b c)")[:, 0:nseg * nk]
                nm_out = negmax[:, slot, 0:1]
            else:
                view = psum[:, b:b + 2, 0:nseg // 2 * nk].rearrange("p b (h k) -> p b h k", k=nk)
                nm_out = negmax[:, slot, 0:nseg].rearrange("p (h b) -> p b h", b=2)
            mx = op("dve", lambda e: e.tensor_reduce(nm_out, view, AX.X, ALU.max, negate=True),
                    [s] + held(("negmax", slot)))
            for n in range(nmax):
                src = view if joint else pieces_l[n][1]
                dst_p = pr[:, 0:nseg * nk] if joint else pr[:, n * nk:n * nk + nk]
                ex = op("act", lambda e, n=n, src=src, dst_p=dst_p: e.activation(
                    dst_p, src, ACT.Exp, bias=negmax[:, slot, n:n + 1], accum_out=expsum[:, slot, n:n + 1]),
                    [mx] + held(("prob", slot), ("expsum", slot)))
            free[("negmax", slot)] = [ex]
            yield
            rc = op("dve", lambda e: e.reciprocal(recip[:, slot, 0:nmax], expsum[:, slot, 0:nmax]),
                    [ex] + held(("recip", slot)))
            free[("expsum", slot)] = [rc]
            pready = ex
            if joint:
                for n in range(1, nseg):
                    pready = op("dve", lambda e, n=n: e.tensor_tensor(
                        pr[:, 0:nk], pr[:, 0:nk], pr[:, n * nk:n * nk + nk], ALU.add), [pready])
            pieces = [(n, kb) for n in range(nmax) for kb in range(nk // P)]
            turned = []
            for g in range(0, len(pieces), 4):
                some = pieces[g:g + 4]
                to = pt[:, g * P:(g + len(some)) * P]
                turned += transpose_to(lambda i: pr[:, i[0] * nk + i[1] * P:i[0] * nk + i[1] * P + P], [pready], some,
                                       to.rearrange("p (c s) -> p c s", s=P) if len(some) > 1 else to,
                                       "act" if (g // 4) % 2 else "dve", hold=held(("probt", slot), "idx"))
            free[("prob", slot)] = list(turned)
            yield
            vals = [[values(n, kb) for kb in range(nk // P)] for n in range(nmax)]
            w = vals[0][0][0].shape[1]

            def weighted(e):
                for n in range(nmax):
                    for kb in range(nk // P):
                        c = n * (nk // P) + kb
                        m = e.matmul(psum[:, b, n * w:n * w + w], pt[:, c * P:c * P + P], vals[n][kb][0],
                                     start=kb == 0, stop=kb == nk // P - 1)
                return m
            wv = op("pe", weighted, turned + [ex] + [m for v in vals for _, m in v])
            free[("probt", slot)] = [wv]
            nm = op("dve", lambda e: e.tensor_tensor(
                dst.rearrange("p (h d) -> p h d", d=w), psum[:, b, 0:nmax * w].rearrange("p (h d) -> p h d", d=w),
                recip[:, slot, 0:nmax].unsqueeze(2).broadcast_to([P, nmax, w]), ALU.mult), [wv, rc])
            free[("bank", b)] = free[("bank", b + 1)] = [nm]
            free[("recip", slot)] = [nm]
            finished.append(nm)

        def indexer(a, xt_ready, chosen):
            wide = 2 * HD
            marks = gemm_block(("w_in_a", a, 3 * MIX), xt_hi, xt_lo, xt_ready, GEMM)
            idx_free = held(("probt", 0), ("probt", 1))
            qi = evacuate(GEMM, marks, lambda rb: idx[:, rb, 0:IDX_W], idx_free)

            def part(rb):
                def fn(e, hi, lo):
                    w = IDX_H + HD
                    for k in range(KC):
                        m = products(e, psum[:, GEMM[rb], 0:w], xt_hi[:, k, rb * P:rb * P + P],
                                     xt_lo[:, k, rb * P:rb * P + P], hi[:, k * w:k * w + w],
                                     lo[:, k * w:k * w + w], k == 0, k == KC - 1)
                    return m
                return (fn, held(("bank", GEMM[rb])), None)
            marks = use_tile(("w_in_a", a, None, "narrow", 0), [part(rb) for rb in range(RB)])

            k_w, ki_ready = [], []
            for rb in range(RB):
                bank = psum[:, GEMM[rb], 0:IDX_H + HD]
                k_w.append(op("dve", lambda e, rb=rb, bank=bank: e.tensor_scalar(
                    idx[:, rb, IDX_W:IDX_W + IDX_H], bank[:, 0:IDX_H], float((IDX_H * HD) ** -0.5), None, ALU.mult),
                    [marks[rb]] + idx_free))
                ki_ready.append(op("dve", lambda e, rb=rb, bank=bank: e.tensor_copy(
                    idx[:, rb, IDX_W + IDX_H:IDX_W + IDX_H + HD], bank[:, IDX_H:IDX_H + HD]), [marks[rb]]))
                free[("bank", GEMM[rb])] = [ki_ready[rb]]

            def work_on():
                tr, ms = [], []
                for rb in range(RB):
                    ki = idx[:, rb, IDX_W + IDX_H:IDX_W + IDX_H + HD]
                    ms.append(norm_stats(rb, [ki], [ki_ready[rb]]))
                for rb in range(RB):
                    q = rope_heads(rb, idx[:, rb, 0:IDX_W], IDX_H, [qi[rb]] + k_rope)
                    tr += transpose_to(lambda c: idx[:, rb, c * P:c * P + P], [q], range(4),
                                       qit[:, :, rb * P:rb * P + P], "act", hold=held("qit"))
                yield
                for rb in range(RB):
                    ki = idx[:, rb, IDX_W + IDX_H:IDX_W + IDX_H + HD]
                    ki2 = idx[:, rb, IDX_W + IDX_H + HD:IDX_W + IDX_H + wide]
                    both = idx[:, rb, IDX_W + IDX_H:IDX_W + IDX_H + wide]
                    am, rm = ms[rb]
                    r = norm_gain(rb, [ki], [kn_par[:, 2 * a, :]], [am] + k_kn[a])
                    r = norm_bias(rb, [ki], [kn_par[:, 2 * a + 1, :]], r, rm)
                    r = rope_heads(rb, ki, 1, r + k_rope)
                    r = op("dve", lambda e, ki=ki, ki2=ki2: e.tensor_copy(ki2, ki), [r])
                    tr += transpose_to(lambda c, both=both: both, [r], [0], kit[:, rb * P:rb * P + P], "act",
                                       hold=held("qit"))
                yield
                ms = [k_causal, k_causal]
                for rb in range(RB):
                    nk = (rb + 1) * P
                    per = 1024 // nk
                    keep = causal[:, (1 - rb) * P:(1 - rb) * P + nk]
                    acc = keep
                    for g in range(0, IDX_H, per):
                        b = wide_pair()
                        dots = psum[:, b:b + 2, :]
                        pieces = score_pieces(b, per, nk, False)
                        slot = state["slot"] % 2
                        state["slot"] += 1

                        def fn(e, g=g, pieces=pieces, per=per, nk=nk, rb=rb):
                            return accumulate(e, pieces, [
                                (n, head_cols(qit, g + n, rb * P, P), kit[HD * (n % 2):HD * (n % 2) + HD, 0:nk], None)
                                for n in range(per)], nk)
                        m = op("pe", fn, tr + held(("bank", b), ("bank", b + 1)))
                        r = op("act", lambda e, dots=dots, slot=slot: e.activation(
                            prob[slot].rearrange("p (b c) -> p b c", b=2), dots, ACT.Relu), [m] + held(("prob", slot)))
                        free[("bank", b)] = free[("bank", b + 1)] = [r]
                        for n in range(per):
                            h, at = g + n, n % 2 * BLK + n // 2 * nk
                            ms[rb] = op("dve", lambda e, at=at, h=h, slot=slot, acc=acc, nk=nk, rb=rb: e.scalar_tensor_tensor(
                                out=score[:, rb, 0:nk], in0=prob[slot][:, at:at + nk],
                                scalar=idx[:, rb, IDX_W + h:IDX_W + h + 1], in1=acc, op0=ALU.mult, op1=ALU.add),
                                [ms[rb], r, k_w[rb]])
                            acc = score[:, rb, 0:nk]
                        free[("prob", slot)] = [ms[rb]]
                    yield
                v = [score[:, rb, 0:(rb + 1) * P] for rb in range(RB)]
                for n in range(TOPK // 8):
                    for rb in range(RB):
                        ms[rb] = op("dve", lambda e, rb=rb: e.max(top8[:, rb, :], v[rb]), [ms[rb]])
                    for rb in range(RB):
                        ms[rb] = op("dve", lambda e, rb=rb: e.match_replace(v[rb], top8[:, rb, :], v[rb], TAKEN), [ms[rb]])
                    if n % 3 == 2:
                        yield
                for rb in range(RB):
                    nk = (rb + 1) * P
                    m = op("dve", lambda e, rb=rb: e.tensor_scalar(v[rb], v[rb], -2.0e38, BIG, ALU.is_ge, ALU.mult), [ms[rb]])
                    chosen[rb] = op("dve", lambda e, rb=rb, nk=nk: e.tensor_tensor(
                        select[:, rb, 0:nk], v[rb], causal[:, (1 - rb) * P:(1 - rb) * P + nk], ALU.add), [m] + held("select"))
                free["idx"] = free["qit"] = [chosen[1]]
            background.append(work_on())

        def feed_forward(layer, xt_ready):
            acc = [[2 + 2 * rb + h for h in range(2)] for rb in range(RB)]

            def up(step, ready, banks_free):
                for half in range(2):
                    def part(rb, half=half):
                        def fn(e, hi, lo):
                            for k in range(4):
                                kk = 4 * half + k
                                m = products(e, psum[:, GEMM[rb], :], xt_hi[:, kk, rb * P:rb * P + P],
                                             xt_lo[:, kk, rb * P:rb * P + P], hi[:, k * BLK:k * BLK + BLK],
                                             lo[:, k * BLK:k * BLK + BLK], kk == 0, kk == KC - 1)
                            return m
                        w = list(banks_free[rb]) if half == 0 else []
                        if half == 0 and ready:
                            w += ready[rb]
                        return (fn, w, c_gate if half else None)
                    marks = use_tile(("w_gate_up", layer, step, "up", 4 * half), [part(rb) for rb in range(RB)])
                return marks

            def gate(marks, muls, tr):
                done = []
                for rb in range(RB):
                    bank = psum[:, GEMM[rb], :]
                    s = op("act", lambda e, rb=rb, bank=bank: e.activation(ff_silu[:, rb, :], bank[:, 0:FF_STEP], ACT.Silu),
                           [marks[rb], muls[rb]] if muls else [marks[rb]] + held("proj"))
                    done.append(op("dve", lambda e, rb=rb, bank=bank: e.tensor_tensor(
                        ff_h[:, rb, :], ff_silu[:, rb, :], bank[:, FF_STEP:BLK], ALU.mult),
                        [s] + ([tr] if tr else []), inc=c_mul))
                return done

            def turn_h(muls, lo, used):
                def fn(e):
                    for c in range(2):
                        for rb in range(RB):
                            m = e.transpose(psum[:, 6, (2 * c + rb) * P:(2 * c + rb + 1) * P],
                                            ff_h[:, rb, c * P:c * P + P], ident[:, :])
                    return m
                tr = op("pe", fn, list(muls) + ([lo] if lo else held(("bank", 6))), inc=c_tr)
                v = psum[:, 6, :].rearrange("p (c s) -> p c s", s=SEQ)
                h = op("act", lambda e: e.activation(ht_hi[:, :, :], v, ACT.Copy), [tr] + used, inc=c_ht_hi)
                low = op("dve", lambda e: e.tensor_tensor(ht_lo[:, :, :], v, ht_hi[:, :, :].bitcast(F32),
                                                          ALU.subtract), [h], inc=c_ht_lo)
                return tr, low

            def down(step, low, first, last):
                def part(rb):
                    def fn(e, hi, lo):
                        for c in range(2):
                            for h in range(2):
                                w = c * D + h * BLK
                                m = products(e, psum[:, acc[rb][h], :], ht_hi[:, c, rb * P:rb * P + P],
                                             ht_lo[:, c, rb * P:rb * P + P], hi[:, w:w + BLK], lo[:, w:w + BLK],
                                             first and c == 0, last and c == 1)
                        return m
                    w = [low] if rb == 0 else []
                    if first:
                        w += held(("bank", acc[rb][0]), ("bank", acc[rb][1]))
                    return (fn, w, None)
                return use_tile(("w_down", layer, step, "down", 0), [part(rb) for rb in range(RB)])

            marks = up(0, xt_ready, [held(("bank", GEMM[rb])) for rb in range(RB)])
            muls = gate(marks, None, None)
            tr, low = turn_h(muls, None, [])
            marks = up(1, None, [[m] for m in muls])
            muls = gate(marks, muls, tr)
            used = down(0, low, True, False)
            tr, low = turn_h(muls, low, [used[-1]])
            plan.begin(FF_STEPS - 2)
            t_in = state["tile"]
            marks = up(2, None, [[m] for m in muls])
            muls = gate(marks, muls, tr)
            used = down(1, low, False, False)
            tr, low = turn_h(muls, low, [used[-1]])
            loop = plan.end()
            more = (FF_STEPS - 3) * 3
            assert state["tile"] - t_in == 3
            for step in range(3, FF_STEPS):
                order.extend([("w_gate_up", layer, step, "up", k0) for k0 in (0, 4)]
                             + [("w_down", layer, step - 1, "down", 0)])
            state["tile"] += more
            state["split"] += more
            muls = [plan.last_trip(loop, m) for m in muls]
            low = plan.last_trip(loop, low)
            for rb in range(RB):
                free[("bank", GEMM[rb])] = [muls[rb]]
            free[("bank", 6)] = [low]
            free["proj"] = [muls[1]]
            marks = down(FF_STEPS - 1, low, False, True)
            return marks, acc

        def residual_norm(marks, banks, s, par_ready):
            gains, biases = halves(par[:, s, 0:D]), halves(par[:, s, D:2 * D])
            v = [halves(x[:, rb, :]) for rb in range(RB)]
            used = [(c_tile, state["tile"])]

            def mean_of(rb):
                for h in range(2):
                    m = op("dve", lambda e, rb=rb, h=h: e.scalar_tensor_tensor(
                        out=v[rb][h], in0=v[rb][h], scalar=ALPHA, in1=psum[:, banks[rb][h], :], op0=ALU.mult,
                        op1=ALU.add), [marks[rb][h]])
                    free[("bank", banks[rb][h])] = [m]
                am, rm = norm_stats(rb, v[rb], [m])
                return norm_gain(rb, v[rb], gains, [am] + par_ready), rm
            g0, r0 = mean_of(0)
            g1, r1 = mean_of(1)
            ready = []
            for rb, (g, r) in enumerate(((g0, r0), (g1, r1))):
                b = norm_bias(rb, v[rb], biases, g, r)
                free[("par", s)] = [b[1]]
                ready.append(to_stationary(x[:, rb, :], [[b[0]], [b[1]]], xt_hi, xt_lo, rb, hold=used))
            return ready

        def out_product(name, layer, ready):
            banks = [[2 + 2 * rb + h for h in range(2)] for rb in range(RB)]
            marks = [[None, None], [None, None]]
            for h in range(2):
                done = gemm_block((name, layer, h * BLK), xt_hi, xt_lo, ready, [banks[rb][h] for rb in range(RB)])
                for rb in range(RB):
                    marks[rb][h] = done[rb]
            return marks, banks

        ada_left = [(layer, c) for layer in range(DEPTH_2) for c in range(6)]

        def ada_blocks(count):
            for _ in range(count):
                layer, c = ada_left.pop(0)
                bank, row = GEMM[c % 2], 6 * layer + c
                marks = gemm_block(("w_ada_2", layer, c * BLK), cond_hi, cond_lo, {0: [k_col]}, [bank], [0], shared=True)
                m = op("dve", lambda e, bank=bank, row=row: e.scalar_tensor_tensor(
                    out=ada[:, :], in0=psum[0:12, bank, :], scalar=ident[0:12, row:row + 1], in1=ada[:, :],
                    op0=ALU.mult, op1=ALU.add), [marks[0]] + held("ada") + [k_ada])
                free["ada"] = free[("bank", bank)] = [m]

        a = 0
        for layer, kind in enumerate(KINDS):
            ln1, k_ln1 = load_norm(f"ln1_{layer}", T["ln1_g"][layer], T["ln1_b"][layer])
            chosen = [None, None]
            if kind == "A":
                w_in = ("w_in_a", a)
                indexer(a, xt, chosen)
                a += 1
            else:
                w_in = ("w_in_b" if kind == "B" else "w_in_c", 0)
            if layer == 0:
                background.append(memory_work())
            blocks = {}

            def project(c, hold):
                marks = gemm_block(w_in + (("proj", c),), xt_hi, xt_lo, xt, GEMM)
                blocks[c] = evacuate(GEMM, marks, lambda rb: proj[:, rb, c * BLK:c * BLK + BLK], hold)

            for c in range(3):
                project(c, held("proj"))
            drain_background()
            turned = []
            for rb in range(RB):
                r = rope_heads(rb, proj[:, rb, 0:2 * MIX], 2 * NH, [blocks[c][rb] for c in range(3)] + k_rope)
                for n0, n1, dst, scale in ((0, 4, qt, HD ** -0.5), (4, 6, qt, HD ** -0.5), (0, 4, kt, 1.0), (4, 6, kt, 1.0)):
                    c0 = (0 if dst is qt else MIX)
                    turned += transpose_to(lambda n: proj[:, rb, c0 + n * P:c0 + n * P + P], [r], range(n0, n1),
                                           dst[:, n0:n1, rb * P:rb * P + P], "act" if n0 == 0 else "dve", scale,
                                           held("heads"))
            outs = [[], []]
            memory = {}
            q_turned = list(turned)

            def own_units(rb):
                nk = (rb + 1) * P
                if kind == "B":
                    for h in range(DIL_H):
                        seg = [(head_cols(qt, g * DIL_H + h, rb * P, P), head_cols(kt, g * DIL_H + h, 0, nk),
                                m_pair[g] if rb else m_pair[g][:, P:2 * P], nk) for g in range(DIL)]
                        c0 = 2 * MIX + h * DIL_V

                        def values(n, kb, c0=c0):
                            return proj[:, kb, c0:c0 + DIL_V], blocks[(c0 + DIL_V - 1) // BLK][kb]
                        yield attention_unit(seg, True, values, mixed[:, rb, h * DIL_V:h * DIL_V + DIL_V],
                                             lambda: q_turned, outs[rb])
                    return
                per = 4 if rb else 6
                for h0 in range(0, NH, per):
                    bias = select[:, rb, 0:nk] if kind == "A" else m_causal
                    seg = [(head_cols(qt, h, rb * P, P), head_cols(kt, h, 0, nk), bias, nk) for h in range(h0, h0 + per)]

                    def values(n, kb, h0=h0):
                        c0 = 2 * MIX + (h0 + n) * HD
                        return proj[:, kb, c0:c0 + HD], blocks[c0 // BLK][kb]
                    yield attention_unit(seg, False, values, mixed[:, rb, h0 * HD:(h0 + per) * HD],
                                         lambda: q_turned + [m for m in (chosen[rb], k_maskb) if m], outs[rb])

            def memory_unit(rb):
                seg = [(head_cols(qmt, h, rb * P, P), head_cols(mkt, h, 0, SEQ), None, SEQ) for h in range(MEM_H)]
                return attention_unit(seg, False, lambda n, kb: (mkv[:, kb, MEMW + n * HD:MEMW + n * HD + HD],
                                                                 memory["kv"][kb]),
                                      mixed[:, rb, MIX:MIX + MEMW], lambda: memory["turned"], outs[rb])

            project(3, held("values"))
            background.append(pipelined(list(own_units(0)) + list(own_units(1)) + [memory_unit(0), memory_unit(1)]))
            project(4, held("values"))
            xt_used = (c_tile, state["tile"])
            tm = []
            for rb in range(RB):
                tm += transpose_to(lambda n: proj[:, rb, 3 * MIX + n * P:3 * MIX + n * P + P], [blocks[4][rb]],
                                   range(2), qmt[:, :, rb * P:rb * P + P], "act", HD ** -0.5, held("heads"))
            marks = gemm_block(("w_mem_kv", layer, 0), mt_hi, mt_lo, mt, GEMM)
            mk = evacuate(GEMM, marks, lambda rb: mkv[:, rb, :], held("mkv"))
            for rb in range(RB):
                tm += transpose_to(lambda n: mkv[:, rb, n * P:n * P + P], [mk[rb]], range(2),
                                   mkt[:, :, rb * P:rb * P + P], "dve", 1.0, held("mkv"))
            memory["kv"], memory["turned"] = mk, tm
            ada_blocks(3)
            drain_background()
            free["heads"] = free["select"] = free["mkv"] = free["values"] = [outs[1][-1]]
            mx = [to_stationary(mixed[:, rb, :], [[outs[rb][-1]]] * 2, xt_hi, xt_lo, rb, hold=[xt_used])
                  for rb in range(RB)]
            free["proj"] = [m for t in mx for m in t]
            marks, banks = out_product("w_out", layer, mx)
            ln2, k_ln2 = load_norm(f"ln2_{layer}", T["ln2_g"][layer], T["ln2_b"][layer])
            xt = residual_norm(marks, banks, ln1, k_ln1)
            marks, banks = feed_forward(layer, xt)
            xt = residual_norm([[m, m] for m in marks], banks, ln2, k_ln2)

        mod = par[:, :, :].rearrange("p s c -> p (s c)")
        shift, gain, gate_row, gvec = [mod[:, n * D:n * D + D] for n in range(4)]
        decay = kv[:, 0:1536].rearrange("p (h c) -> p h c", h=RET_H)
        memory_scope.close()
        rt = sb("heads_t2", [P, 16, SEQ])
        k_decay = load("decay", decay, T["decay"], held("mkv"))
        ret_cs = score
        k_ret = load("ret_cs", ret_cs[:, :, 0:P], T["ret_cos_sin"].rearrange("(r p) c -> p r c", p=P), held("select"))
        tri = causal
        k_tri = load("tri", tri[:, :], T["tri"], held("select"))
        k_strict = load("strict", strict[:, :], T["strict"])
        strict_b_f = rt[:, 0, 0:P]
        k_sbf = load("strict_bias", strict_b_f, T["strict_bias"], held("mkv"))
        strict_b = masks[:, P:2 * P]
        k_sb = op("dve", lambda e: e.tensor_copy(strict_b, strict_b_f), [k_sbf] + held("select"))
        k_par_free = held(("par", 0), ("par", 1))
        free["rt"] = [k_sb]
        xready = [[m for t in xt for m in t]] * RB

        def rms(rb, ready, scratch):
            q = op("act", lambda e: e.activation(scratch, x[:, rb, :], ACT.Square, accum_out=expsum[:, rb, 0:1]),
                   list(ready) + held(("expsum", 0), ("expsum", 1), "rows2"))
            m = op("dve", lambda e: e.tensor_scalar(rstd[:, rb, 0:1], expsum[:, rb, 0:1], 1.0 / D, EPS_2,
                                                    ALU.mult, ALU.add), [q])
            free[("expsum", rb)] = [m]
            return power(rb, 1, [m])

        for layer in range(DEPTH_2):
            k_g = load(f"g2_{layer}", gvec, rows(T["norm_g_2"][layer]), k_par_free)
            mods = []
            for c in range(6):
                bank, row = GEMM[c % 2], 6 * layer + c
                m = op("pe", lambda e, bank=bank, row=row: e.matmul(
                    psum[:, bank, :], ident[0:12, row:row + 1].broadcast_to([12, P]), ada[:, :], start=True, stop=True),
                    held(("bank", bank), "ada"))
                v, b = mod[:, c * BLK:c * BLK + BLK], psum[:, bank, :]
                if c in (2, 3):
                    g = gvec[:, (c - 2) * BLK:(c - 1) * BLK]
                    m = op("dve", lambda e, v=v, b=b, g=g: e.scalar_tensor_tensor(
                        out=v, in0=b, scalar=1.0, in1=g, op0=ALU.add, op1=ALU.mult), [m, k_g] + k_par_free)
                else:
                    m = op("act", lambda e, v=v, b=b: e.activation(v, b, ACT.Copy), [m] + k_par_free)
                free[("bank", bank)] = [m]
                mods.append(m)
            rs = [rms(rb, xready[rb], rows2[:, rb, :]) for rb in range(RB)]
            ready = []
            for rb in range(RB):
                done = []
                for h in range(2):
                    v, cols = rows2[:, rb, h * BLK:h * BLK + BLK], slice(h * BLK, h * BLK + BLK)
                    m = op("dve", lambda e, rb=rb, v=v, cols=cols: e.scalar_tensor_tensor(
                        out=v, in0=x[:, rb, cols], scalar=rstd[:, rb, 0:1], in1=gain[:, cols], op0=ALU.mult,
                        op1=ALU.mult), [mods[2 + h], rs[rb]])
                    done.append([op("dve", lambda e, v=v, cols=cols: e.tensor_tensor(v, v, shift[:, cols], ALU.add),
                                    [m, mods[h]])])
                ready.append(to_stationary(rows2[:, rb, :], done, xt_hi, xt_lo, rb, hold=[(c_tile, state["tile"])]))
            x_rows_used = [m for t in ready for m in t]
            blocks = {}

            def project(c):
                marks = gemm_block(("w_in_2", layer, c * BLK), xt_hi, xt_lo, ready, GEMM)
                blocks[c] = evacuate(GEMM, marks, lambda rb: proj2[:, rb, c * BLK:c * BLK + BLK],
                                     held("proj", "heads", "values"), ACT.Silu if c % 4 == 3 else ACT.Copy)

            def turn_block(c, dst, scale, engine, marks_in=None):
                out_m = []
                for rb in range(RB):
                    out_m += transpose_to(lambda n: proj2[:, rb, c * BLK + n * P:c * BLK + n * P + P],
                                          marks_in or [blocks[c][rb]], range(4), dst[:, :, rb * P:rb * P + P],
                                          engine, scale, held("rt"))
                return out_m
            sqt, skt, rqt, rkt = [rt[:, 4 * n:4 * n + 4, :] for n in range(4)]
            project(4)
            turned = turn_block(4, sqt, SB_D ** -0.5, "act")
            project(5)
            turned += turn_block(5, skt, 1.0, "dve")
            sb_bufs = [arena[:, 8192 + 1024 * n:8192 + 1024 * n + 1024] for n in range(2)]
            y_sb, y_ret = [], []

            def stick_breaking(h):
                b = wide_pair()
                z = psum[:, b, 0:384]
                buf = sb_bufs[h % 2]
                mag, sp = buf[:, 0:384], buf[:, 384:768]
                key = [head_cols(skt, h, n * P, P) for n in range(2)]
                qry = [head_cols(sqt, h, n * P, P) for n in range(2)]

                def fn(e):
                    e.matmul(z[:, 0:128], key[0], qry[0], start=True, stop=False)
                    e.matmul(z[:, 128:256], key[1], qry[1], start=False, stop=False)
                    return e.matmul(z[:, 256:384], key[0], qry[1], start=False, stop=True)
                m = op("pe", fn, turned + held(("bank", b)))
                s1 = op("act", lambda e: e.activation(mag, z, ACT.Abs), [m] + held(("sbuf", h % 2), "heads"))
                s2 = op("act", lambda e: e.activation(mag, mag, ACT.Exp, scale=-1.0), [s1])
                s3 = op("act", lambda e: e.activation(mag, mag, ACT.Ln, bias=1.0), [s2])
                yield
                m = op("dve", lambda e: e.scalar_tensor_tensor(out=sp, in0=z, scalar=0.0, in1=mag, op0=ALU.max,
                                                               op1=ALU.add), [s3])
                v = sp[:, 0:256].rearrange("p (b q) -> p b q", b=2)
                m = op("dve", lambda e: e.tensor_tensor(v, v, strict[:, :].unsqueeze(1).broadcast_to([P, 2, P]),
                                                        ALU.mult), [m, k_strict])

                def less_later(e):
                    on = dict(start=False, skip_group_check=True)
                    e.matmul(z, tri[:, 0:P], sp, stop=False, **on)
                    e.matmul(z[:, 256:384], tri[:, P:SEQ], sp[:, 128:256], stop=False, **on)
                    e.matmul(z[:, 0:128], identb, strict_b, stop=False, **on)
                    return e.matmul(z[:, 128:256], identb, strict_b, stop=True, **on)
                m = op("pe", less_later, [m, k_tri, k_sb])
                a1 = op("act", lambda e: e.activation(mag, z, ACT.Exp), [m])
                yield

                def weighted(e):
                    v = [proj2[:, kb, 3072 + h * HD:3072 + h * HD + HD] for kb in range(RB)]
                    e.matmul(psum[:, b + 1, 0:64], mag[:, 0:128], v[0], start=True, stop=True)
                    e.matmul(psum[:, b + 1, 64:128], mag[:, 256:384], v[0], start=True, stop=False)
                    return e.matmul(psum[:, b + 1, 64:128], mag[:, 128:256], v[1], start=False, stop=True)
                o = op("pe", weighted, [a1] + blocks[6] + held(("bank", b + 1)))
                free[("sbuf", h % 2)] = [o]
                m = op("dve", lambda e: e.tensor_copy(rows2[:, :, 512 + h * HD:512 + h * HD + HD],
                                                      psum[:, b + 1, 0:128].rearrange("p (r d) -> p r d", r=RB)),
                       [o] + x_rows_used)
                free[("bank", b)] = free[("bank", b + 1)] = [m]
                y_sb.append(m)

            def turn_retention():
                tmp = [tmp2[:, k * 512:k * 512 + 512] for k in range(4)]
                done = []
                for rb in range(RB):
                    v = proj2[:, rb, 0:D].rearrange("p (h d) -> p h d", d=RET_D)
                    done.append(rotary(rb, v, 8, RET_D // 2, ret_cs[:, rb, 0:64], ret_cs[:, rb, 64:128], tmp,
                                       [blocks[0][rb], blocks[1][rb], k_ret] + held("rows2")))
                    yield
                ret_turned.extend(turn_block(0, rqt, 1.0, "dve", done))
                ret_turned.extend(turn_block(1, rkt, 1.0, "act", done))
            ret_turned = []

            def retention(h):
                b = wide_pair()
                s = tmp2[:, 512 * (h % 2):512 * (h % 2) + 384]

                def fn(e):
                    e.matmul(psum[:, b, 0:256], rkt[:, h, 0:P], rqt[:, h, :], start=True, stop=True)
                    return e.matmul(psum[:, b, 256:384], rkt[:, h, P:SEQ], rqt[:, h, P:SEQ], start=True, stop=True)
                m = op("pe", fn, ret_turned + held(("bank", b)))
                d = op("dve", lambda e: e.tensor_tensor(s, psum[:, b, 0:384], decay[:, h, :], ALU.mult),
                       [m, k_decay] + held("rope_tmp", ("ret_s", h % 2)))
                yield

                def weighted(e):
                    v = [proj2[:, kb, D + h * P:D + h * P + P] for kb in range(RB)]
                    e.matmul(psum[:, b + 1, 0:128], s[:, 0:128], v[0], start=True, stop=True)
                    e.matmul(psum[:, b + 1, 128:256], s[:, 128:256], v[0], start=True, stop=False)
                    return e.matmul(psum[:, b + 1, 128:256], s[:, 256:384], v[1], start=False, stop=True)
                o = op("pe", weighted, [d] + blocks[2] + held(("bank", b + 1)))
                free[("ret_s", h % 2)] = [o]
                yield
                for rb in range(RB):
                    src = psum[:, b + 1, rb * P:rb * P + P]
                    m = op("dve", lambda e, rb=rb, src=src: e.bn_stats(stats[:, rb, h, :], src), [o])
                for rb in range(RB):
                    m = op("dve", lambda e, rb=rb: e.bn_aggr(agg[:, rb, h, :], stats[:, rb, h, :]), [m])
                for rb in range(RB):
                    m = op("dve", lambda e, rb=rb: e.tensor_scalar(
                        rows2[:, rb, h * P:h * P + P], psum[:, b + 1, rb * P:rb * P + P], agg[:, rb, h, 0:1], None,
                        ALU.subtract), [m] + x_rows_used)
                free[("bank", b)] = free[("bank", b + 1)] = [m]
                y_ret.append(m)

            background.append(pipelined([stick_breaking(h) for h in range(SB_H)]))
            for c in (6, 0, 1):
                project(c)
            background.append(turn_retention())
            background.append(pipelined([retention(h) for h in range(RET_H)]))
            for c in (2, 3, 7):
                project(c)
            drain_background()
            xt_used = (c_tile, state["tile"])
            free["rt"] = [y_sb[-1], y_ret[-1]]
            for rb in range(RB):
                m = op("dve", lambda e, rb=rb: e.tensor_scalar(rstd[:, rb, :], agg[:, rb, :, 1], EPS_2, None, ALU.add),
                       [y_ret[-1]])
                y_ret.append(power(rb, RET_H, [m]))
            yt = []
            for rb in range(RB):
                v = rows2[:, rb, 512:1024]
                g = op("dve", lambda e, rb=rb, v=v: e.tensor_tensor(v, v, proj2[:, rb, 3584:4096], ALU.mult),
                       [y_sb[-1], blocks[7][rb]])
                for h in range(RET_H):
                    m = op("dve", lambda e, rb=rb, h=h: e.scalar_tensor_tensor(
                        out=rows2[:, rb, h * P:h * P + P], in0=rows2[:, rb, h * P:h * P + P], scalar=rstd[:, rb, h:h + 1],
                        in1=proj2[:, rb, 1536 + h * P:1536 + h * P + P], op0=ALU.mult, op1=ALU.mult),
                        [y_ret[-RB + rb], blocks[3][rb]])
                yt.append(to_stationary(rows2[:, rb, :], [[m], [g]], xt_hi, xt_lo, rb, hold=[xt_used]))
            free["proj"] = free["heads"] = free["values"] = [m for t in yt for m in t]
            marks, banks = out_product("w_out_2", layer, yt)
            xready = [[], []]
            for h in range(2):
                for rb in range(RB):
                    t = tmp2[:, (2 * h + rb) * 512:(2 * h + rb) * 512 + 512]
                    v = x[:, rb, h * BLK:h * BLK + BLK]
                    m = op("dve", lambda e, t=t, h=h, bank=banks[rb][h]: e.tensor_tensor(
                        t, psum[:, bank, :], gate_row[:, h * BLK:h * BLK + BLK], ALU.mult), [marks[rb][h], mods[-1], mods[-2]])
                    free[("bank", banks[rb][h])] = [m]
                    xready[rb].append(op("dve", lambda e, t=t, v=v: e.tensor_tensor(v, v, t, ALU.add), [m]))
            free["rows2"] = [xready[1][1]] + yt[0] + yt[1]
            k_par_free = [xready[1][1]]

        k_f = load("final_g", shift, rows(T["final_g_2"]), k_par_free)
        rs = [rms(rb, xready[rb], rows2[:, rb, :]) for rb in range(RB)]
        for rb in range(RB):
            m = op("dve", lambda e, rb=rb: e.scalar_tensor_tensor(
                out=x[:, rb, :], in0=x[:, rb, :], scalar=rstd[:, rb, 0:1], in1=shift, op0=ALU.mult, op1=ALU.mult),
                [rs[rb], k_f])
            op("act", lambda e, rb=rb: e.dma_start(out[rb * P:rb * P + P, :], x[:, rb, :]), [m], inc=c_out, by=16)
        assert state["tile"] == len(order) == N_TILES and not ada_left

        block = ctx.enter_context(nc.Block())

        @block.sync
        def _(sp):
            n = N_TILES
            W = T["weights"]
            for t in range(RING):
                sp.dma_start(raw[:, t, :], W[t]).then_inc(c_raw[t].sem, 16)
            trips = (n - RING) // RING
            with sp.Fori(0, trips) as i:
                for s in range(RING):
                    sp.wait_ge(c_lo.sem, i * RING + s + 1)
                    src = W[bass.ds(i * RING + RING + s, 1), :, :].rearrange("a p c -> (a p) c")
                    sp.dma_start(raw[:, s, :], src).then_inc(c_raw[s].sem, 16)
            for t in range(RING + trips * RING, n):
                sp.wait_ge(c_lo.sem, t - RING + 1)
                sp.dma_start(raw[:, t % RING, :], W[t]).then_inc(c_raw[t % RING].sem, 16)

        @block.tensor
        def _(e):
            plan.emit("pe", e)

        @block.scalar
        def _(e):
            plan.emit("act", e)
            e.wait_ge(c_out.sem, 16 * RB)

        @block.vector
        def _(e):
            plan.emit("dve", e)

        @block.gpsimd
        def _(e):
            plan.emit("pool", e)
    return order



def pack_weights(order, inputs):
    w = np.zeros((len(order), P, TW), np.float32)

    def chunks(a):
        k, n = a.shape
        return a.reshape(k // P, P, n).transpose(1, 0, 2).reshape(P, -1)

    for n, (name, layer, cols, what, k0) in enumerate(order):
        m = inputs[name][layer]
        r = slice(k0 * P, k0 * P + 4 * P)
        if what == "half" and isinstance(cols, tuple):
            c0 = cols[1] * BLK
            own = m[r, c0:min(c0 + BLK, 3 * MIX)]
            if c0 + BLK > 3 * MIX:
                own = np.concatenate([own, m[r, m.shape[1] - MEMW:]], axis=1)
        elif what == "half":
            own = m[r, cols:cols + BLK]
        elif what == "narrow":
            c0 = 3 * MIX + IDX_W
            own = m[:, c0:c0 + IDX_H + HD]
        elif what == "up":
            c0 = cols * FF_STEP
            own = np.concatenate([m[r, c0:c0 + FF_STEP], m[r, D_FF + c0:D_FF + c0 + FF_STEP]], axis=1)
        else:
            own = m[cols * FF_STEP:(cols + 1) * FF_STEP, :]
        own = chunks(own)
        w[n, :, 0:own.shape[1]] = own
    return w


def shape_constants():
    i = np.arange(P)
    q, s = i[:, None], i[None, :]
    big = lambda keep: np.where(keep, 0.0, BIG).astype(np.float32)
    pieces = [np.eye(P, dtype=np.float32), big(s >= q), big(s <= q)]
    for dil in (4, 16):
        same = (q - s) % dil == 0
        pieces += [big(same), big(same & (s <= q))]
    n, m = np.arange(SEQ)[None, :], np.arange(SEQ)[:, None]
    head = np.arange(RET_H, dtype=np.float64)
    log_gamma = np.log1p(-(2.0 ** (-5.0 - head)))
    seen = m // CHUNK <= n // CHUNK
    decay = np.where(seen, np.exp(np.abs(n - m)[None] * log_gamma[:, None, None]), 0.0) * RET_D ** -0.5
    decay = np.concatenate([decay[:, 0:P, :], decay[:, P:, P:]], axis=2).transpose(1, 0, 2)
    half = RET_D // 2
    inv2 = ROPE_BASE ** (-np.arange(half, dtype=np.float32) / np.float32(half))
    ang = np.arange(SEQ, dtype=np.float32)[:, None] * inv2.astype(np.float32)[None, :]
    f = lambda a: np.ascontiguousarray(a, dtype=np.float32)
    return {
        "ident": np.eye(P, dtype=np.float32),
        "masks": f(np.concatenate(pieces, axis=1)),
        "causal": f(np.concatenate([np.zeros((P, P)), big(s <= q)], axis=1)),
        "inv_freq": f(np.float32(ROPE_THETA) ** (-np.arange(ROPE_HALF, dtype=np.float32) / np.float32(ROPE_HALF))),
        "decay": f(decay),
        "ret_cos_sin": f(np.concatenate([np.cos(ang), np.sin(ang)], axis=1)),
        "tri": f(np.concatenate([-(q >= s).astype(np.float32), -np.ones((P, P))], axis=1)),
        "strict": f(q < s),
        "strict_bias": big(q < s),
    }


_SMALL = ["x", "mem", "positions", "mem_ln_g", "mem_ln_b", "idx_kn_g", "idx_kn_b", "ln1_g", "ln1_b", "ln2_g",
          "ln2_b", "c_2", "norm_g_2", "b_ada_2", "final_g_2"]
_FLAT = {"x": (SEQ, D), "mem": (SEQ, D)}


def kernel(**inputs):
    import concourse.bacc as _bacc
    from concourse.bass_utils import run_bass_kernel_spmd as _run

    nc = _bacc.Bacc("TRN2", target_bir_lowering=False, num_devices=1)
    given = {k: np.asarray(v) for k, v in inputs.items()}
    arrays = {k: np.ascontiguousarray(given[k].reshape(_FLAT.get(k, given[k].shape))) for k in _SMALL}
    for name in ("positions", "c_2"):
        arrays[name] = np.ascontiguousarray(given[name].reshape(-1, P).T)
    arrays.update(shape_constants())
    T, feed = {}, {}
    for name, a in arrays.items():
        feed[f"in_{name}"] = a
        T[name] = nc.dram_tensor(f"in_{name}", a.shape, mybir.dt.from_np(a.dtype), kind="ExternalInput").ap()
    T["weights"] = nc.dram_tensor("in_weights", (N_TILES, P, TW), F32, kind="ExternalInput").ap()
    out = nc.dram_tensor("out_rows", (SEQ, D), F32, kind="ExternalOutput").ap()
    order = stack_kernel(nc, T, out)
    feed["in_weights"] = pack_weights(order, given)
    r = _run(nc, [feed], core_ids=[0])
    return r.results[0]["out_rows"].reshape(1, SEQ, D)
```

```python
from contextlib import ExitStack

import numpy as np

import concourse.bass as bass
from concourse import mybir

F32 = mybir.dt.float32
F32R = mybir.dt.float32r
BF16 = mybir.dt.bfloat16
I32 = mybir.dt.int32
ALU = mybir.AluOpType
ACT = mybir.ActivationFunctionType
AX = mybir.AxisListType

P = 128
D = 1024
SEQ = 256
RB = SEQ // P
KC = D // P
KINDS = "ABCA"
N_A, N_BC = 2, 1
HD = 64
NH = 12
MIX = NH * HD
MEM_H = 4
MEMW = MEM_H * HD
IDX_H = 8
IDX_W = IDX_H * HD
ROPE_HALF = HD // 8
ROPE_THETA = 500000.0
TOPK = min(256, SEQ // 4)
DIL = 3
DIL_H = 4
DIL_V = MIX // DIL_H
D_FF = 2816
FF_STEP = 256
FF_STEPS = D_FF // FF_STEP
ALPHA = float((2 * len(KINDS)) ** 0.25)
LN_EPS = 1e-5
DEPTH_2 = 2
CHUNK = 64
RET_H, RET_D = 4, 128
SB_H, SB_D = 8, 64
D_HALF = 512
EPS_2 = 1e-6
ROPE_BASE = 10000.0

TW = 2048
BLK = 512
RING = 3
BIG = -1.0e30
TAKEN = -3.0e38


N_TILES = (2 * KINDS.count("A") * 1 + KINDS.count("A")
           + len(KINDS) * 2 * (5 + 1 + 2) + len(KINDS) * 3 * FF_STEPS
           + DEPTH_2 * 2 * (6 + 8 + 2))



class Counter:

    def __init__(self, sem):
        self.sem, self.n = sem, 0


class Loop:
    def __init__(self, trips, counters):
        self.trips, self.start, self.per = trips, {c: c.n for c in counters}, {}


class Late:

    def __init__(self, make):
        self.make = make


class Plan:
    ENGINES = ("pe", "act", "dve", "pool")

    def __init__(self, nc, ctx):
        self.nc, self.ctx = nc, ctx
        self.queue = {e: [] for e in self.ENGINES}
        self.counters = []
        self.loop = None
        self.done = {e: self.counter(f"{e}_done") for e in self.ENGINES}

    def counter(self, name):
        c = Counter(self.ctx.enter_context(self.nc.semaphore(name)))
        self.counters.append(c)
        return c

    def op(self, engine, fn, wait=(), inc=None, by=1):
        inc = inc or self.done[engine]
        inc.n += by
        self.queue[engine].append((fn, tuple(wait), inc, by))
        return (inc, inc.n)

    def begin(self, trips):
        self.loop = Loop(trips, self.counters)
        for q in self.queue.values():
            q.append(self.loop)

    def end(self):
        loop, self.loop = self.loop, None
        for c, n in loop.start.items():
            loop.per[c] = c.n - n
            c.n += (loop.trips - 1) * loop.per[c]
        for q in self.queue.values():
            q.append(None)
        return loop

    @staticmethod
    def last_trip(loop, mark):
        c, v = mark
        return (c, v + (loop.trips - 1) * loop.per[c])

    def emit(self, name, engine):
        items = iter(self.queue[name])
        waited = {}

        def one(item, loop, i):
            fn, waits, inc, by = item
            for c, v in waits:
                per = loop.per[c] if loop else 0
                if per:
                    engine.wait_ge(c.sem, i * per + v)
                elif waited.get(c, 0) < v:
                    engine.wait_ge(c.sem, v)
                    waited[c] = v
            fn(engine).then_inc(inc.sem, by)

        for item in items:
            if isinstance(item, Loop):
                loop, body = item, []
                for inner in items:
                    if inner is None:
                        break
                    body.append(inner)
                if body:
                    with engine.Fori(0, loop.trips) as i:
                        for inner in body:
                            one(inner, loop, i)
            else:
                one(item, None, None)



def stack_kernel(nc, T, out):
    order = []
    with ExitStack() as ctx:
        plan = Plan(nc, ctx)
        op = plan.op

        def sb(name, shape, dt=F32):
            return ctx.enter_context(nc.sbuf_tensor(name, shape, dt))

        raw = sb("w_raw", [P, RING, TW])
        w_hi = sb("w_high", [P, RING, TW], F32R)
        w_lo = sb("w_low", [P, RING, TW], F32R)
        xt_hi = sb("xt_high", [P, KC, SEQ], F32R)
        xt_lo = sb("xt_low", [P, KC, SEQ], F32R)
        ht_hi = sb("ht_high", [P, 2, SEQ], F32R)
        ht_lo = sb("ht_low", [P, 2, SEQ], F32R)
        x = sb("x_rows", [P, RB, D])
        arena = sb("arena", [P, 10240])
        work = sb("work", [P, 4096])
        kv = sb("mem_kv", [P, 1536])
        par = sb("norm_params", [P, 2, 2 * D])
        proj = arena[:, 0:5120].rearrange("p (r c) -> p r c", r=RB)
        mixed = proj[:, :, 0:D]
        qt = arena[:, 5120:6656].rearrange("p (c s) -> p c s", s=SEQ)
        kt = arena[:, 6656:8192].rearrange("p (c s) -> p c s", s=SEQ)
        qmt = arena[:, 8192:8704].rearrange("p (c s) -> p c s", s=SEQ)
        qit = arena[:, 8704:9728].rearrange("p (c s) -> p c s", s=SEQ)
        kit = arena[:, 9728:9984]
        ff_silu = arena[:, 0:512].rearrange("p (r c) -> p r c", r=RB)
        ff_h = arena[:, 512:1024].rearrange("p (r c) -> p r c", r=RB)
        prob = [work[:, 1024 * n:1024 * n + 1024] for n in range(2)]
        probt = [work[:, 2048 + 1024 * n:3072 + 1024 * n] for n in range(2)]
        idx = work[:, 2048:2048 + RB * 704].rearrange("p (r c) -> p r c", r=RB)
        mkv = kv[:, 0:1024].rearrange("p (r c) -> p r c", r=RB)
        mkt = kv[:, 1024:1536].rearrange("p (c s) -> p c s", s=SEQ)
        score = sb("idx_score", [P, RB, SEQ])
        select = sb("select_bias", [P, RB, SEQ], BF16)
        proj2 = arena[:, 0:8192].rearrange("p (r c) -> p r c", r=RB)
        rows2 = work[:, 0:2048].rearrange("p (r c) -> p r c", r=RB)
        tmp2 = work[:, 2048:4096]
        ident = sb("ident", [P, P])
        masks = sb("masks", [P, 7 * P], BF16)
        identb, m_win, m_causal = masks[:, 0:128], masks[:, 128:256], masks[:, 256:384]
        m_pair = [masks[:, 128:384], masks[:, 384:640], masks[:, 640:896]]
        causal = sb("causal", [P, SEQ])
        half_neg = sb("half_neg", [P, 8])
        rope_c = sb("rope_cos", [P, RB, ROPE_HALF])
        rope_s = sb("rope_sin", [P, RB, ROPE_HALF])
        rope_t = sb("rope_tmp", [P, 4, 24 * ROPE_HALF])
        kn_par = sb("idx_norm_params", [P, 4, HD])
        ada = sb("ada_rows", [12, BLK])
        cond_hi = sb("c_high", [P, KC], F32R)
        cond_lo = sb("c_low", [P, KC], F32R)
        stats = sb("norm_stats", [P, RB, 4, 6])
        agg = sb("norm_mean_var", [P, RB, 4, 2])
        rstd = sb("norm_rstd", [P, RB, 4])
        negmax = sb("neg_max", [P, 2, 8])
        expsum = sb("exp_sum", [P, 2, 8])
        recip = sb("recip", [P, 2, 8])
        top8 = sb("top8", [P, RB, 8])
        col = sb("c_col", [P, KC])
        pos_i = sb("pos_int", [P, RB], I32)
        pos = sb("pos", [P, RB])
        inv = sb("inv_freq", [P, ROPE_HALF])
        ang = sb("angle", [P, RB, ROPE_HALF])
        turn = sb("turns", [P, RB, ROPE_HALF])
        strict = sb("strict", [P, P])
        memory_scope = ctx.enter_context(ExitStack())
        mt_hi = memory_scope.enter_context(nc.sbuf_tensor("memt_high", [P, KC, SEQ], F32R))
        mt_lo = memory_scope.enter_context(nc.sbuf_tensor("memt_low", [P, KC, SEQ], F32R))

        psum = ctx.enter_context(nc.psum_tensor("psum", [P, 8, BLK], F32))
        GEMM, WIDE, TRB = (0, 1), (2, 4), (6, 7)

        c_raw = [plan.counter(f"w_raw_{n}") for n in range(RING)]
        c_hi = plan.counter("w_high_done")
        c_lo = plan.counter("w_low_done")
        c_tile = plan.counter("tile_used")
        c_gate = plan.counter("ff_gate_ready")
        c_mul = plan.counter("ff_h_ready")
        c_tr = plan.counter("ff_transposed")
        c_ht_hi = plan.counter("ff_ht_high")
        c_ht_lo = plan.counter("ff_ht_low")
        c_out = plan.counter("out_stored")

        def load(name, dst, src, wait=()):
            return op("pool", lambda e: e.dma_start(dst, src), wait, inc=plan.counter(f"ld_{name}"), by=16)

        def rows(vec):
            return vec.partition_broadcast(P)

        free = {("bank", n): [] for n in range(8)}

        def held(*keys):
            return [m for k in keys for m in free.get(k, [])]

        state = {"split": 0, "tile": 0, "trb": 0, "wide": 0, "slot": 0, "par": 0, "low_by": "dve", "low_last": "dve"}
        background = []

        def step_background():
            if background and next(background[0], background) is background:
                background.pop(0)

        def drain_background():
            while background:
                step_background()

        def pipelined(units):
            waiting, middle, oldest = list(units), None, None
            while waiting or middle or oldest:
                new = waiting.pop(0) if waiting else None
                for unit in (middle, new, oldest, middle):
                    if unit:
                        next(unit, None)
                oldest, middle = middle, new
                yield

        def abreast(*generators):
            left = list(generators)
            while left:
                left = [g for g in left if next(g, left) is not left]
                yield

        def preceded(act, unit):
            act()
            yield from unit

        def followed(unit, act):
            yield from unit
            act()

        def split_up_to(t):
            while state["split"] <= t:
                split_next()

        def split_next():
            t = state["split"]
            state["split"] += 1
            if t >= N_TILES:
                return
            s = t % RING
            c_raw[s].n += 16
            arrived = (c_raw[s], c_raw[s].n)
            used = [(c_tile, t - RING + 1)] if t >= RING else []
            hi = op("act", lambda e: e.activation(w_hi[:, s, :], raw[:, s, :], ACT.Copy),
                    [arrived] + used, inc=c_hi)
            last = [(c_lo, c_lo.n)] if state["low_by"] != state["low_last"] else []
            state["low_last"] = state["low_by"]
            op(state["low_by"], lambda e: e.tensor_tensor(w_lo[:, s, :], raw[:, s, :],
                                                          w_hi[:, s, :].bitcast(F32), ALU.subtract),
               [hi] + last, inc=c_lo)

        def products(e, dst, a_hi, a_lo, b_hi, b_lo, first, last):
            e.matmul(dst, a_hi, b_hi, start=first, stop=False)
            e.matmul(dst, a_hi, b_lo, start=False, stop=False)
            return e.matmul(dst, a_lo, b_hi, start=False, stop=last)

        def use_tile(tile, parts, then=None):
            order.append(tile)
            t = state["tile"]
            state["tile"] += 1
            split_up_to(t + 2)
            s = t % RING
            marks = []
            for n, (fn, waits, inc) in enumerate(parts):
                ready = [(c_lo, t + 1)] if n == 0 else []
                fin = n == len(parts) - 1
                marks.append(op("pe", lambda e, fn=fn: fn(e, w_hi[:, s, :], w_lo[:, s, :]),
                                ready + list(waits), inc=c_tile if fin else inc))
            if then:
                then(marks)
            step_background()
            return marks

        def two_tiles(tiles, part, ready, then=None):
            order.extend(tiles)
            t = state["tile"]
            state["tile"] += 2
            slots = [(t + n) % RING for n in range(2)]

            def queue(rb, half, inc):
                fn, waits = part(rb, half)
                hi, low = w_hi[:, slots[half], :], w_lo[:, slots[half], :]
                return op("pe", lambda e: fn(e, hi, low), ([(c_lo, t + half + 1)] if rb == 0 else []) + waits, inc=inc)
            split_up_to(t + 2)
            queue(0, 0, None)
            ready[1] = ready[1].make()
            first = queue(0, 1, None)
            queue(1, 0, c_tile)
            split_up_to(t + 3)
            second = queue(1, 1, c_tile)
            if then:
                then([first, second])
            step_background()
            return [first, second]

        def block_products(e, rb, half, bank, a_hi, a_lo, hi, lo):
            for k in range(4):
                kk = 4 * half + k
                left = [v[:, kk, rb * P:rb * P + P] if v.shape[-1] == SEQ else v[:, kk:kk + 1].broadcast_to([P, P])
                        for v in (a_hi, a_lo)]
                m = products(e, psum[:, bank, :], left[0], left[1], hi[:, k * BLK:k * BLK + BLK],
                             lo[:, k * BLK:k * BLK + BLK], kk == 0, kk == KC - 1)
            return m

        def gemm_block(weight, a_hi, a_lo, ready, banks, then=None):

            def part(rb, half):
                waits = (held(("bank", banks[rb])) if half == 0 else []) + [ready[rb][half]]
                return (lambda e, hi, lo: block_products(e, rb, half, banks[rb], a_hi, a_lo, hi, lo)), waits
            tiles = [weight + ("half", 4 * half) for half in range(2)]
            if isinstance(ready[1], Late):
                return two_tiles(tiles, part, ready, then)
            for half, tile in enumerate(tiles):
                marks = use_tile(tile, [part(rb, half) + (None,) for rb in range(RB)], then if half else None)
            return marks

        def turn_bank():
            state["trb"] += 1
            return TRB[state["trb"] % 2]

        def transpose_in(src, src_ready, chunks, dst_fn, width=P):
            b = turn_bank()
            pieces = [src(c) for c in chunks]

            def fn(e):
                for n, piece in enumerate(pieces):
                    m = e.transpose(psum[0:width, b, n * P:n * P + P], piece, ident[:, :])
                return m
            done = op("pe", fn, held(("bank", b)) + list(src_ready))
            marks = dst_fn(psum[0:width, b, 0:len(chunks) * P], done)
            free[("bank", b)] = marks
            return marks

        def to_stationary(src, ready, dst_hi, dst_lo, rb, hold=()):
            marks = []
            for g in range(2):
                def copy(bank, done):
                    v = bank.rearrange("p (c s) -> p c s", s=P)
                    h = dst_hi[:, 4 * g:4 * g + 4, rb * P:rb * P + P]
                    low = dst_lo[:, 4 * g:4 * g + 4, rb * P:rb * P + P]
                    a = op("act", lambda e: e.activation(h, v, ACT.Copy), [done] + list(hold))
                    return [op("dve", lambda e: e.tensor_tensor(low, v, h.bitcast(F32), ALU.subtract),
                               [a, done])]
                marks += transpose_in(lambda c: src[:, c * P:c * P + P], ready[g], range(4 * g, 4 * g + 4), copy)
            return marks

        def transpose_to(src, ready, chunks, dst, engine, scale=1.0, hold=()):
            def copy(bank, done):
                v = bank.rearrange("p (c s) -> p c s", s=P) if len(chunks) > 1 else bank
                if engine == "act":
                    return [op("act", lambda e: e.activation(dst, v, ACT.Copy, scale=scale), [done] + list(hold))]
                return [op("dve", lambda e: e.tensor_scalar(dst, v, scale, None, ALU.mult), [done] + list(hold))]
            return transpose_in(src, ready, chunks, copy)

        def power(rb, n, ready, at=0):
            v = rstd[:, rb, at:at + n]
            return op("pool", lambda e: e.tensor_tensor(v, v, half_neg[:, 0:n], ALU.pow), list(ready) + [k_hneg])

        def norm_aggregate(rb, n, ready, eps=LN_EPS, at=0):
            src = stats[:, rb, 2 * at:2 * at + n, :].rearrange("p a b -> p (a b)")
            m2 = op("dve", lambda e: e.bn_aggr(agg[:, rb, at, :], src), ready)
            m3 = op("dve", lambda e: e.tensor_scalar(rstd[:, rb, at:at + 1], agg[:, rb, at:at + 1, 1], eps, None,
                                                     ALU.add), [m2])
            return m2, power(rb, 1, [m3], at)

        def norm_stats(rb, pieces, ready, at=0):
            for n, piece in enumerate(pieces):
                m = op("dve", lambda e, n=n, piece=piece: e.bn_stats(stats[:, rb, 2 * at + n, :], piece), list(ready))
            return norm_aggregate(rb, len(pieces), [m], at=at)

        def norm_gain(rb, pieces, gains, ready, at=0):
            return [op("dve", lambda e, v=v, g=g: e.scalar_tensor_tensor(
                out=v, in0=v, scalar=agg[:, rb, at, 0:1], in1=g, op0=ALU.subtract, op1=ALU.mult), ready)
                for v, g in zip(pieces, gains)]

        def norm_bias(rb, pieces, biases, marks, ready, at=0):
            return [op("dve", lambda e, v=v, b=b, m=m: e.scalar_tensor_tensor(
                out=v, in0=v, scalar=rstd[:, rb, at:at + 1], in1=b, op0=ALU.mult, op1=ALU.add), [m, ready])
                for v, b, m in zip(pieces, biases, marks)]

        def halves(v):
            return [v[:, h * BLK:h * BLK + BLK] for h in range(2)]

        def load_norm(name, g, b):
            s = state["par"] % 2
            state["par"] += 1
            hold = held(("par", s))
            mg = load(name + "_g", par[:, s, 0:D], rows(g), hold)
            mb = load(name + "_b", par[:, s, D:2 * D], rows(b), hold)
            return s, [mg, mb]

        k_ident = op("act", lambda e: e.dma_start(ident[:, :], T["ident"]), inc=plan.counter("ld_ident"), by=16)
        c_x = [plan.counter(f"ld_x{rb}") for rb in range(RB)]
        for c in c_x:
            c.n += 16
        k_x = [(c, c.n) for c in c_x]
        k_pos = load("pos", pos_i[:, :], T["positions"])
        k_inv = load("inv", inv[:, :], rows(T["inv_freq"]))
        k_kn = [[load(f"idx_g{a}", kn_par[:, 2 * a, :], rows(T["idx_kn_g"][a])),
                 load(f"idx_b{a}", kn_par[:, 2 * a + 1, :], rows(T["idx_kn_b"][a]))] for a in range(KINDS.count("A"))]
        k_causal = load("causal", causal[:, :], T["causal"])
        masks_f = arena[:, 5120:5120 + 7 * P]
        k_masks = load("masks", masks_f, T["masks"])
        k_c = load("c", col[:, :], T["c_2"])
        k_ada = load("b_ada", ada[:, :], T["b_ada_2"].rearrange("l (c n) -> (l c) n", n=BLK))
        mem_rows = proj[:, :, 3 * BLK:5 * BLK]
        k_mem = [load(f"mem{rb}", mem_rows[:, rb, :], T["mem"][rb * P:rb * P + P, :]) for rb in range(RB)]
        mem_par, k_mem_par = load_norm("mem", T["mem_ln_g"], T["mem_ln_b"])
        op("dve", lambda e: e.memset(half_neg[:, :], -0.5))
        k_hneg = (plan.done["dve"], plan.done["dve"].n)

        xt = [to_stationary(x[:, rb, :], [[k_ident, k_x[rb]]] * 2, xt_hi, xt_lo, rb) for rb in range(RB)]
        split_up_to(1)

        two_pi = 2.0 * np.pi
        parts, rest = [], two_pi
        for bits in (8, 8, 8):
            exp = int(np.floor(np.log2(rest)))
            unit = 2.0 ** (exp - bits + 1)
            head = float(np.floor(rest / unit) * unit)
            parts.append(head)
            rest -= head
        parts.append(float(rest))
        MAGIC = 12582912.0
        PI = 3.1415925
        m = op("dve", lambda e: e.tensor_copy(pos[:, :], pos_i[:, :]), [k_pos])
        for rb in range(RB):
            ma = op("dve", lambda e, rb=rb: e.tensor_scalar(ang[:, rb, :], inv[:, :], pos[:, rb:rb + 1], None,
                                                            ALU.mult), [m, k_inv])
        m = op("dve", lambda e: e.tensor_scalar(turn[:, :, :], ang[:, :, :], float(1.0 / two_pi), MAGIC,
                                                ALU.mult, ALU.add), [ma])
        m = op("dve", lambda e: e.tensor_scalar(turn[:, :, :], turn[:, :, :], MAGIC, None, ALU.subtract), [m])
        for part in parts:
            m = op("dve", lambda e, part=part: e.scalar_tensor_tensor(
                out=ang[:, :, :], in0=turn[:, :, :], scalar=-part, in1=ang[:, :, :], op0=ALU.mult,
                op1=ALU.add), [m])
        m = op("dve", lambda e: e.tensor_scalar(rope_c[:, :, :], ang[:, :, :], float(np.pi / 2), None, ALU.add), [m])
        m = op("dve", lambda e: e.tensor_scalar(turn[:, :, :], rope_c[:, :, :], PI, -two_pi, ALU.is_gt, ALU.mult), [m])
        m = op("dve", lambda e: e.tensor_tensor(rope_c[:, :, :], rope_c[:, :, :], turn[:, :, :], ALU.add), [m])
        m = op("dve", lambda e: e.tensor_scalar(rope_c[:, :, :], rope_c[:, :, :], PI, -PI, ALU.min, ALU.max), [m])
        m = op("dve", lambda e: e.tensor_scalar(ang[:, :, :], ang[:, :, :], PI, -PI, ALU.min, ALU.max), [m])
        k_cos = op("act", lambda e: e.activation(rope_c[:, :, :], rope_c[:, :, :], ACT.Sin), [m])
        k_rope = [k_cos, op("act", lambda e: e.activation(rope_s[:, :, :], ang[:, :, :], ACT.Sin), [m])]

        k_maskb = op("dve", lambda e: e.tensor_copy(masks[:, :], masks_f), [k_masks])
        free["heads"] = [k_maskb]
        m = op("act", lambda e: e.activation(col[:, :], col[:, :], ACT.Silu), [k_c])
        m = op("act", lambda e: e.activation(cond_hi[:, :], col[:, :], ACT.Copy), [m])
        k_col = op("dve", lambda e: e.tensor_tensor(cond_lo[:, :], col[:, :], cond_hi[:, :].bitcast(F32), ALU.subtract), [m])

        mt = []

        def memory_work():
            for rb in range(RB):
                v = halves(mem_rows[:, rb, :])
                am, rm = norm_stats(rb, v, [k_mem[rb]], at=1)
                r = norm_gain(rb, v, halves(par[:, mem_par, 0:D]), [am] + k_mem_par, at=1)
                yield
                r = norm_bias(rb, v, halves(par[:, mem_par, D:2 * D]), r, rm, at=1)
                free[("par", mem_par)] = [r[1]]
                mt.append(to_stationary(mem_rows[:, rb, :], [[r[0]], [r[1]]], mt_hi, mt_lo, rb))
                free["values"] = mt[-1]
                yield

        def evacuate(banks, marks, dst, wait=(), func=ACT.Copy):
            done = []
            for rb in range(RB):
                v = psum[:, banks[rb], :]
                w = [marks[rb]] + list(wait)
                if rb == 0 or func != ACT.Copy:
                    d = op("act", lambda e, rb=rb, v=v: e.activation(dst(rb), v, func), w)
                else:
                    d = op("dve", lambda e, rb=rb, v=v: e.tensor_copy(dst(rb), v), w)
                free[("bank", banks[rb])] = [d]
                done.append(d)
            return done

        def rotary(rb, v, heads, half, cos, sin, tmp, ready):
            n = heads * half
            t = [tmp[k].rearrange("p (h d) -> p h d", d=half) for k in range(4)]
            c = cos.unsqueeze(1).broadcast_to([P, heads, half])
            s = sin.unsqueeze(1).broadcast_to([P, heads, half])
            x1, x2 = v[:, :, 0:half], v[:, :, half:2 * half]
            w = list(ready) + held("rope_tmp")
            for k, (a, b) in enumerate(((x1, c), (x2, s), (x2, c), (x1, s))):
                m = op("dve", lambda e, k=k, a=a, b=b: e.tensor_tensor(t[k], a, b, ALU.mult), w)
            op("dve", lambda e: e.tensor_tensor(x1, t[0], t[1], ALU.subtract), [m])
            m = op("dve", lambda e: e.tensor_tensor(x2, t[2], t[3], ALU.add), [m])
            free["rope_tmp"] = [m]
            return m

        def rope_heads(rb, cols, heads, ready):
            v = cols.rearrange("p (h d) -> p h d", d=HD)
            tmp = [rope_t[:, k, 0:heads * ROPE_HALF] for k in range(4)]
            return rotary(rb, v, heads, ROPE_HALF, rope_c[:, rb, :], rope_s[:, rb, :], tmp, ready)

        def head_cols(t, h, s0, n):
            p0 = HD * (h % 2)
            return t[p0:p0 + HD, h // 2, s0:s0 + n]

        def wide_pair():
            b = WIDE[state["wide"] % 2]
            state["wide"] += 1
            return b

        def score_pieces(b, n_pieces, nk, joint):
            if joint:
                flat = psum[:, b:b + 2, :].rearrange("p b c -> p (b c)")
                return [(n * nk // BLK, flat[:, n * nk:n * nk + nk]) for n in range(n_pieces)]
            return [(n % 2, psum[:, b + n % 2, n // 2 * nk:n // 2 * nk + nk]) for n in range(n_pieces)]

        def accumulate(e, pieces, products_of, nk):
            banks = [pieces[n][0] for n, *_ in products_of]
            for i, (n, left, right, cols) in enumerate(products_of):
                dst = pieces[n][1] if cols is None else pieces[n][1][:, nk - cols:nk]
                m = e.matmul(dst, left, right, start=banks[i] not in banks[:i], stop=banks[i] not in banks[i + 1:])
            return m

        def attention_unit(segments, joint, values, dst, ready, finished):
            nk = segments[0][3]
            b = wide_pair()
            slot = state["slot"] % 2
            state["slot"] += 1
            pr, pt = prob[slot], probt[slot]
            nseg = len(segments)
            pieces_l = score_pieces(b, nseg, nk, joint)

            def scores(e):
                work_list = [(n, q, k, None) for n, (q, k, _, _) in enumerate(segments)]
                work_list += [(n, identb, bias, bias.shape[1]) for n, (_, _, bias, _) in enumerate(segments)
                              if bias is not None]
                return accumulate(e, pieces_l, work_list, nk)
            s = op("pe", scores, list(ready()) + held(("bank", b), ("bank", b + 1)))
            nmax = 1 if joint else nseg
            if joint:
                view = psum[:, b:b + 2, :].rearrange("p b c -> p (b c)")[:, 0:nseg * nk]
                nm_out = negmax[:, slot, 0:1]
            else:
                view = psum[:, b:b + 2, 0:nseg // 2 * nk].rearrange("p b (h k) -> p b h k", k=nk)
                nm_out = negmax[:, slot, 0:nseg].rearrange("p (h b) -> p b h", b=2)
            mx = op("dve", lambda e: e.tensor_reduce(nm_out, view, AX.X, ALU.max, negate=True),
                    [s] + held(("negmax", slot)))
            for n in range(nmax):
                src = view if joint else pieces_l[n][1]
                dst_p = pr[:, 0:nseg * nk] if joint else pr[:, n * nk:n * nk + nk]
                ex = op("act", lambda e, n=n, src=src, dst_p=dst_p: e.activation(
                    dst_p, src, ACT.Exp, bias=negmax[:, slot, n:n + 1], accum_out=expsum[:, slot, n:n + 1]),
                    [mx] + held(("prob", slot), ("expsum", slot)))
            free[("negmax", slot)] = [ex]
            free[("bank", b)] = free[("bank", b + 1)] = [ex]
            yield
            rc = op("dve", lambda e: e.reciprocal(recip[:, slot, 0:nmax], expsum[:, slot, 0:nmax]),
                    [ex] + held(("recip", slot)))
            free[("expsum", slot)] = [rc]
            pready = ex
            if joint:
                for n in range(1, nseg):
                    pready = op("dve", lambda e, n=n: e.tensor_tensor(
                        pr[:, 0:nk], pr[:, 0:nk], pr[:, n * nk:n * nk + nk], ALU.add), [pready])
            yield
            pieces = [(n, kb) for n in range(nmax) for kb in range(nk // P)]
            turned = []
            for g in range(0, len(pieces), 4):
                some = pieces[g:g + 4]
                to = pt[:, g * P:(g + len(some)) * P]
                turned += transpose_to(lambda i: pr[:, i[0] * nk + i[1] * P:i[0] * nk + i[1] * P + P], [pready], some,
                                       to.rearrange("p (c s) -> p c s", s=P) if len(some) > 1 else to,
                                       "act" if (g // 4) % 2 else "dve", hold=held(("probt", slot), "idx"))
            free[("prob", slot)] = list(turned)
            yield
            vals = [[values(n, kb) for kb in range(nk // P)] for n in range(nmax)]
            w = vals[0][0][0].shape[1]
            to = turn_bank()

            def weighted(e):
                for n in range(nmax):
                    for kb in range(nk // P):
                        c = n * (nk // P) + kb
                        m = e.matmul(psum[:, to, n * w:n * w + w], pt[:, c * P:c * P + P], vals[n][kb][0],
                                     start=kb == 0, stop=kb == nk // P - 1)
                return m
            wv = op("pe", weighted, turned + held(("bank", to)) + [m for v in vals for _, m in v])
            free[("probt", slot)] = [wv]
            nm = op("dve", lambda e: e.tensor_tensor(
                dst.rearrange("p (h d) -> p h d", d=w), psum[:, to, 0:nmax * w].rearrange("p (h d) -> p h d", d=w),
                recip[:, slot, 0:nmax].unsqueeze(2).broadcast_to([P, nmax, w]), ALU.mult), [wv, rc])
            free[("bank", to)] = [nm]
            free[("recip", slot)] = [nm]
            finished.append(nm)

        def indexer(a, xt_ready, chosen):
            marks = gemm_block(("w_in_a", a, 3 * MIX), xt_hi, xt_lo, xt_ready, GEMM)
            idx_free = held(("probt", 0), ("probt", 1))
            qi = evacuate(GEMM, marks, lambda rb: idx[:, rb, 0:IDX_W], idx_free)

            def part(rb):
                def fn(e, hi, lo):
                    w = IDX_H + HD
                    for k in range(KC):
                        m = products(e, psum[:, GEMM[rb], 0:w], xt_hi[:, k, rb * P:rb * P + P],
                                     xt_lo[:, k, rb * P:rb * P + P], hi[:, k * w:k * w + w],
                                     lo[:, k * w:k * w + w], k == 0, k == KC - 1)
                    return m
                return (fn, held(("bank", GEMM[rb])), None)
            marks = use_tile(("w_in_a", a, None, "narrow", 0), [part(rb) for rb in range(RB)])

            k_w, ki_ready = [], []
            for rb in range(RB):
                bank = psum[:, GEMM[rb], 0:IDX_H + HD]
                k_w.append(op("dve", lambda e, rb=rb, bank=bank: e.tensor_scalar(
                    idx[:, rb, IDX_W:IDX_W + IDX_H], bank[:, 0:IDX_H], float((IDX_H * HD) ** -0.5), None, ALU.mult),
                    [marks[rb]] + idx_free))
                ki_ready.append(op("dve", lambda e, rb=rb, bank=bank: e.tensor_copy(
                    idx[:, rb, IDX_W + IDX_H:IDX_W + IDX_H + HD], bank[:, IDX_H:IDX_H + HD]), [marks[rb]]))
                free[("bank", GEMM[rb])] = [ki_ready[rb]]

            def work_on():
                tr, ms = [], []
                for rb in range(RB):
                    ki = idx[:, rb, IDX_W + IDX_H:IDX_W + IDX_H + HD]
                    ms.append(norm_stats(rb, [ki], [ki_ready[rb]]))
                q = [rope_heads(rb, idx[:, rb, 0:IDX_W], IDX_H, [qi[rb]] + k_rope) for rb in range(RB)]
                yield
                for rb in range(RB):
                    tr += transpose_to(lambda c: idx[:, rb, c * P:c * P + P], [q[rb]], range(4),
                                       qit[:, :, rb * P:rb * P + P], "act", hold=held("qit"))
                both = []
                for rb in range(RB):
                    ki = idx[:, rb, IDX_W + IDX_H:IDX_W + IDX_H + HD]
                    ki2 = idx[:, rb, IDX_W + IDX_H + HD:IDX_W + IDX_H + 2 * HD]
                    am, rm = ms[rb]
                    r = norm_gain(rb, [ki], [kn_par[:, 2 * a, :]], [am] + k_kn[a])
                    r = norm_bias(rb, [ki], [kn_par[:, 2 * a + 1, :]], r, rm)
                    r = rope_heads(rb, ki, 1, r + k_rope)
                    both.append(op("dve", lambda e, ki=ki, ki2=ki2: e.tensor_copy(ki2, ki), [r]))
                yield
                for rb in range(RB):
                    tr += transpose_to(lambda c: idx[:, rb, IDX_W + IDX_H:IDX_W + IDX_H + 2 * HD], [both[rb]], [0],
                                       kit[:, rb * P:rb * P + P], "act", hold=held("qit"))
                ms = [k_causal, k_causal]
                for rb in range(RB):
                    nk = (rb + 1) * P
                    per = 1024 // nk
                    keep = causal[:, (1 - rb) * P:(1 - rb) * P + nk]
                    acc = keep
                    for g in range(0, IDX_H, per):
                        b = wide_pair()
                        dots = psum[:, b:b + 2, :]
                        pieces = score_pieces(b, per, nk, False)
                        slot = state["slot"] % 2
                        state["slot"] += 1

                        def fn(e, g=g, pieces=pieces, per=per, nk=nk, rb=rb):
                            return accumulate(e, pieces, [
                                (n, head_cols(qit, g + n, rb * P, P), kit[HD * (n % 2):HD * (n % 2) + HD, 0:nk], None)
                                for n in range(per)], nk)
                        m = op("pe", fn, tr + held(("bank", b), ("bank", b + 1)))
                        r = op("act", lambda e, dots=dots, slot=slot: e.activation(
                            prob[slot].rearrange("p (b c) -> p b c", b=2), dots, ACT.Relu), [m] + held(("prob", slot)))
                        free[("bank", b)] = free[("bank", b + 1)] = [r]
                        for n in range(per):
                            h, at = g + n, n % 2 * BLK + n // 2 * nk
                            ms[rb] = op("dve", lambda e, at=at, h=h, slot=slot, acc=acc, nk=nk, rb=rb: e.scalar_tensor_tensor(
                                out=score[:, rb, 0:nk], in0=prob[slot][:, at:at + nk],
                                scalar=idx[:, rb, IDX_W + h:IDX_W + h + 1], in1=acc, op0=ALU.mult, op1=ALU.add),
                                [ms[rb], r, k_w[rb]])
                            acc = score[:, rb, 0:nk]
                        free[("prob", slot)] = [ms[rb]]
                    yield
                v = [score[:, rb, 0:(rb + 1) * P] for rb in range(RB)]
                for n in range(TOPK // 8):
                    for rb in range(RB):
                        ms[rb] = op("dve", lambda e, rb=rb: e.max(top8[:, rb, :], v[rb]), [ms[rb]])
                    for rb in range(RB):
                        ms[rb] = op("dve", lambda e, rb=rb: e.match_replace(v[rb], top8[:, rb, :], v[rb], TAKEN), [ms[rb]])
                    if n % 3 == 2:
                        yield
                for rb in range(RB):
                    nk = (rb + 1) * P
                    m = op("dve", lambda e, rb=rb: e.tensor_scalar(v[rb], v[rb], -2.0e38, BIG, ALU.is_ge, ALU.mult), [ms[rb]])
                    chosen[rb] = op("dve", lambda e, rb=rb, nk=nk: e.tensor_tensor(
                        select[:, rb, 0:nk], v[rb], causal[:, (1 - rb) * P:(1 - rb) * P + nk], ALU.add), [m] + held("select"))
                free["idx"] = free["qit"] = [chosen[1]]
            background.append(work_on())

        def feed_forward(layer, xt_ready):
            acc = [[2 + 2 * rb + h for h in range(2)] for rb in range(RB)]

            def up(step, ready, banks_free):
                def part(rb, half):
                    w = (list(banks_free[rb]) if half == 0 else []) + ([ready[rb][half]] if ready else [])
                    return (lambda e, hi, lo: block_products(e, rb, half, GEMM[rb], xt_hi, xt_lo, hi, lo)), w
                tiles = [("w_gate_up", layer, step, "up", 4 * half) for half in range(2)]
                if ready and isinstance(ready[1], Late):
                    done = two_tiles(tiles, part, ready)
                    return [done[0], done[1]]
                for half, tile in enumerate(tiles):
                    marks = use_tile(tile, [part(rb, half) + (c_gate if half else None,) for rb in range(RB)])
                return marks

            def gate(marks, muls, tr):
                done = []
                for rb in range(RB):
                    bank = psum[:, GEMM[rb], :]
                    s = op("act", lambda e, rb=rb, bank=bank: e.activation(ff_silu[:, rb, :], bank[:, 0:FF_STEP], ACT.Silu),
                           [marks[rb], muls[rb]] if muls else [marks[rb]] + held("proj"))
                    done.append(op("dve", lambda e, rb=rb, bank=bank: e.tensor_tensor(
                        ff_h[:, rb, :], ff_silu[:, rb, :], bank[:, FF_STEP:BLK], ALU.mult),
                        [s] + ([tr] if tr else []), inc=c_mul))
                return done

            def turn_h(muls, lo, used):
                def fn(e):
                    for c in range(2):
                        for rb in range(RB):
                            m = e.transpose(psum[:, 6, (2 * c + rb) * P:(2 * c + rb + 1) * P],
                                            ff_h[:, rb, c * P:c * P + P], ident[:, :])
                    return m
                tr = op("pe", fn, list(muls) + ([lo] if lo else held(("bank", 6))), inc=c_tr)
                v = psum[:, 6, :].rearrange("p (c s) -> p c s", s=SEQ)
                h = op("act", lambda e: e.activation(ht_hi[:, :, :], v, ACT.Copy), [tr] + used, inc=c_ht_hi)
                low = op("dve", lambda e: e.tensor_tensor(ht_lo[:, :, :], v, ht_hi[:, :, :].bitcast(F32),
                                                          ALU.subtract), [h], inc=c_ht_lo)
                return tr, low

            def down(step, low, first, last):
                def part(rb):
                    def fn(e, hi, lo):
                        for c in range(2):
                            for h in range(2):
                                w = c * D + h * BLK
                                m = products(e, psum[:, acc[rb][h], :], ht_hi[:, c, rb * P:rb * P + P],
                                             ht_lo[:, c, rb * P:rb * P + P], hi[:, w:w + BLK], lo[:, w:w + BLK],
                                             first and c == 0, last and c == 1)
                        return m
                    w = [low] if rb == 0 else []
                    if first:
                        w += held(("bank", acc[rb][0]), ("bank", acc[rb][1]))
                    return (fn, w, None)
                return use_tile(("w_down", layer, step, "down", 0), [part(rb) for rb in range(RB)])

            marks = up(0, xt_ready, [held(("bank", GEMM[rb])) for rb in range(RB)])
            muls = gate(marks, None, None)
            for _ in ada_block(WIDE[1]):
                pass
            tr, low = turn_h(muls, None, [])
            marks = up(1, None, [[m] for m in muls])
            muls = gate(marks, muls, tr)
            if layer == len(KINDS) - 1:
                mods.extend(modulation(0, range(4), load_gain(0)))
            used = down(0, low, True, False)
            tr, low = turn_h(muls, low, [used[-1]])
            plan.begin(FF_STEPS - 2)
            t_in = state["tile"]
            marks = up(2, None, [[m] for m in muls])
            muls = gate(marks, muls, tr)
            used = down(1, low, False, False)
            tr, low = turn_h(muls, low, [used[-1]])
            loop = plan.end()
            more = (FF_STEPS - 3) * 3
            assert state["tile"] - t_in == 3
            for step in range(3, FF_STEPS):
                order.extend([("w_gate_up", layer, step, "up", k0) for k0 in (0, 4)]
                             + [("w_down", layer, step - 1, "down", 0)])
            state["tile"] += more
            state["split"] += more
            muls = [plan.last_trip(loop, m) for m in muls]
            low = plan.last_trip(loop, low)
            for rb in range(RB):
                free[("bank", GEMM[rb])] = [muls[rb]]
            free[("bank", 6)] = [low]
            free["proj"] = [muls[1]]
            marks = down(FF_STEPS - 1, low, False, True)
            return marks, acc

        def add_residual(rb, h, mark, bank):
            v = halves(x[:, rb, :])[h]
            m = op("dve", lambda e: e.scalar_tensor_tensor(
                out=v, in0=v, scalar=ALPHA, in1=psum[:, bank, :], op0=ALU.mult, op1=ALU.add), [mark])
            free[("bank", bank)] = [m]
            return op("dve", lambda e: e.bn_stats(stats[:, rb, h, :], v), [m])

        def residual_norm(left, s, par_ready, fill=None, stationary=True):
            gains, biases = halves(par[:, s, 0:D]), halves(par[:, s, D:2 * D])
            v = [halves(x[:, rb, :]) for rb in range(RB)]

            def mean_of(rb):
                m = [add_residual(rb, h, mark, bank) for h, mark, bank in left[rb]][-1]
                return norm_aggregate(rb, 2, [m])

            def fill_on():
                if fill:
                    state["low_by"] = "pool"
                    next(fill, None)
                    state["low_by"] = "dve"
            used = [(c_tile, state["tile"])]
            am, rm = mean_of(0)
            g = norm_gain(0, v[0], gains, [am] + par_ready)
            fill_on()
            am1, rm1 = mean_of(1)
            b = norm_bias(0, v[0], biases, g, rm)
            fill_on()
            ready = [b]
            if stationary:
                ready = [to_stationary(x[:, 0, :], [[b[0]], [b[1]]], xt_hi, xt_lo, 0, hold=used)]
            g = norm_gain(1, v[1], gains, [am1] + par_ready)
            b = norm_bias(1, v[1], biases, g, rm1)
            free[("par", s)] = [b[1]]
            fill_on()
            if not stationary:
                return [ready[0], b]
            return ready + [Late(lambda: to_stationary(x[:, 1, :], [[b[0]], [b[1]]], xt_hi, xt_lo, 1, hold=used))]

        def out_product(name, layer, ready, after_first=None):
            banks = [[GEMM[rb], WIDE[0] + rb] for rb in range(RB)]
            marks = [[None, None], [None, None]]
            for h in range(2):
                done = gemm_block((name, layer, h * BLK), xt_hi, xt_lo, ready, [banks[rb][h] for rb in range(RB)])
                for rb in range(RB):
                    marks[rb][h] = done[rb]
                if h == 0 and after_first:
                    after_first([(done[rb], banks[rb][0]) for rb in range(RB)])
            return marks, banks

        ada_left = [(layer, c) for layer in range(DEPTH_2) for c in range(6)]

        def ada_block(bank=0):
            layer, c = ada_left.pop(0)
            row = 6 * layer + c
            for half in range(2):
                waits = held(("bank", bank)) + [k_col] if half == 0 else []
                marks = use_tile(("w_ada_2", layer, c * BLK, "half", 4 * half), [
                    (lambda e, hi, lo, half=half: block_products(e, 0, half, bank, cond_hi, cond_lo, hi, lo), waits, None)])
                yield
            m = op("dve", lambda e: e.scalar_tensor_tensor(
                out=ada[:, :], in0=psum[0:12, bank, :], scalar=ident[0:12, row:row + 1], in1=ada[:, :],
                op0=ALU.mult, op1=ALU.add), [marks[0]] + held("ada") + [k_ada])
            free["ada"] = free[("bank", bank)] = [m]

        mod = par[:, :, :].rearrange("p s c -> p (s c)")
        shift, gain = mod[:, 2 * D:3 * D], mod[:, 3 * D:4 * D]

        def load_gain(layer):
            return load(f"g2_{layer}", gain, rows(T["norm_g_2"][layer]), held("mods", ("par", 1)))

        def modulation(layer, parts, k_g=None):
            marks = []
            hold = {0: held("mods", ("par", 1)), 4: held("gate", ("par", 0))}[parts[0]]
            for c in parts:
                bank, row = WIDE[1] + c % 2, 6 * layer + c
                m = op("pe", lambda e, bank=bank, row=row: e.matmul(
                    psum[:, bank, :], ident[0:12, row:row + 1].broadcast_to([12, P]), ada[:, :], start=True, stop=True),
                    held(("bank", bank), "ada"))
                at = {0: 2 * D, 2: 3 * D, 4: 0}[c // 2 * 2] + c % 2 * BLK
                v, b = mod[:, at:at + BLK], psum[:, bank, :]
                if c in (2, 3):
                    m = op("dve", lambda e, v=v, b=b: e.scalar_tensor_tensor(
                        out=v, in0=b, scalar=1.0, in1=v, op0=ALU.add, op1=ALU.mult), [m, k_g])
                else:
                    m = op("act", lambda e, v=v, b=b: e.activation(v, b, ACT.Copy), [m] + hold)
                free[("bank", bank)] = [m]
                marks.append(m)
            return marks

        memory, mods = {}, []

        def memory_products(layer):
            for half in range(2):
                def part(rb, half=half):
                    waits = (held(("bank", GEMM[rb])) if half == 0 else []) + [mt[rb][half]]
                    return (lambda e, hi, lo: block_products(e, rb, half, GEMM[rb], mt_hi, mt_lo, hi, lo)), waits, None
                marks = use_tile(("w_mem_kv", layer, 0, "half", 4 * half), [part(rb) for rb in range(RB)])
                yield
            memory["kv"] = evacuate(GEMM, marks, lambda rb: mkv[:, rb, :], held("mkv"))

        def turn_memory():
            mk = memory["kv"]
            memory["turned"] = []
            for rb in range(RB):
                memory["turned"] += transpose_to(lambda n: mkv[:, rb, n * P:n * P + P], [mk[rb]], range(2),
                                                 mkt[:, :, rb * P:rb * P + P], "dve", 1.0, held("mkv"))

        a = 0
        for layer, kind in enumerate(KINDS):
            ln1, k_ln1 = load_norm(f"ln1_{layer}", T["ln1_g"][layer], T["ln1_b"][layer])
            chosen = [None, None]
            if kind == "A":
                w_in = ("w_in_a", a)
                indexer(a, xt, chosen)
                a += 1
            else:
                w_in = ("w_in_b" if kind == "B" else "w_in_c", 0)
            if layer == 0:
                background[0] = abreast(memory_work(), background[0])
            state["low_by"] = "pool"
            blocks = {}

            def project(c, hold):
                def then(marks):
                    blocks[c] = evacuate(GEMM, marks, lambda rb: proj[:, rb, c * BLK:c * BLK + BLK], hold)
                gemm_block(w_in + (("proj", c),), xt_hi, xt_lo, xt, GEMM, then)

            def turn_heads(of_q):
                c0, dst, scale = (0, qt, HD ** -0.5) if of_q else (MIX, kt, 1.0)
                from_blocks = (0, 1) if of_q else (1, 2)

                def turn(rb, r):
                    for n0, n1 in ((0, 4), (4, 6)):
                        turned.extend(transpose_to(
                            lambda n: proj[:, rb, c0 + n * P:c0 + n * P + P], [r], range(n0, n1),
                            dst[:, n0:n1, rb * P:rb * P + P], "act" if n0 == 0 else "dve", scale, held("heads")))
                rotated = [rope_heads(rb, proj[:, rb, c0:c0 + MIX], NH, [blocks[c][rb] for c in from_blocks] + k_rope)
                           for rb in range(RB)]
                yield
                turn(0, rotated[0])
                yield
                turn(1, rotated[1])
            turned = []

            for c in range(3):
                project(c, held("proj"))
                if c == 0 and layer:
                    turn_memory()
                if c > 0:
                    background[:] = [abreast(*background, turn_heads(c == 1))]
            if layer == 0:
                for _ in memory_products(layer):
                    pass
                turn_memory()
            outs = [[], []]

            def own_units(rb):
                nk = (rb + 1) * P
                if kind == "B":
                    for h in range(DIL_H):
                        seg = [(head_cols(qt, g * DIL_H + h, rb * P, P), head_cols(kt, g * DIL_H + h, 0, nk),
                                m_pair[g] if rb else m_pair[g][:, P:2 * P], nk) for g in range(DIL)]
                        c0 = 2 * MIX + h * DIL_V

                        def values(n, kb, c0=c0):
                            return proj[:, kb, c0:c0 + DIL_V], blocks[(c0 + DIL_V - 1) // BLK][kb]
                        yield attention_unit(seg, True, values, mixed[:, rb, h * DIL_V:h * DIL_V + DIL_V],
                                             lambda: turned, outs[rb])
                    return
                per = 4 if rb else 6
                for h0 in range(0, NH, per):
                    bias = select[:, rb, 0:nk] if kind == "A" else m_causal
                    seg = [(head_cols(qt, h, rb * P, P), head_cols(kt, h, 0, nk), bias, nk) for h in range(h0, h0 + per)]

                    def values(n, kb, h0=h0):
                        c0 = 2 * MIX + (h0 + n) * HD
                        return proj[:, kb, c0:c0 + HD], blocks[c0 // BLK][kb]
                    yield attention_unit(seg, False, values, mixed[:, rb, h0 * HD:(h0 + per) * HD],
                                         lambda: turned + [m for m in (chosen[rb], k_maskb) if m], outs[rb])

            def memory_unit(rb):
                seg = [(head_cols(qmt, h, rb * P, P), head_cols(mkt, h, 0, SEQ), None, SEQ) for h in range(MEM_H)]
                return attention_unit(seg, False, lambda n, kb: (mkv[:, kb, MEMW + n * HD:MEMW + n * HD + HD],
                                                                 memory["kv"][kb]),
                                      mixed[:, rb, MIX:MIX + MEMW], lambda: memory["turned"] + qm_turned + turned, outs[rb])

            project(4, held("values"))
            drain_background()
            xt_used = (c_tile, state["tile"] + 2)
            qm_turned = []

            def turn_qm():
                for rb in range(RB):
                    qm_turned.extend(transpose_to(
                        lambda n: proj[:, rb, 3 * MIX + n * P:3 * MIX + n * P + P], [blocks[4][rb]], range(2),
                        qmt[:, :, rb * P:rb * P + P], "act", HD ** -0.5, held("heads")))
            mx = [[], Late(lambda: turn_mixed(1))]

            def turn_mixed(rb):
                if rb == 1:
                    drain_background()
                return to_stationary(mixed[:, rb, :], [[outs[rb][-1]]] * 2, xt_hi, xt_lo, rb, hold=[xt_used])
            units = [memory_unit(0)] + list(own_units(0)) if kind == "A" else list(own_units(0)) + [memory_unit(0)]
            units[-1] = followed(units[-1], lambda: mx[0].extend(turn_mixed(0)))
            units[0] = preceded(turn_qm, units[0])
            background.append(pipelined(units + [memory_unit(1)] + list(own_units(1))))
            project(3, held("values"))
            last = layer == len(KINDS) - 1
            for _ in ada_block(GEMM[0]):
                pass
            state["low_by"] = "dve"
            while not mx[0]:
                step_background()
            marks, banks = out_product("w_out", layer, mx, lambda of: [add_residual(rb, 0, *of[rb]) for rb in range(RB)])
            free["heads"] = free["select"] = free["mkv"] = free["values"] = [outs[1][-1]]
            free["proj"] = mx[0] + mx[1]
            ln2, k_ln2 = load_norm(f"ln2_{layer}", T["ln2_g"][layer], T["ln2_b"][layer])
            xt = residual_norm([[(1, marks[rb][1], banks[rb][1])] for rb in range(RB)], ln1, k_ln1, ada_block(WIDE[1]))
            if layer == len(KINDS) - 1:
                decay = kv[:, 0:1536].rearrange("p (h c) -> p h c", h=RET_H)
                memory_scope.close()
                rt = sb("heads_t2", [P, 16, SEQ])
                k_decay = load("decay", decay, T["decay"], held("mkv"))
                ret_cs = score
                k_ret = load("ret_cs", ret_cs[:, :, 0:P], T["ret_cos_sin"].rearrange("(r p) c -> p r c", p=P), held("select"))
                tri = causal
                k_tri = load("tri", tri[:, :], T["tri"], held("select"))
                k_strict = load("strict", strict[:, :], T["strict"])
                strict_b_f = rt[:, 0, 0:P]
                k_sbf = load("strict_bias", strict_b_f, T["strict_bias"], held("mkv"))
                strict_b = masks[:, P:2 * P]
            marks, banks = feed_forward(layer, xt)
            xt = residual_norm([[(h, marks[rb], banks[rb][h]) for h in range(2)] for rb in range(RB)], ln2, k_ln2,
                               None if last else memory_products(layer + 1), not last)

        gate_row = mod[:, 0:D]
        k_sb = op("dve", lambda e: e.tensor_copy(strict_b, strict_b_f), [k_sbf] + held("select"))
        free["rt"] = [k_sb]
        xready = list(xt)

        def rms(rb, ready, scratch):
            q = op("act", lambda e: e.activation(scratch, x[:, rb, :], ACT.Square, accum_out=expsum[:, rb, 0:1]),
                   list(ready) + held(("expsum", 0), ("expsum", 1), "rows2"))
            m = op("dve", lambda e: e.tensor_scalar(rstd[:, rb, 0:1], expsum[:, rb, 0:1], 1.0 / D, EPS_2,
                                                    ALU.mult, ALU.add), [q])
            free[("expsum", rb)] = [m]
            return power(rb, 1, [m])

        for layer in range(DEPTH_2):
            rs = [rms(rb, xready[rb], rows2[:, rb, :]) for rb in range(RB)]
            if layer:
                mods = modulation(layer, range(4), k_g)
            gates = modulation(layer, (4, 5))

            def modulated(rb):
                done = []
                for h in range(2):
                    v, cols = rows2[:, rb, h * BLK:h * BLK + BLK], slice(h * BLK, h * BLK + BLK)
                    m = op("dve", lambda e, v=v, cols=cols: e.scalar_tensor_tensor(
                        out=v, in0=x[:, rb, cols], scalar=rstd[:, rb, 0:1], in1=gain[:, cols], op0=ALU.mult,
                        op1=ALU.mult), [mods[2 + h], rs[rb]])
                    done.append([op("dve", lambda e, v=v, cols=cols: e.tensor_tensor(v, v, shift[:, cols], ALU.add),
                                    [m, mods[h]])])
                return done
            used = [(c_tile, state["tile"])]
            ready = [to_stationary(rows2[:, 0, :], modulated(0), xt_hi, xt_lo, 0, hold=used)]
            done = modulated(1)
            free["mods"] = done[0] + done[1]
            ready.append(Late(lambda: to_stationary(rows2[:, 1, :], done, xt_hi, xt_lo, 1, hold=used)))
            blocks = {}

            def project(c):
                def then(marks):
                    blocks[c] = evacuate(GEMM, marks, lambda rb: proj2[:, rb, c * BLK:c * BLK + BLK],
                                         held("proj", "heads", "values"), ACT.Silu if c % 4 == 3 else ACT.Copy)
                gemm_block(("w_in_2", layer, c * BLK), xt_hi, xt_lo, ready, GEMM, then)

            def turn_block(c, rbs, dst, scale, engine, marks=None):
                return [m for rb in rbs for m in transpose_to(
                    lambda n: proj2[:, rb, c * BLK + n * P:c * BLK + n * P + P], marks or [blocks[c][rb]], range(4),
                    dst[:, :, rb * P:rb * P + P], engine, scale, held("rt"))]
            sqt, skt, rqt, rkt = [rt[:, 4 * n:4 * n + 4, :] for n in range(4)]
            sb_turned, ret_turned, y_sb, y_ret = [], [], [], []
            sb_weights = [tmp2[:, 768 * n:768 * n + 768] for n in range(2)]
            sb_bufs = [arena[:, 8192 + 768 * n:8192 + 768 * n + 768] for n in range(2)]

            def turn_retention(c, dst, engine):
                tmp = [tmp2[:, k * 512:k * 512 + 256] for k in range(4)]
                rotated = []
                for rb in range(RB):
                    v = proj2[:, rb, c * BLK:c * BLK + BLK].rearrange("p (h d) -> p h d", d=RET_D)
                    rotated.append(rotary(rb, v, RET_H, RET_D // 2, ret_cs[:, rb, 0:64], ret_cs[:, rb, 64:128], tmp,
                                          [blocks[c][rb], k_ret] + held("rows2", "tmp2")))
                yield
                for rb in range(RB):
                    ret_turned.extend(turn_block(c, [rb], dst, 1.0, engine, [rotated[rb]]))

            def retention(h):
                b = wide_pair()
                s = tmp2[:, 512 * (h % 2):512 * (h % 2) + 384]

                def fn(e):
                    e.matmul(psum[:, b, 0:256], rkt[:, h, 0:P], rqt[:, h, :], start=True, stop=True)
                    return e.matmul(psum[:, b, 256:384], rkt[:, h, P:SEQ], rqt[:, h, P:SEQ], start=True, stop=True)
                m = op("pe", fn, ret_turned + held(("bank", b)))
                d = op("dve", lambda e: e.tensor_tensor(s, psum[:, b, 0:384], decay[:, h, :], ALU.mult),
                       [m, k_decay] + held("rope_tmp", ("ret_s", h % 2), "tmp2"))
                free[("bank", b)] = [d]
                yield
                yield
                to = turn_bank()

                def weighted(e):
                    v = [proj2[:, kb, D + h * P:D + h * P + P] for kb in range(RB)]
                    e.matmul(psum[:, to, 0:128], s[:, 0:128], v[0], start=True, stop=True)
                    e.matmul(psum[:, to, 128:256], s[:, 128:256], v[0], start=True, stop=False)
                    return e.matmul(psum[:, to, 128:256], s[:, 256:384], v[1], start=False, stop=True)
                o = op("pe", weighted, [d] + blocks[2] + held(("bank", to)))
                free[("ret_s", h % 2)] = [o]
                v = rows2[:, :, h * P:h * P + P]
                c = op("act", lambda e: e.activation(v, psum[:, to, 0:256].rearrange("p (r d) -> p r d", r=RB), ACT.Copy),
                       [o] + ret_turned)
                free[("bank", to)] = [c]
                yield
                for rb in range(RB):
                    m = op("dve", lambda e, rb=rb: e.bn_stats(stats[:, rb, h, :], v[:, rb, :]), [c])
                for rb in range(RB):
                    m = op("dve", lambda e, rb=rb: e.bn_aggr(agg[:, rb, h, :], stats[:, rb, h, :]), [m])
                for rb in range(RB):
                    m = op("dve", lambda e, rb=rb: e.tensor_scalar(v[:, rb, :], v[:, rb, :], agg[:, rb, h, 0:1], None,
                                                                   ALU.subtract), [m])
                y_ret.append(m)

            def ret_rstd():
                for rb in range(RB):
                    m = op("dve", lambda e, rb=rb: e.tensor_scalar(rstd[:, rb, :], agg[:, rb, :, 1], EPS_2, None,
                                                                   ALU.add), [y_ret[-1]])
                    ret_norm.append(power(rb, RET_H, [m]))
            ret_norm = []

            def ret_gate():
                for rb in range(RB):
                    for h in range(RET_H):
                        m = op("dve", lambda e, rb=rb, h=h: e.scalar_tensor_tensor(
                            out=rows2[:, rb, h * P:h * P + P], in0=rows2[:, rb, h * P:h * P + P],
                            scalar=rstd[:, rb, h:h + 1], in1=proj2[:, rb, 1536 + h * P:1536 + h * P + P],
                            op0=ALU.mult, op1=ALU.mult), [ret_norm[rb], blocks[3][rb]])
                    ret_done.append(m)
            ret_done = []

            def stick_breaking(pair):
                b = wide_pair()
                z = psum[:, b:b + 2, 0:384]
                buf, weight = [v[pair % 2].rearrange("p (n c) -> p n c", n=2) for v in (sb_bufs, sb_weights)]

                def fn(e):
                    for n in range(2):
                        key = [head_cols(skt, 2 * pair + n, k * P, P) for k in range(2)]
                        qry = [head_cols(sqt, 2 * pair + n, k * P, P) for k in range(2)]
                        e.matmul(z[:, n, 0:128], key[0], qry[0], start=True, stop=False)
                        e.matmul(z[:, n, 128:256], key[1], qry[1], start=False, stop=False)
                        m = e.matmul(z[:, n, 256:384], key[0], qry[1], start=False, stop=True)
                    return m
                m = op("pe", fn, sb_turned + held(("bank", b), ("bank", b + 1)))
                s1 = op("act", lambda e: e.activation(buf, z, ACT.Abs), [m] + held(("sbuf", pair % 2), "heads"))
                s2 = op("act", lambda e: e.activation(buf, buf, ACT.Exp, scale=-1.0), [s1])
                s3 = op("act", lambda e: e.activation(buf, buf, ACT.Ln, bias=1.0), [s2])
                yield
                m = op("dve", lambda e: e.scalar_tensor_tensor(out=buf, in0=z, scalar=0.0, in1=buf, op0=ALU.max,
                                                               op1=ALU.add), [s3])
                for n in range(2):
                    v = buf[:, n, 0:256].rearrange("p (b q) -> p b q", b=2)
                    m = op("dve", lambda e, v=v: e.tensor_tensor(
                        v, v, strict[:, :].unsqueeze(1).broadcast_to([P, 2, P]), ALU.mult), [m, k_strict])
                yield

                def less_later(e):
                    on = dict(start=False, skip_group_check=True)
                    for n in range(2):
                        e.matmul(z[:, n, :], tri[:, 0:P], buf[:, n, :], stop=False, **on)
                        e.matmul(z[:, n, 256:384], tri[:, P:SEQ], buf[:, n, 128:256], stop=False, **on)
                        e.matmul(z[:, n, 0:128], identb, strict_b, stop=False, **on)
                        m = e.matmul(z[:, n, 128:256], identb, strict_b, stop=True, **on)
                    return m
                m = op("pe", less_later, [m, k_tri, k_sb])
                free[("sbuf", pair % 2)] = [m]
                a1 = op("act", lambda e: e.activation(weight, z, ACT.Exp),
                        [m] + held(("sb_weight", pair % 2), ("ret_s", 0), ("ret_s", 1)))
                free[("bank", b)] = free[("bank", b + 1)] = [a1]
                yield
                to = turn_bank()

                def weighted(e):
                    for n in range(2):
                        c = 3072 + (2 * pair + n) * HD
                        v = [proj2[:, kb, c:c + HD] for kb in range(RB)]
                        at = [psum[:, to, r * P + n * HD:r * P + n * HD + HD] for r in range(RB)]
                        e.matmul(at[0], weight[:, n, 0:128], v[0], start=True, stop=True)
                        e.matmul(at[1], weight[:, n, 256:384], v[0], start=True, stop=False)
                        m = e.matmul(at[1], weight[:, n, 128:256], v[1], start=False, stop=True)
                    return m
                o = op("pe", weighted, [a1] + blocks[6] + held(("bank", to)))
                free[("sb_weight", pair % 2)] = [o]
                m = op("dve", lambda e: e.tensor_copy(rows2[:, :, 512 + pair * P:512 + pair * P + P],
                                                      psum[:, to, 0:256].rearrange("p (r d) -> p r d", r=RB)),
                       [o] + ret_turned)
                free[("bank", to)] = [m]
                y_sb.append(m)

            def turn_sticks(c, dst, scale, engine):
                return lambda: sb_turned.extend(turn_block(c, range(RB), dst, scale, engine))
            ret_units = [retention(h) for h in range(RET_H)]
            sb_units = [stick_breaking(n) for n in range(SB_H // 2)]
            ret_units[2] = preceded(turn_sticks(4, sqt, SB_D ** -0.5, "act"), ret_units[2])
            sb_units[0] = preceded(turn_sticks(5, skt, 1.0, "dve"), sb_units[0])
            ret_units[-1] = followed(ret_units[-1], ret_rstd)
            sb_units[-2] = followed(sb_units[-2], ret_gate)
            state["low_by"] = "pool"
            project(0)
            background.append(turn_retention(0, rqt, "dve"))
            project(1)
            drain_background()
            background.append(turn_retention(1, rkt, "act"))
            project(2)
            drain_background()
            background.append(pipelined(ret_units + sb_units))
            for c in (4, 5, 6, 3, 7):
                project(c)
            state["low_by"] = "dve"
            xt_used = (c_tile, state["tile"])
            drain_background()
            free["rt"] = [y_sb[-1], y_ret[-1]]
            for rb in range(RB):
                v = rows2[:, rb, 512:1024]
                g = op("dve", lambda e, rb=rb, v=v: e.tensor_tensor(v, v, proj2[:, rb, 3584:4096], ALU.mult),
                       [y_sb[-1], blocks[7][rb]])
                if rb == 0:
                    yt = [to_stationary(rows2[:, 0, :], [[ret_done[0]], [g]], xt_hi, xt_lo, 0, hold=[xt_used])]
            if layer + 1 < DEPTH_2:
                k_g = load_gain(layer + 1)
            yt.append(Late(lambda: to_stationary(rows2[:, 1, :], [[ret_done[1]], [g]], xt_hi, xt_lo, 1, hold=[xt_used])))
            xready = [None, None]

            def add_gated(rb, h, mark, bank):
                t = tmp2[:, (2 * h + rb) * 512:(2 * h + rb) * 512 + 512]
                v = x[:, rb, h * BLK:h * BLK + BLK]
                m = op("dve", lambda e: e.tensor_tensor(t, psum[:, bank, :], gate_row[:, h * BLK:h * BLK + BLK],
                                                        ALU.mult), [mark, gates[h]] + held("rope_tmp", "tmp2"))
                free[("bank", bank)] = [m]
                xready[rb] = [op("dve", lambda e: e.tensor_tensor(v, v, t, ALU.add), [m])]
            free["tmp2"] = [y_sb[-1], y_ret[-1]] + held(("sb_weight", 0), ("sb_weight", 1))
            marks, banks = out_product("w_out_2", layer, yt, lambda of: [add_gated(rb, 0, *of[rb]) for rb in range(RB)])
            free["proj"] = free["heads"] = free["values"] = yt[0] + yt[1]
            for rb in range(RB):
                add_gated(rb, 1, marks[rb][1], banks[rb][1])
            free["rows2"] = xready[1] + yt[0] + yt[1]
            free["gate"] = free["tmp2"] = xready[1]

        k_f = load("final_g", shift, rows(T["final_g_2"]), held("mods"))
        rs = [rms(rb, xready[rb], rows2[:, rb, :]) for rb in range(RB)]
        for rb in range(RB):
            m = op("dve", lambda e, rb=rb: e.scalar_tensor_tensor(
                out=x[:, rb, :], in0=x[:, rb, :], scalar=rstd[:, rb, 0:1], in1=shift, op0=ALU.mult, op1=ALU.mult),
                [rs[rb], k_f])
            op("act", lambda e, rb=rb: e.dma_start(out[rb * P:rb * P + P, :], x[:, rb, :]), [m], inc=c_out, by=16)
        assert state["tile"] == len(order) == N_TILES and not ada_left

        block = ctx.enter_context(nc.Block())

        @block.sync
        def _(sp):
            n = N_TILES
            W = T["weights"]
            for rb in range(RB):
                sp.dma_start(x[:, rb, :], T["x"][rb * P:rb * P + P, :]).then_inc(c_x[rb].sem, 16)
            for t in range(RING):
                sp.dma_start(raw[:, t, :], W[t]).then_inc(c_raw[t].sem, 16)
            trips = (n - RING) // RING
            with sp.Fori(0, trips) as i:
                for s in range(RING):
                    sp.wait_ge(c_lo.sem, i * RING + s + 1)
                    src = W[bass.ds(i * RING + RING + s, 1), :, :].rearrange("a p c -> (a p) c")
                    sp.dma_start(raw[:, s, :], src).then_inc(c_raw[s].sem, 16)
            for t in range(RING + trips * RING, n):
                sp.wait_ge(c_lo.sem, t - RING + 1)
                sp.dma_start(raw[:, t % RING, :], W[t]).then_inc(c_raw[t % RING].sem, 16)

        @block.tensor
        def _(e):
            plan.emit("pe", e)

        @block.scalar
        def _(e):
            plan.emit("act", e)
            e.wait_ge(c_out.sem, 16 * RB)

        @block.vector
        def _(e):
            plan.emit("dve", e)

        @block.gpsimd
        def _(e):
            plan.emit("pool", e)
    return order



def pack_weights(order, inputs):
    w = np.zeros((len(order), P, TW), np.float32)

    def chunks(a):
        k, n = a.shape
        return a.reshape(k // P, P, n).transpose(1, 0, 2).reshape(P, -1)

    for n, (name, layer, cols, what, k0) in enumerate(order):
        m = inputs[name][layer]
        r = slice(k0 * P, k0 * P + 4 * P)
        if what == "half" and isinstance(cols, tuple):
            c0 = cols[1] * BLK
            own = m[r, c0:min(c0 + BLK, 3 * MIX)]
            if c0 + BLK > 3 * MIX:
                own = np.concatenate([own, m[r, m.shape[1] - MEMW:]], axis=1)
        elif what == "half":
            own = m[r, cols:cols + BLK]
        elif what == "narrow":
            c0 = 3 * MIX + IDX_W
            own = m[:, c0:c0 + IDX_H + HD]
        elif what == "up":
            c0 = cols * FF_STEP
            own = np.concatenate([m[r, c0:c0 + FF_STEP], m[r, D_FF + c0:D_FF + c0 + FF_STEP]], axis=1)
        else:
            own = m[cols * FF_STEP:(cols + 1) * FF_STEP, :]
        own = chunks(own)
        w[n, :, 0:own.shape[1]] = own
    return w


def shape_constants():
    i = np.arange(P)
    q, s = i[:, None], i[None, :]
    big = lambda keep: np.where(keep, 0.0, BIG).astype(np.float32)
    pieces = [np.eye(P, dtype=np.float32), big(s >= q), big(s <= q)]
    for dil in (4, 16):
        same = (q - s) % dil == 0
        pieces += [big(same), big(same & (s <= q))]
    n, m = np.arange(SEQ)[None, :], np.arange(SEQ)[:, None]
    head = np.arange(RET_H, dtype=np.float64)
    log_gamma = np.log1p(-(2.0 ** (-5.0 - head)))
    seen = m // CHUNK <= n // CHUNK
    decay = np.where(seen, np.exp(np.abs(n - m)[None] * log_gamma[:, None, None]), 0.0) * RET_D ** -0.5
    decay = np.concatenate([decay[:, 0:P, :], decay[:, P:, P:]], axis=2).transpose(1, 0, 2)
    half = RET_D // 2
    inv2 = ROPE_BASE ** (-np.arange(half, dtype=np.float32) / np.float32(half))
    ang = np.arange(SEQ, dtype=np.float32)[:, None] * inv2.astype(np.float32)[None, :]
    f = lambda a: np.ascontiguousarray(a, dtype=np.float32)
    return {
        "ident": np.eye(P, dtype=np.float32),
        "masks": f(np.concatenate(pieces, axis=1)),
        "causal": f(np.concatenate([np.zeros((P, P)), big(s <= q)], axis=1)),
        "inv_freq": f(np.float32(ROPE_THETA) ** (-np.arange(ROPE_HALF, dtype=np.float32) / np.float32(ROPE_HALF))),
        "decay": f(decay),
        "ret_cos_sin": f(np.concatenate([np.cos(ang), np.sin(ang)], axis=1)),
        "tri": f(np.concatenate([-(q >= s).astype(np.float32), -np.ones((P, P))], axis=1)),
        "strict": f(q < s),
        "strict_bias": big(q < s),
    }


_SMALL = ["x", "mem", "positions", "mem_ln_g", "mem_ln_b", "idx_kn_g", "idx_kn_b", "ln1_g", "ln1_b", "ln2_g",
          "ln2_b", "c_2", "norm_g_2", "b_ada_2", "final_g_2"]
_FLAT = {"x": (SEQ, D), "mem": (SEQ, D)}


def kernel(**inputs):
    import concourse.bacc as _bacc
    from concourse.bass_utils import run_bass_kernel_spmd as _run

    nc = _bacc.Bacc("TRN2", target_bir_lowering=False, num_devices=1)
    given = {k: np.asarray(v) for k, v in inputs.items()}
    arrays = {k: np.ascontiguousarray(given[k].reshape(_FLAT.get(k, given[k].shape))) for k in _SMALL}
    for name in ("positions", "c_2"):
        arrays[name] = np.ascontiguousarray(given[name].reshape(-1, P).T)
    arrays.update(shape_constants())
    T, feed = {}, {}
    for name, a in arrays.items():
        feed[f"in_{name}"] = a
        T[name] = nc.dram_tensor(f"in_{name}", a.shape, mybir.dt.from_np(a.dtype), kind="ExternalInput").ap()
    T["weights"] = nc.dram_tensor("in_weights", (N_TILES, P, TW), F32, kind="ExternalInput").ap()
    out = nc.dram_tensor("out_rows", (SEQ, D), F32, kind="ExternalOutput").ap()
    order = stack_kernel(nc, T, out)
    feed["in_weights"] = pack_weights(order, given)
    r = _run(nc, [feed], core_ids=[0])
    return r.results[0]["out_rows"].reshape(1, SEQ, D)
```
